# Optimizing a Trainium2 kernel written in Bass

```python
import jax, jax.numpy as jnp
from jax import lax
import numpy as np

D_MODEL = 1024
BATCH = 1
SEQ = 256
DEPTH = 2

N_MIXERS = 2
N_A_LAYERS = (DEPTH + 1) // 2
N_B_LAYERS = DEPTH // 2
EPS = 1e-6

HG_HEADS = 6
HG_KDIM = 128
HG_VDIM = 128
HG_CHUNK = 64
HG_F = HG_HEADS * HG_KDIM
HG_V = HG_HEADS * HG_VDIM

MLA_HEADS = 6
MLA_Q_LORA = 384
MLA_KV_LORA = 256
MLA_NOPE = 128
MLA_ROPE = 64
MLA_QK = MLA_NOPE + MLA_ROPE
MLA_VDIM = 128
ROPE_THETA = 10000.0
Q_BLOCK = 128

MEM_LEN = 256
MEM_HEADS = 4
MEM_HDIM = 64
MEM_W = MEM_HEADS * MEM_HDIM

MIX_W = 768
OUT_W = MIX_W + MEM_W
HG_IN_W = 2 * HG_F + 2 * HG_V + MEM_W
MLA_IN_W = MLA_Q_LORA + MLA_KV_LORA + MLA_ROPE + MEM_W

D_FF = 2816
CONV_W = 3


def rms_norm(x, g):
    xf = x.astype(jnp.float32)
    y = xf * lax.rsqrt(jnp.mean(xf * xf, axis=-1, keepdims=True) + EPS)
    return (y * g.astype(jnp.float32)).astype(x.dtype)

def rope_tables(positions):
    half = MLA_ROPE // 2
    inv = ROPE_THETA ** (-jnp.arange(half, dtype=jnp.float32) / half)
    ang = positions.astype(jnp.float32)[..., None] * inv
    return jnp.cos(ang)[:, :, None, :], jnp.sin(ang)[:, :, None, :]

def apply_rope(x, cos, sin):
    half = MLA_ROPE // 2
    xf = x.astype(jnp.float32)
    x1, x2 = xf[..., :half], xf[..., half:]
    return jnp.concatenate([x1 * cos - x2 * sin, x1 * sin + x2 * cos], axis=-1).astype(x.dtype)

def hgrn2_mixer(z, lb, onorm_g):
    B, S, _ = z.shape
    C = HG_CHUNK
    N = S // C
    q, f, i, g = jnp.split(z, [HG_F, 2 * HG_F, 2 * HG_F + HG_V], axis=-1)
    q = jax.nn.silu(q.astype(jnp.float32)) * (HG_KDIM ** -0.5)
    fg = lb + (1.0 - lb) * jax.nn.sigmoid(f.astype(jnp.float32))
    k = 1.0 - fg
    logf = jnp.log(fg)
    v = i.astype(jnp.float32)

    def to_chunks(t, d):
        return t.reshape(B, N, C, HG_HEADS, d).transpose(1, 0, 3, 2, 4)

    qc, kc, lc = to_chunks(q, HG_KDIM), to_chunks(k, HG_KDIM), to_chunks(logf, HG_KDIM)
    vc = to_chunks(v, HG_VDIM)
    causal = jnp.tril(jnp.ones((C, C), dtype=bool))[:, :, None]

    def step(state, xs):
        q_, k_, v_, lf = xs
        b = jnp.cumsum(lf, axis=2)
        o_inter = jnp.einsum('bhtk,bhkv->bhtv', q_ * jnp.exp(b), state)
        diff = b[:, :, :, None, :] - b[:, :, None, :, :]
        decay = jnp.exp(jnp.where(causal, diff, -jnp.inf))
        attn = jnp.einsum('bhtk,bhtsk,bhsk->bhts', q_, decay, k_)
        o = o_inter + jnp.einsum('bhts,bhsv->bhtv', attn, v_)
        b_last = b[:, :, -1, :]
        state = state * jnp.exp(b_last)[..., None] + jnp.einsum(
            'bhsk,bhsv->bhkv', k_ * jnp.exp(b_last[:, :, None, :] - b), v_)
        return state, o

    s0 = jnp.zeros((B, HG_HEADS, HG_KDIM, HG_VDIM), jnp.float32)
    _, o = lax.scan(step, s0, (qc, kc, vc, lc))
    o = o.transpose(1, 0, 3, 2, 4).reshape(B, S, HG_HEADS, HG_VDIM)
    gate = g.astype(jnp.float32).reshape(B, S, HG_HEADS, HG_VDIM)
    o = rms_norm(o, onorm_g) * jax.nn.silu(gate)
    return o.reshape(B, S, HG_V).astype(z.dtype)

def causal_block_attention(q, k, v):
    B, S, H, Dq = q.shape
    nb = S // Q_BLOCK
    scale = Dq ** -0.5
    qb = q.reshape(B, nb, Q_BLOCK, H, Dq).transpose(1, 0, 2, 3, 4)
    kpos = jnp.arange(S)

    def one_block(args):
        qi, idx = args
        s = jnp.einsum('bqhd,bkhd->bhqk', qi, k).astype(jnp.float32) * scale
        qpos = idx * Q_BLOCK + jnp.arange(Q_BLOCK)
        s = jnp.where(kpos[None, :] <= qpos[:, None], s, -jnp.inf)
        p = jax.nn.softmax(s, axis=-1)
        return jnp.einsum('bhqk,bkhd->bqhd', p.astype(v.dtype), v)

    out = lax.map(one_block, (qb, jnp.arange(nb)))
    return out.transpose(1, 0, 2, 3, 4).reshape(B, S, H, v.shape[-1])

def mla_mixer(z, cos, sin, qa_g, kva_g, w_uq, w_ukv, qn_g, kn_g):
    B, S, _ = z.shape
    cq, ckv, kpe = jnp.split(z, [MLA_Q_LORA, MLA_Q_LORA + MLA_KV_LORA], axis=-1)
    q = (rms_norm(cq, qa_g) @ w_uq).reshape(B, S, MLA_HEADS, MLA_QK)
    kv = (rms_norm(ckv, kva_g) @ w_ukv).reshape(B, S, MLA_HEADS, MLA_NOPE + MLA_VDIM)
    k_nope, v = kv[..., :MLA_NOPE], kv[..., MLA_NOPE:]
    k_rope = jnp.broadcast_to(kpe[:, :, None, :], (B, S, MLA_HEADS, MLA_ROPE))
    k = jnp.concatenate([k_nope, k_rope], axis=-1)
    q = rms_norm(q, qn_g)
    k = rms_norm(k, kn_g)
    q = jnp.concatenate([q[..., :MLA_NOPE], apply_rope(q[..., MLA_NOPE:], cos, sin)], axis=-1)
    k = jnp.concatenate([k[..., :MLA_NOPE], apply_rope(k[..., MLA_NOPE:], cos, sin)], axis=-1)
    o = causal_block_attention(q, k, v)
    return o.reshape(B, S, MLA_HEADS * MLA_VDIM)

def memory_attention(qm, mem_n, w_mem_kv, qn_g, kn_g):
    B, S, _ = qm.shape
    M = mem_n.shape[1]
    kv = mem_n @ w_mem_kv
    q = rms_norm(qm.reshape(B, S, MEM_HEADS, MEM_HDIM), qn_g)
    k = rms_norm(kv[..., :MEM_W].reshape(B, M, MEM_HEADS, MEM_HDIM), kn_g)
    v = kv[..., MEM_W:].reshape(B, M, MEM_HEADS, MEM_HDIM)
    s = jnp.einsum('bshd,bmhd->bhsm', q, k).astype(jnp.float32) * (MEM_HDIM ** -0.5)
    p = jax.nn.softmax(s, axis=-1)
    o = jnp.einsum('bhsm,bmhd->bshd', p.astype(v.dtype), v)
    return o.reshape(B, S, MEM_W)

def conv_ffn(h, w_up, conv_w, conv_b, w_down):
    u = h @ w_up
    u = lax.conv_general_dilated(
        u, conv_w[:, None, :].astype(u.dtype), window_strides=(1,),
        padding=[(CONV_W - 1, 0)], dimension_numbers=('NWC', 'WIO', 'NWC'),
        feature_group_count=u.shape[-1]) + conv_b
    a, b = u[..., :D_FF], u[..., D_FF:]
    return (jax.nn.silu(a) * b) @ w_down

def first_inputs(seed: int = 0) -> dict:
    key = jax.random.key(seed)
    ks = jax.random.split(key, 32)
    nrm = lambda k, shape, scale: jax.random.normal(k, shape, jnp.float32) * scale
    gain = lambda k, shape: 1.0 + 0.02 * jax.random.normal(k, shape, jnp.float32)
    offs = jax.random.randint(ks[2], (BATCH, 1), 0, 1024, dtype=jnp.int32)
    positions = offs + jnp.arange(SEQ, dtype=jnp.int32)[None, :]
    return {
        "x": nrm(ks[0], (BATCH, SEQ, D_MODEL), 1.0),
        "mem": nrm(ks[1], (BATCH, MEM_LEN, D_MODEL), 1.0),
        "positions": positions,
        "mix_norm_g": gain(ks[3], (DEPTH, D_MODEL)),
        "ffn_norm_g": gain(ks[4], (DEPTH, D_MODEL)),
        "mem_norm_g": gain(ks[5], (DEPTH, D_MODEL)),
        "w_mem_kv": nrm(ks[6], (DEPTH, D_MODEL, 2 * MEM_W), D_MODEL ** -0.5),
        "mem_q_norm_g": gain(ks[7], (DEPTH, MEM_HDIM)),
        "mem_k_norm_g": gain(ks[8], (DEPTH, MEM_HDIM)),
        "w_out": nrm(ks[9], (DEPTH, OUT_W, D_MODEL), OUT_W ** -0.5),
        "w_up": nrm(ks[10], (DEPTH, D_MODEL, 2 * D_FF), D_MODEL ** -0.5),
        "conv_w": nrm(ks[11], (DEPTH, CONV_W, 2 * D_FF), CONV_W ** -0.5),
        "conv_b": nrm(ks[12], (DEPTH, 2 * D_FF), 0.02),
        "w_down": nrm(ks[13], (DEPTH, D_FF, D_MODEL), D_FF ** -0.5),
        "hg_w_in": nrm(ks[14], (N_A_LAYERS, D_MODEL, HG_IN_W), D_MODEL ** -0.5),
        "hg_lb_logits": nrm(ks[15], (DEPTH + 1, HG_F), 0.5),
        "hg_out_norm_g": gain(ks[16], (N_A_LAYERS, HG_VDIM)),
        "mla_w_in": nrm(ks[17], (N_B_LAYERS, D_MODEL, MLA_IN_W), D_MODEL ** -0.5),
        "mla_qa_norm_g": gain(ks[18], (N_B_LAYERS, MLA_Q_LORA)),
        "mla_kva_norm_g": gain(ks[19], (N_B_LAYERS, MLA_KV_LORA)),
        "mla_w_uq": nrm(ks[20], (N_B_LAYERS, MLA_Q_LORA, MLA_HEADS * MLA_QK), MLA_Q_LORA ** -0.5),
        "mla_w_ukv": nrm(ks[21], (N_B_LAYERS, MLA_KV_LORA, MLA_HEADS * (MLA_NOPE + MLA_VDIM)), MLA_KV_LORA ** -0.5),
        "mla_q_norm_g": gain(ks[22], (N_B_LAYERS, MLA_QK)),
        "mla_k_norm_g": gain(ks[23], (N_B_LAYERS, MLA_QK)),
    }

def first_block(x, mem, positions, mix_norm_g, ffn_norm_g, mem_norm_g, w_mem_kv,
              mem_q_norm_g, mem_k_norm_g, w_out, w_up, conv_w, conv_b, w_down,
              hg_w_in, hg_lb_logits, hg_out_norm_g, mla_w_in, mla_qa_norm_g,
              mla_kva_norm_g, mla_w_uq, mla_w_ukv, mla_q_norm_g, mla_k_norm_g):
    cos, sin = rope_tables(positions)
    lower_bounds = jnp.cumsum(jax.nn.softmax(hg_lb_logits.astype(jnp.float32), axis=0), axis=0)
    for layer in range(DEPTH):
        h = rms_norm(x, mix_norm_g[layer])
        j = layer // N_MIXERS
        if layer % N_MIXERS == 0:
            z = h @ hg_w_in[j]
            y = hgrn2_mixer(z[..., :-MEM_W], lower_bounds[layer], hg_out_norm_g[j])
        else:
            z = h @ mla_w_in[j]
            y = mla_mixer(z[..., :-MEM_W], cos, sin, mla_qa_norm_g[j], mla_kva_norm_g[j],
                          mla_w_uq[j], mla_w_ukv[j], mla_q_norm_g[j], mla_k_norm_g[j])
        m = memory_attention(z[..., -MEM_W:], rms_norm(mem, mem_norm_g[layer]), w_mem_kv[layer],
                             mem_q_norm_g[layer], mem_k_norm_g[layer])
        x = x + jnp.concatenate([y, m], axis=-1) @ w_out[layer]
        x = x + conv_ffn(rms_norm(x, ffn_norm_g[layer]), w_up[layer], conv_w[layer],
                         conv_b[layer], w_down[layer])
    return x


DEPTH_2 = 1

CHUNK = 64
D_PLE = 256
D_CONV = 512
CONV_WIDTH = 31
N_HEADS_GLA = 4
D_GLA_K = 256
D_GLA_V = 512
HEAD_K = D_GLA_K // N_HEADS_GLA
HEAD_V = D_GLA_V // N_HEADS_GLA
GATE_RANK = 16
GATE_TAU = 16.0
D_MIX = D_CONV + D_GLA_V
D_IN = 2 * D_CONV + 2 * D_GLA_K + 2 * D_GLA_V + GATE_RANK
SPLIT_POINTS = (
    D_CONV,
    2 * D_CONV,
    2 * D_CONV + D_GLA_K,
    2 * D_CONV + 2 * D_GLA_K,
    2 * D_CONV + 2 * D_GLA_K + D_GLA_V,
    2 * D_CONV + 2 * D_GLA_K + 2 * D_GLA_V,
)


def _rmsnorm(x, g):
    xf = x.astype(jnp.float32)
    y = xf * lax.rsqrt(jnp.mean(xf * xf, axis=-1, keepdims=True) + EPS)
    return (y * g.astype(jnp.float32)).astype(x.dtype)

def _layernorm(x, g, b):
    xf = x.astype(jnp.float32)
    mu = jnp.mean(xf, axis=-1, keepdims=True)
    var = jnp.mean(jnp.square(xf - mu), axis=-1, keepdims=True)
    y = (xf - mu) * lax.rsqrt(var + EPS)
    return (y * g.astype(jnp.float32) + b.astype(jnp.float32)).astype(x.dtype)

def _swiglu(x, w_in, w_out):
    gate, up = jnp.split(x @ w_in, 2, axis=-1)
    return (jax.nn.silu(gate) * up) @ w_out

def _conv_module(a, b, w_dw, b_dw, ln_g, ln_b):
    glu = a * jax.nn.sigmoid(b)
    y = lax.conv_general_dilated(
        glu, w_dw[:, None, :],
        window_strides=(1,),
        padding=((CONV_WIDTH - 1, 0),),
        dimension_numbers=("NWC", "WIO", "NWC"),
        feature_group_count=D_CONV,
    ) + b_dw
    return jax.nn.silu(_layernorm(y, ln_g, ln_b))

def _to_chunks(t, n_heads):
    bsz, seq, width = t.shape
    return t.reshape(bsz, seq // CHUNK, CHUNK, n_heads, width // n_heads).transpose(0, 1, 3, 2, 4)

def _gla(q, k, v, r, g_lr, w_gate_up, b_gate, o_norm):
    bsz, seq, _ = q.shape
    f32 = jnp.float32
    log_a = jax.nn.log_sigmoid((g_lr @ w_gate_up + b_gate).astype(f32)) / GATE_TAU
    qc = _to_chunks(q.astype(f32), N_HEADS_GLA) * (HEAD_K ** -0.5)
    kc = _to_chunks(k.astype(f32), N_HEADS_GLA)
    vc = _to_chunks(v.astype(f32), N_HEADS_GLA)
    cum = jnp.cumsum(_to_chunks(log_a, N_HEADS_GLA), axis=3)
    e_pos = jnp.exp(cum)
    e_neg = jnp.exp(-cum)
    q_dec = qc * e_pos
    a_low = jnp.einsum("bnhtd,bnhsd->bnhts", q_dec, kc * e_neg)
    a_up = jnp.einsum("bnhtd,bnhsd->bnhts", qc * e_neg, kc * e_pos)
    pos = jnp.arange(CHUNK)
    scores = jnp.where(pos[:, None] >= pos[None, :], a_low, a_up)
    o_intra = jnp.einsum("bnhts,bnhsv->bnhtv", scores, vc)
    cum_end = cum[:, :, :, -1:, :]
    kv = jnp.einsum("bnhsd,bnhsv->bnhdv", kc * jnp.exp(cum_end - cum), vc)
    decay = jnp.exp(cum_end[:, :, :, 0, :])

    def step(state, inp):
        dec, kv_c = inp
        return dec[..., None] * state + kv_c, state

    s0 = jnp.zeros((bsz, N_HEADS_GLA, HEAD_K, HEAD_V), f32)
    _, s_prev = lax.scan(step, s0, (jnp.moveaxis(decay, 1, 0), jnp.moveaxis(kv, 1, 0)))
    s_prev = jnp.moveaxis(s_prev, 0, 1)
    o_inter = jnp.einsum("bnhtd,bnhdv->bnhtv", q_dec, s_prev)
    o = (o_intra + o_inter).transpose(0, 1, 3, 2, 4).reshape(bsz, seq, N_HEADS_GLA, HEAD_V)
    o = o * lax.rsqrt(jnp.mean(o * o, axis=-1, keepdims=True) + EPS)
    o = o * o_norm.astype(f32).reshape(N_HEADS_GLA, HEAD_V)
    return (o.reshape(bsz, seq, D_GLA_V) * jax.nn.silu(r.astype(f32))).astype(q.dtype)

def second_inputs(seed: int = 0) -> dict:
    key = jax.random.key(seed)
    ks = jax.random.split(key, 24)
    f32 = jnp.float32

    def w(k, shape, fan_in):
        return jax.random.normal(k, shape, f32) * (fan_in ** -0.5)

    def gain(k, shape):
        return 1.0 + 0.05 * jax.random.normal(k, shape, f32)

    def bias(k, shape, scale=0.02):
        return scale * jax.random.normal(k, shape, f32)

    return {
        "x": jax.random.normal(ks[0], (BATCH, SEQ, D_MODEL), f32),
        "p": jax.random.normal(ks[1], (DEPTH_2, BATCH, SEQ, D_PLE), f32),
        "ffn1_norm": gain(ks[2], (DEPTH_2, D_MODEL)),
        "ffn1_w_in": w(ks[3], (DEPTH_2, D_MODEL, 2 * D_FF), D_MODEL),
        "ffn1_w_out": w(ks[4], (DEPTH_2, D_FF, D_MODEL), D_FF),
        "mix_norm": gain(ks[5], (DEPTH_2, D_MODEL)),
        "w_in": w(ks[6], (DEPTH_2, D_MODEL, D_IN), D_MODEL),
        "conv_w": w(ks[7], (DEPTH_2, CONV_WIDTH, D_CONV), CONV_WIDTH),
        "conv_b": bias(ks[8], (DEPTH_2, D_CONV)),
        "conv_ln_g": gain(ks[9], (DEPTH_2, D_CONV)),
        "conv_ln_b": bias(ks[10], (DEPTH_2, D_CONV)),
        "gate_w_up": w(ks[11], (DEPTH_2, GATE_RANK, D_GLA_K), GATE_RANK),
        "gate_b": bias(ks[12], (DEPTH_2, D_GLA_K), 0.1),
        "gla_norm": gain(ks[13], (DEPTH_2, D_GLA_V)),
        "w_out": w(ks[14], (DEPTH_2, D_MIX, D_MODEL), D_MIX),
        "ffn2_norm": gain(ks[15], (DEPTH_2, D_MODEL)),
        "ffn2_w_in": w(ks[16], (DEPTH_2, D_MODEL, 2 * D_FF), D_MODEL),
        "ffn2_w_out": w(ks[17], (DEPTH_2, D_FF, D_MODEL), D_FF),
        "ple_norm": gain(ks[18], (DEPTH_2, D_MODEL)),
        "ple_w_gate": w(ks[19], (DEPTH_2, D_MODEL, D_MODEL), D_MODEL),
        "ple_w_proj": w(ks[20], (DEPTH_2, D_PLE, D_MODEL), D_PLE),
        "final_norm": gain(ks[21], (D_MODEL,)),
    }

def second_block(x, p, ffn1_norm, ffn1_w_in, ffn1_w_out, mix_norm, w_in, conv_w, conv_b,
              conv_ln_g, conv_ln_b, gate_w_up, gate_b, gla_norm, w_out, ffn2_norm,
              ffn2_w_in, ffn2_w_out, ple_norm, ple_w_gate, ple_w_proj, final_norm):
    h = x
    for i in range(DEPTH_2):
        h = h + 0.5 * _swiglu(_rmsnorm(h, ffn1_norm[i]), ffn1_w_in[i], ffn1_w_out[i])
        z = _rmsnorm(h, mix_norm[i]) @ w_in[i]
        conv_a, conv_gt, q, k, v, r, g_lr = jnp.split(z, SPLIT_POINTS, axis=-1)
        y_conv = _conv_module(conv_a, conv_gt, conv_w[i], conv_b[i], conv_ln_g[i], conv_ln_b[i])
        y_gla = _gla(q, k, v, r, g_lr, gate_w_up[i], gate_b[i], gla_norm[i])
        h = h + jnp.concatenate([y_conv, y_gla], axis=-1) @ w_out[i]
        h = h + 0.5 * _swiglu(_rmsnorm(h, ffn2_norm[i]), ffn2_w_in[i], ffn2_w_out[i])
        gate = jax.nn.sigmoid(_rmsnorm(h, ple_norm[i]) @ ple_w_gate[i])
        h = h + gate * (p[i] @ ple_w_proj[i])
    return _rmsnorm(h, final_norm)


def setup_inputs(seed=0):
    out = dict(first_inputs(seed))
    for name, value in second_inputs(seed + 1).items():
        if name != "x":
            out[name + "_2"] = value
    return out


def reference(
    x, mem, positions, mix_norm_g, ffn_norm_g, mem_norm_g, w_mem_kv, mem_q_norm_g, mem_k_norm_g,
    w_out, w_up, conv_w, conv_b, w_down, hg_w_in, hg_lb_logits, hg_out_norm_g, mla_w_in,
    mla_qa_norm_g, mla_kva_norm_g, mla_w_uq, mla_w_ukv, mla_q_norm_g, mla_k_norm_g, p_2,
    ffn1_norm_2, ffn1_w_in_2, ffn1_w_out_2, mix_norm_2, w_in_2, conv_w_2, conv_b_2, conv_ln_g_2,
    conv_ln_b_2, gate_w_up_2, gate_b_2, gla_norm_2, w_out_2, ffn2_norm_2, ffn2_w_in_2,
    ffn2_w_out_2, ple_norm_2, ple_w_gate_2, ple_w_proj_2, final_norm_2,
):
    x = first_block(
        x, mem, positions, mix_norm_g, ffn_norm_g, mem_norm_g, w_mem_kv, mem_q_norm_g,
        mem_k_norm_g, w_out, w_up, conv_w, conv_b, w_down, hg_w_in, hg_lb_logits, hg_out_norm_g,
        mla_w_in, mla_qa_norm_g, mla_kva_norm_g, mla_w_uq, mla_w_ukv, mla_q_norm_g,
        mla_k_norm_g,
    )
    return second_block(
        x, p_2, ffn1_norm_2, ffn1_w_in_2, ffn1_w_out_2, mix_norm_2, w_in_2, conv_w_2, conv_b_2,
        conv_ln_g_2, conv_ln_b_2, gate_w_up_2, gate_b_2, gla_norm_2, w_out_2, ffn2_norm_2,
        ffn2_w_in_2, ffn2_w_out_2, ple_norm_2, ple_w_gate_2, ple_w_proj_2, final_norm_2,
    )


_drawn_inputs = setup_inputs


def setup_inputs(seed=0):
    import zlib

    import numpy as np

    out = dict(_drawn_inputs(seed))
    spreads = {}
    factors = {'mix_norm_g': 3.113,
     'mem_norm_g': 8.0,
     'mem_q_norm_g': 8.0,
     'mem_k_norm_g': 8.0,
     'conv_b': 2.706,
     'hg_out_norm_g': 4.366,
     'mla_qa_norm_g': 8.0,
     'mla_kva_norm_g': 8.0,
     'mla_q_norm_g': 8.0,
     'mla_k_norm_g': 8.0,
     'ffn1_norm_2': 3.646,
     'conv_b_2': 17.719,
     'conv_ln_g_2': 128.215,
     'conv_ln_b_2': 200.0,
     'gate_b_2': 5.132,
     'gla_norm_2': 31.392,
     'ffn2_norm_2': 27.147,
     'ple_norm_2': 200.0,
     'ffn_norm_g': 3.608,
     'mix_norm_2': 3.178,
     'gate_w_up_2': 2.836,
     'p_2': 4.297,
     'ple_w_gate_2': 6.14,
     'ple_w_proj_2': 4.305}
    for name, (base, spread) in spreads.items():
        noise = np.random.default_rng([zlib.crc32(name.encode()), seed]).standard_normal(out[name].shape)
        drawn = base * np.exp(spread * noise) if base else spread * noise
        out[name] = __import__('jax').numpy.asarray(drawn.astype(out[name].dtype))
    for name, factor in factors.items():
        out[name] = (out[name] * factor).astype(out[name].dtype)
    return out
```

```python
from contextlib import ExitStack

import numpy as np

import concourse.bass as bass
from concourse import mybir

F32 = mybir.dt.float32
F32R = mybir.dt.float32r
BF16 = mybir.dt.bfloat16
I32 = mybir.dt.int32
U8 = mybir.dt.uint8
ALU = mybir.AluOpType
ACT = mybir.ActivationFunctionType
AX = mybir.AxisListType.X

P = 128
S = 256
T = S // P
D = 1024
KT = D // P
EPS = 1e-6
UNIT = 3072
PIECE = UNIT // 3
NC3 = UNIT // KT
SLOTS = 3
D_FF = 2816
CH = D_FF // P
FFN_UNITS = CH + 1
HEADS = 6
HW = HEADS * P
MEM_HEADS, MEM_HD, MEM_W = 4, 64, 256
ROPE, HALF, QK = 64, 32, 192
G_HEADS, G_K = 4, 64
TAPS = 31
CHUNK = 64
LEVELS = 8

U_MEM0 = 0
U_F = 2
U_Q = 4
U_I = 6
U_MEM1 = 8
U_G = 10
U_OUT0 = 12
U_FFN0 = U_OUT0 + 3
U_MLA = U_FFN0 + FFN_UNITS
U_UQ = U_MLA + 3
U_UKV = U_UQ + 2
U_OUT1 = U_UKV + 1
U_FFN1 = U_OUT1 + 3
U_FFN2 = U_FFN1 + FFN_UNITS
U_IN2 = U_FFN2 + FFN_UNITS
U_OUT2 = U_IN2 + 7
U_FFN3 = U_OUT2 + 3
U_PROJ = U_FFN3 + FFN_UNITS
U_GATE = U_PROJ + 1
UNITS = U_GATE + 3

_cols = {}
_at = 0
for _name, _n in (
    ("mix0", KT), ("mix1", KT), ("ffn0", KT), ("ffn1", KT), ("mem0", KT), ("mem1", KT),
    ("ffn2", KT), ("mix2", KT), ("ffn3", KT), ("ple", KT),
    ("cw0", CH * 8), ("cw1", CH * 8), ("mq", 2), ("mk", 2), ("lb", 18), ("hgn", 1), ("qa", 3), ("kva", 2),
    ("dw", 4 * TAPS), ("db", 4), ("lng", 4), ("lnb", 4), ("glan", 4),
    ("gb", 256), ("qn", QK), ("kn", QK), ("inv", HALF), ("gup", 256),
    ("ident", P), ("causal", P), ("tri", P), ("ones", P),
):
    _cols[_name] = (_at, _n)
    _at += _n
NV = _at
MASKS = LEVELS - 1
MU, MX = MASKS * 64, MASKS * 64 + P
NM = MX + P


TWO_PI = (6.28125, 0.0019350051879882812, float(2 * np.pi - 6.28125 - 0.0019350051879882812))


class Count:

    def __init__(self, sem):
        self.sem, self.n, self.turn, self.per = sem, 0, None, 0

    def inc(self, ins):
        ins.then_inc(self.sem, 1)
        self.n += 1
        return self.n

    def at(self, n):
        return n if self.turn is None else self.turn * self.per + n

    def enter(self, turn, per):
        self.turn, self.per, self.was = turn, per, self.n

    def leave(self, turns):
        assert self.n - self.was == self.per, (self.n, self.was, self.per)
        self.turn, self.n = None, self.was + self.per * turns


def build(nc, stream, vectors, masks, x_in, mem_in, pos_in, ple_in, fin_in, out):
    with ExitStack() as ctx:
        def sb(name, shape, dt=F32):
            return ctx.enter_context(nc.sbuf_tensor(name, shape, dt))

        sems = {}

        def sem(name):
            if name not in sems:
                sems[name] = ctx.enter_context(nc.semaphore(name))
            return sems[name]

        raw = sb("raw", [P, SLOTS, UNIT])
        w_hi = sb("w_hi", [P, SLOTS, UNIT], F32R)
        w_lo = sb("w_lo", [P, SLOTS, UNIT], F32R)
        x = sb("x", [P, T, D])
        h_hi = sb("h_hi", [P, KT, S], F32R)
        h_lo = sb("h_lo", [P, KT, S], F32R)
        y_hi = sb("y_hi", [P, KT, S], F32R)
        y_lo = sb("y_lo", [P, KT, S], F32R)
        mem_k = sb("mem_k", [P, 2, 2, S])
        mem_v = sb("mem_v", [P, 2, T, MEM_W])
        vec = sb("vec", [P, NV])
        msk = sb("msk", [P, NM], U8)
        zero = sb("zero", [P, P], BF16)
        trig = sb("trig", [P, 2, T, HALF])
        small = sb("small", [P, 192])
        mk_sq = sb("mk_sq", [P, T, MEM_W])[:, :, :]
        arena = sb("arena", [P, 9984])
        ps = ctx.enter_context(nc.psum_tensor("ps", [P, 8, 512], F32))

        def V(name, i=0, n=1):
            a, w = _cols[name]
            return vec[:, a + i:a + i + n]

        def room(tile, at, shape):
            v = tile[:, at:at + int(np.prod(shape))]
            if len(shape) == 2:
                v = v.rearrange("p (a b) -> p a b", b=shape[1])
            return v

        def A(at, *shape):
            return room(arena, at, shape)

        xflat = x[:, :, :].rearrange("p t d -> p (t d)")
        kflat = mem_k[:, :, :, :].rearrange("p a b c -> p (a b c)")
        vflat = mem_v[:, :, :, :].rearrange("p a b c -> p (a b c)")
        ident, causal, tri, ones = V("ident", 0, P), V("causal", 0, P), V("tri", 0, P), V("ones", 0, P)

        xn, junk = A(0, T, D), A(2048, T, D)
        memn = A(4096, KT, S)
        mk_tok = [mem_k[:, l, :, :] for l in range(2)]
        tr = [A(7168 + 64 * i, T, HALF) for i in range(4)]
        msk_f = A(8192, NM)
        hq, hk = A(0, HEADS, S), A(1536, HEADS, S)
        hD, hR = A(3072, HEADS, S), A(4608, HEADS, S)
        hE = A(6144, HEADS, S)
        hA = A(7680, HEADS * T, P)
        hO = A(9216, HEADS, P)
        hv, qm0 = room(xflat, 0, (T, HW)), room(xflat, 1536, (T, MEM_W))
        ho, hsq, hg = A(3072, T, HW), A(4608, T, HW), A(0, T, HW)
        ma_sq, ma_qT, ma_p, ma_pT = A(4608, T, MEM_W), A(5120, 2, S), A(5632, 8, S), A(7680, 8, S)
        cq, ckv, qm1 = A(0, T, 384), A(768, T, 320), A(1408, T, MEM_W)
        q, kv, krh = A(1920, T, 1152), A(4224, T, 1536), A(7296, T, 384)
        rt = [A(8064 + 384 * i, T, 192) for i in range(4)]
        kr = A(9600, T, ROPE)
        qkT = (A(0, 4, S), A(8064, 4, S))
        mp = (A(9088, 3, P), A(9472, 3, P))
        mpT = (room(kflat, 0, (3, P)), room(vflat, 0, (3, P)))
        ga, gs, glu, cy = A(0, 4, S), A(1024, 4, S), A(2048, 4, S + TAPS - 1), A(3192, 4, S)
        gq, gk, glr = A(4216, 2, S), A(4728, 2, S), A(5240, S)
        gv, gr, la = A(5496, T, 512), A(6520, T, 512), A(7544, T, 256)
        lnr = [A(4216 + 3840 + 256 * i, S) for i in range(4)]
        ple = A(9088, T, 256)
        ep, en, ec = A(0, 2, S), A(512, 2, S), A(1024, 2, S)
        qd, kd, qu, ku, ke = [A(1536 + 512 * i, 2, S) for i in range(5)]
        q7, k7 = A(8056, 2, P), A(8312, 2, P)
        gA = [room(kflat, 512 * i, (4, P)) for i in range(2)]
        gO = [room(vflat, 256 * i, (2, P)) for i in range(2)]
        cum = room(vflat, 512, (2, S))
        go, gosq = A(0, T, 512), A(1024, T, 512)
        g_abs = A(8056, T, 256)
        cv, sa, gg = A(0, 3, 512), A(1536, 3, S), A(2304, 3, S)
        fin, proj, sg = A(4096, D), A(5120, T, D), A(0, T, D)

        rings = [sem(f"raw_loaded{i}") for i in range(SLOTS)]
        s_hi, s_lo, s_used = sem("hi_ready"), sem("lo_ready"), sem("unit_used")
        s_evac, s_chain = sem("unit_evacuated"), sem("dve_chain")
        FFNS = ((U_FFN0, "cw0"), (U_FFN1, "cw1"), (U_FFN2, None), (U_FFN3, None))
        UP0 = (0, CH, None, None)
        FFN_NORM = (1, 3, 4, 6)
        HG_UNITS = [U_I, U_I + 1, U_MEM1, U_MEM1 + 1, U_G, U_G + 1]
        PLAIN = [0, 1, 2, 3, 4, 5] + HG_UNITS + [U_MLA, U_MLA + 1, U_MLA + 2, U_UQ, U_UQ + 1, U_UKV] + \
                list(range(U_IN2, U_IN2 + 7)) + [U_PROJ]
        EV = {u: i + 1 for i, u in enumerate(PLAIN)}

        def right(v, m):
            return v.rearrange("p h (b z m) -> p (h b) z m", z=2, m=m)[:, :, 1, :]

        def left(v, m):
            return v.rearrange("p h (b z m) -> p (h b) z m", z=2, m=m)[:, :, 0, :]

        block = ctx.enter_context(nc.Block())

        @block.sync
        def _(sp):
            sp.dma_start(junk, mem_in).then_inc(sem("mem_loaded"), 16)
            sp.dma_start(vec[:, :], vectors).then_inc(sem("vec_loaded"), 16)
            for s in range(SLOTS):
                sp.dma_start(raw[:, s, :], stream[s]).then_inc(rings[s], 16)
                if s == 0:
                    sp.dma_start(x[:, :, :], x_in).then_inc(sem("x_loaded"), 16)
                    sp.dma_start(small[:, 186:188].bitcast(I32), pos_in).then_inc(sem("pos_loaded"), 16)
                    sp.dma_start(msk_f, masks).then_inc(sem("msk_loaded"), 16)

            turns = (UNITS - SLOTS) // SLOTS
            with sp.Fori(0, turns) as i:
                for s in range(SLOTS):
                    sp.wait_ge(s_lo, i * 9 + (3 * s + 3))
                    sp.dma_start(raw[:, s, :],
                                 stream[bass.ds(i * SLOTS + (SLOTS + s), 1)].rearrange("a p n -> p (a n)"))\
                        .then_inc(rings[s], 16)
            for u in range(SLOTS * (turns + 1), UNITS):
                sp.wait_ge(s_lo, (u - SLOTS) * 3 + 3)
                sp.dma_start(raw[:, u % SLOTS, :], stream[u]).then_inc(rings[u % SLOTS], 16)
            for i in range(2 * T):
                sp.wait_ge(sem("out_done"), i + 1)
                t, half = i // 2, i % 2
                sp.dma_start(out[t * P:(t + 1) * P, half * 512:half * 512 + 512],
                             xn[:, t, half * 512:half * 512 + 512]).then_inc(sem("out_stored"), 16)
            sp.wait_ge(sem("out_stored"), 16 * 2 * T)

        @block.gpsimd
        def _(pool):
            pool.memset(zero[:, :], 0.0).then_inc(sem("zero_set"), 1)
            pool.wait_ge(sem("hg_o_ready"), 1)
            pool.wait_ge(sem("ma_qT_ready"), 1)
            pool.dma_start(x[:, :, :], x_in).then_inc(sem("x_back"), 16)
            pool.wait_ge(sem("x_done"), 2 * 3)
            pool.dma_start(ple, ple_in).then_inc(sem("ple_loaded"), 16)
            pool.wait_ge(sem("x_done"), 2 * 6)
            pool.dma_start(fin, fin_in).then_inc(sem("fin_loaded"), 16)

        @block.tensor
        def _(pe):
            def pieces(u, end):
                return u * 3 + -(-end // PIECE)

            def three(o, lh, ll, rh, rl, start, stop):
                pe.matmul(o, lh, rh, start=start, stop=False, skip_group_check=True)
                pe.matmul(o, lh, rl, start=False, stop=False, skip_group_check=True)
                return pe.matmul(o, ll, rh, start=False, stop=stop, skip_group_check=True)

            def full(o, l, r, start=True, stop=True):
                return pe.matmul(o, l, r, start=start, stop=stop, skip_group_check=True)

            def rows(u, c0, n, banks, ah, al, kts=KT, width=NC3, col=0):
                s = u % SLOTS
                for k in range(kts):
                    r = slice(k * width + c0, k * width + c0 + n)
                    pe.wait_ge(s_lo, pieces(u, r.stop))
                    for t in range(T):
                        tt = slice(t * P, (t + 1) * P)
                        m = three(ps[:, banks[t], col:col + n], ah[:, k, tt], al[:, k, tt],
                                  w_hi[:, s, r], w_lo[:, s, r], k == 0, k == kts - 1)
                return m

            def cols(u, j, o):
                s = u % SLOTS
                for k in range(KT):
                    r = slice(k * NC3 + j * P, k * NC3 + j * P + P)
                    pe.wait_ge(s_lo, pieces(u, r.stop))
                    m = three(o, w_hi[:, s, r], w_lo[:, s, r], h_hi[:, k, :], h_lo[:, k, :], k == 0, k == KT - 1)
                return m

            def norm(i):
                pe.wait_ge(sem("xn_done0"), i + 1)
                pe.wait_ge(sem("xn_done1"), i + 1)
                for k in range(KT):
                    for t in range(T):
                        m = pe.transpose(ps[:, 4 + k // 2, (k % 2) * S + t * P:(k % 2) * S + (t + 1) * P],
                                         xn[:, t, k * P:(k + 1) * P], ident)
                    if k % 2:
                        m.then_inc(sem("xT_ready"), 1)

            def kt_major(u, ah, al, ready):
                for k in range(KT):
                    s, e = (u + k // 3) % SLOTS, (k % 3) * D
                    pe.wait_ge(s_lo, pieces(u + k // 3, e + D))
                    ready(k)
                    for t in range(T):
                        tt = slice(t * P, (t + 1) * P)
                        for half in range(2):
                            r = slice(e + half * 512, e + half * 512 + 512)
                            m = three(ps[:, 2 * t + half, :], ah[:, k, tt], al[:, k, tt],
                                      w_hi[:, s, r], w_lo[:, s, r], k == 0, k == KT - 1)
                    if k % 3 == 2 or k == KT - 1:
                        m.then_inc(s_used, 1)

            def ffn(i):
                U0, n0 = FFNS[i][0], i * CH

                def lo_at(r, j, p):
                    return 3 * (U0 + j) + p + 1 if r is None else r * 9 + (3 * (U0 + j) + p + 1)

                def up(r, j):
                    s = (U0 + j) % SLOTS
                    for z in range(2):
                        pe.wait_ge(s_lo, lo_at(r, j, z))
                        for k in range(KT):
                            a = slice(z * PIECE + k * P, z * PIECE + k * P + P)
                            m = three(ps[:, 4 + j % 3, z * S:(z + 1) * S], w_hi[:, s, a], w_lo[:, s, a],
                                      h_hi[:, k, :], h_lo[:, k, :], k == 0, k == KT - 1)
                    m.then_inc(sem("up_ready"), 1)

                def down(r, j):
                    s, g = (U0 + j) % SLOTS, (j - 1) % 3
                    pe.wait_ge(s_lo, lo_at(r, j, 2))
                    pe.wait_ge(sem("g_lo_done"), n0 + j if r is None else r * 3 + (n0 + j))
                    for t in range(T):
                        tt = slice(t * P, (t + 1) * P)
                        for half in range(2):
                            a = slice(2 * PIECE + half * 512, 2 * PIECE + half * 512 + 512)
                            m = three(ps[:, 2 * t + half, :], y_hi[:, g, tt], y_lo[:, g, tt],
                                      w_hi[:, s, a], w_lo[:, s, a], False, True)
                    m.then_inc(s_used, 1)

                pe.wait_ge(sem("hT_ready"), 4 * FFN_NORM[i] + 4)
                up(None, 0)
                pe.wait_ge(s_lo, lo_at(None, 0, 2))
                pe.wait_ge(sem("zero_set"), 1)
                for b in range(4):
                    m = full(ps[:, b, :], zero[:, :], zero[:, 0:1].to_broadcast([P, 512]))
                m.then_inc(s_used, 1)
                with pe.Fori(0, (CH - 1) // 3) as r:
                    for j in range(1, 4):
                        up(r, j)
                        down(r, j)
                down(None, CH)

            def mem_keys(l):
                pe.wait_ge(sem("mk_done"), l + 1)
                for pair in range(2):
                    for t in range(T):
                        m = pe.transpose(ps[:, 4, pair * S + t * P:pair * S + (t + 1) * P],
                                         mk_tok[l][:, t, pair * P:(pair + 1) * P], ident)
                m.then_inc(sem("mkT_ready"), 1)

            def mem_attention(l):
                qm = (qm0, qm1)[l]
                pe.wait_ge(sem("ma_q_done"), l + 1)
                for pair in range(2):
                    for t in range(T):
                        m = pe.transpose(ps[:, 3, pair * S + t * P:pair * S + (t + 1) * P],
                                         qm[:, t, pair * P:(pair + 1) * P], ident)
                m.then_inc(sem("ma_qT_ready"), 1)
                pe.wait_ge(sem("ma_qT_done"), l + 1)
                pe.wait_ge(sem("mkT_done"), l + 1)
                for t in range(T):
                    for par in range(2):
                        for pair in range(2):
                            r = slice(par * 64, par * 64 + 64)
                            m = full(ps[:, 4 + 2 * t + par, pair * S:(pair + 1) * S],
                                     ma_qT[r, pair, t * P:(t + 1) * P], mem_k[r, l, pair, :])
                        m.then_inc(sem("ma_s_ready"), 1)
                for t in range(T):
                    for par in range(2):
                        g = 2 * t + par
                        pe.wait_ge(sem("ma_p_done"), 4 * l + g + 1)
                        for pair in range(2):
                            for mt in range(T):
                                m = pe.transpose(ps[:, 2 * pair + par, mt * S + t * P:mt * S + (t + 1) * P],
                                                 ma_p[:, 2 * g + pair, mt * P:(mt + 1) * P], ident)
                m.then_inc(sem("ma_pT_ready"), 1)
                pe.wait_ge(sem("ma_pT_done0"), l + 1)
                pe.wait_ge(sem("ma_pT_done1"), l + 1)
                for h in range(MEM_HEADS):
                    par, pair = h % 2, h // 2
                    for mt in range(T):
                        m = full(ps[par * 64:par * 64 + 64, 4, pair * S:(pair + 1) * S],
                                 mem_v[:, l, mt, h * 64:(h + 1) * 64], ma_pT[:, 2 * h + mt, :], mt == 0, mt == 1)
                m.then_inc(sem("ma_o_ready"), 1)

            pe.wait_ge(sem("vec_loaded"), 16)
            pe.wait_ge(sem("mn_done0"), 1)
            pe.wait_ge(sem("mn_done1"), 1)
            for k in range(KT):
                for t in range(T):
                    m = pe.transpose(ps[:, 4 + k // 2, (k % 2) * S + t * P:(k % 2) * S + (t + 1) * P],
                                     junk[:, t, k * P:(k + 1) * P], ident)
                if k % 2:
                    m.then_inc(sem("mnT_ready"), 1)
            pe.wait_ge(sem("memT_lo_done"), 1)
            rows(U_MEM0, 0, 384, (0, 1), y_hi, y_lo).then_inc(s_used, 1)
            rows(U_MEM0 + 1, 0, P, (2, 3), y_hi, y_lo).then_inc(s_used, 1)
            norm(0)
            pe.wait_ge(sem("hT_ready"), 4)
            for n, u in enumerate((U_F, U_F + 1, U_Q, U_Q + 1)):
                pe.wait_ge(s_evac, EV[u - 2])
                for j in range(3):
                    m = cols(u, j, ps[:, (n % 2) * 2 + j // 2, (j % 2) * S:(j % 2) * S + S])
                m.then_inc(s_used, 1)
                if n == 1:
                    mem_keys(0)
            pe.wait_ge(s_evac, EV[U_Q + 1])
            pe.wait_ge(sem("hk_done"), 2)
            for n in range(HEADS * T):
                h, t = n // T, n % T
                tt = slice(t * P, (t + 1) * P)
                m = full(ps[:, n // 4, (n % 4) * P:(n % 4 + 1) * P], hk[:, h, tt], hq[:, h, tt])
                if n % 4 == 3:
                    m.then_inc(sem("diag_ready"), 1)

            def level(l):
                m_ = 1 << l
                for half in range(2):
                    n = 2 * l + half
                    pe.wait_ge(sem("mult_done"), n + 1)
                    pe.wait_ge(sem("pred_done"), max(min(n + 1, 3), n))
                    for i in range(3):
                        h = 3 * half + i
                        if l < LEVELS - 1:
                            for t in range(T):
                                v = hE[:, h, t * P:(t + 1) * P]
                                qs = v.rearrange("p (b z m) -> p b z m", z=2, m=m_)[:, :, 1, :]
                                c = (2 * i + t) * 64
                                m = full(ps[:, n % 4, c:c + 64].rearrange("p (b m) -> p b m", m=m_), v, qs)
                        else:
                            m = full(ps[:, n % 4, i * P:(i + 1) * P], hE[:, h, 0:P], hE[:, h, P:S])
                    m.then_inc(sem("level_ready"), 1)

            for l in range(LEVELS):
                level(l)
                if l >= len(HG_UNITS):
                    continue
                u = HG_UNITS[l]
                b = (4, 5) if l % 2 == 0 else (6, 7)
                if l >= 2:
                    pe.wait_ge(s_evac, EV[HG_UNITS[l - 2]])
                else:
                    pe.wait_ge(sem("mkT_done"), 1)
                if u in (U_I, U_I + 1):
                    m = rows(u, 0, 384, b, h_hi, h_lo)
                elif u == U_MEM1:
                    pe.wait_ge(sem("memT_lo_done"), 2)
                    m = rows(u, 0, 384, b, y_hi, y_lo)
                elif u == U_MEM1 + 1:
                    rows(u, 0, P, b, y_hi, y_lo)
                    m = rows(u, P, MEM_W, b, h_hi, h_lo, col=P)
                else:
                    m = rows(u, 0, 384, b, h_hi, h_lo)
                m.then_inc(s_used, 1)
            pe.wait_ge(sem("pred_done"), 3 + 2 * LEVELS)
            for t in range(T):
                for h in range(HEADS):
                    o = ps[:, 2 * t + h // 4, (h % 4) * P:(h % 4 + 1) * P]
                    hs = slice(h * P, (h + 1) * P)
                    if t:
                        full(o, hO[:, h, :], hv[:, 0, hs], True, False)
                    m = full(o, hA[:, h * T + t, :], hv[:, t, hs], t == 0, True)
            m.then_inc(sem("hg_o_ready"), 1)
            pe.wait_ge(s_evac, EV[U_G + 1])
            mem_keys(1)
            pe.wait_ge(sem("ho_done"), T)
            for h in range(HEADS):
                for t in range(T):
                    m = pe.transpose(ps[:, h // 2, (h % 2) * S + t * P:(h % 2) * S + (t + 1) * P],
                                     ho[:, t, h * P:(h + 1) * P], ident)
                if h % 2:
                    m.then_inc(sem("yT_ready"), 1)
            pe.wait_ge(sem("mkT_done"), 2)
            mem_attention(0)

            def y_wait(i):
                return lambda k: pe.wait_ge(sem("y_ready"), KT * i + k + 1)

            kt_major(U_OUT0, y_hi, y_lo, y_wait(0))
            norm(1)
            ffn(0)

            norm(2)
            pe.wait_ge(sem("hT_ready"), 12)
            rows(U_MLA, 0, 384, (0, 1), h_hi, h_lo).then_inc(s_used, 1)
            rows(U_MLA + 1, 0, 320, (2, 3), h_hi, h_lo).then_inc(s_used, 1)
            rows(U_MLA + 2, 0, MEM_W, (4, 5), h_hi, h_lo).then_inc(s_used, 1)
            pe.wait_ge(sem("c_done"), 1)
            for i in range(5):
                src = cq[:, :, i * P:(i + 1) * P] if i < 3 else ckv[:, :, (i - 3) * P:(i - 2) * P]
                b = (6, 6, 7, 7, 0)[i]
                for t in range(T):
                    m = pe.transpose(ps[:, b, (i % 2) * S + t * P:(i % 2) * S + (t + 1) * P], src[:, t, :], ident)
                if i % 2 or i == 4:
                    m.then_inc(sem("cT_ready"), 1)
            pe.wait_ge(sem("cT_done"), 3)
            pe.wait_ge(s_evac, EV[U_MLA + 2])
            rows(U_UQ, 0, 384, (1, 2), y_hi, y_lo, 3, 768).then_inc(sem("uq_ready"), 1)
            rows(U_UQ, 384, 384, (3, 4), y_hi, y_lo, 3, 768).then_inc(s_used, 1)
            rows(U_UQ + 1, 0, 384, (5, 6), y_hi, y_lo, 3, 384).then_inc(s_used, 1)
            for j, b in enumerate(((7, 0), (1, 2), (3, 4))):
                if j:
                    pe.wait_ge(s_evac, EV[U_UQ])
                m = rows(U_UKV, 512 * j, 512, b, y_hi[:, 3:5, :], y_lo[:, 3:5, :], 2, 1536)
                m.then_inc(sem("ukv_ready") if j < 2 else s_used, 1)
            pe.wait_ge(sem("q_done"), 1)
            pe.wait_ge(sem("k_done"), 1)
            pe.wait_ge(s_evac, EV[U_UKV])

            def head_T(h):
                b = h % 2
                for n, (src, a, w) in enumerate(((q, h * QK, P), (q, h * QK + P, ROPE),
                                                 (kv, h * 256, P), (krh, h * ROPE, ROPE))):
                    for t in range(T):
                        m = pe.transpose(ps[0:w, 4 + n // 2, (n % 2) * S + t * P:(n % 2) * S + (t + 1) * P],
                                         src[:, t, a:a + w], ident)
                m.then_inc(sem("qkT_ready"), 1)

            def head_S(h):
                r = qkT[h % 2]
                pe.wait_ge(sem("qkT_done"), h + 1)
                if h >= 2:
                    pe.wait_ge(sem("mla_sm_done"), h - 1)
                for n, (t, s_) in enumerate(((0, 0), (1, 1), (1, 0))):
                    o = ps[:, h % 2, n * P:(n + 1) * P]
                    tt, ss = slice(t * P, t * P + P), slice(s_ * P, s_ * P + P)
                    full(o, r[:, 0, tt], r[:, 2, ss], True, False)
                    m = full(o, r[0:ROPE, 1, tt], r[0:ROPE, 3, ss], False, True)
                m.then_inc(sem("mla_s_ready"), 1)

            def head_P(h):
                pe.wait_ge(sem("mla_p_done"), h + 1)
                if h >= 2:
                    pe.wait_ge(sem("mla_pT_done"), h - 1)
                for n, at in enumerate((0, 2, 1)):
                    m = pe.transpose(ps[:, 2 + h % 2, n * P:(n + 1) * P], mp[h % 2][:, at, :], ident)
                m.then_inc(sem("mla_pT_ready"), 1)

            def head_O(h):
                pe.wait_ge(sem("mla_pT_done"), h + 1)
                if h >= 2:
                    pe.wait_ge(sem("y_ready"), KT + h - 1)
                o, vs = ps[:, 6 + h % 2, 0:S], slice(h * 256 + P, h * 256 + 256)
                pT = mpT[h % 2]
                full(o, kv[:, 0, vs], pT[:, 0:2, :].rearrange("p a b -> p (a b)"), True, False)
                full(ps[:, 6 + h % 2, P:S], kv[:, 1, vs], pT[:, 2, :], False, True).then_inc(sem("mla_o_ready"), 1)

            for i in range(HEADS + 3):
                if 1 <= i <= HEADS:
                    head_S(i - 1)
                if i < HEADS:
                    head_T(i)
                if 2 <= i <= HEADS + 1:
                    head_P(i - 2)
                if i >= 3:
                    head_O(i - 3)
            pe.wait_ge(sem("y_ready"), KT + HEADS)
            mem_attention(1)
            kt_major(U_OUT1, y_hi, y_lo, y_wait(1))
            norm(3)
            ffn(1)

            norm(4)
            ffn(2)
            norm(5)
            pe.wait_ge(sem("hT_ready"), 24)
            for n in range(4):
                u = U_IN2 + n
                if n >= 2:
                    pe.wait_ge(s_evac, EV[u - 2])
                for j in range(3):
                    m = cols(u, j, ps[:, (n % 2) * 2 + j // 2, (j % 2) * S:(j % 2) * S + S])
                m.then_inc(s_used, 1)
            rows(U_IN2 + 4, 0, 256, (4, 5), h_hi, h_lo)
            cols(U_IN2 + 4, 2, ps[:, 6, 0:S]).then_inc(s_used, 1)
            pe.wait_ge(s_evac, EV[U_IN2 + 2])
            rows(U_IN2 + 5, 0, 384, (0, 1), h_hi, h_lo).then_inc(s_used, 1)
            pe.wait_ge(s_evac, EV[U_IN2 + 3])
            rows(U_IN2 + 6, 0, 384, (2, 3), h_hi, h_lo).then_inc(s_used, 1)
            pe.wait_ge(s_evac, EV[U_IN2 + 4])
            for t in range(T):
                m = full(ps[:, 7, t * 256:(t + 1) * 256], glr[:, t * P:(t + 1) * P], V("gup", 0, 256))
            m.then_inc(sem("gate_ready"), 1)
            pe.wait_ge(sem("la_done"), 1)
            for f in range(2):
                for t in range(T):
                    m = full(ps[:, 6, f * S + t * P:f * S + (t + 1) * P], la[:, t, f * P:(f + 1) * P], tri)
            m.then_inc(sem("cum_ready"), 1)
            pe.wait_ge(sem("cy_done"), 1)
            for i in range(4):
                m = full(ps[:, 4, 0:S], ones, cy[:, i, :], i == 0, i == 3)
            m.then_inc(sem("mean_ready"), 1)
            pe.wait_ge(sem("ysq_done"), 1)
            for i in range(4):
                m = full(ps[:, 5, 0:S], ones, ga[:, i, :], i == 0, i == 3)
            m.then_inc(sem("var_ready"), 1)
            pe.wait_ge(s_evac, EV[U_IN2 + 6])
            pe.wait_ge(sem("gla_in_done"), 1)
            def pair_scores(bank, lhs, rhs):
                for par in range(2):
                    r = slice(par * 64, par * 64 + 64)
                    for f in range(2):
                        for t in range(T):
                            tt = slice(t * P, (t + 1) * P)
                            m = full(ps[:, bank + par, (2 * f + t) * P:(2 * f + t + 1) * P],
                                     lhs[r, f, tt], rhs[r, f, tt])
                return m
            pair_scores(0, kd, qd).then_inc(sem("g_s_ready"), 1)
            pe.wait_ge(sem("var_used"), 1)
            pair_scores(6, ku, qu).then_inc(sem("g_s_ready"), 1)
            pair_scores(4, ke, qd).then_inc(sem("g_s_ready"), 1)
            for par in range(2):
                r = slice(par * 64, par * 64 + 64)
                for f in range(2):
                    m = full(ps[:, 2 + par, f * P:(f + 1) * P], k7[r, f, :], q7[r, f, :])
            m.then_inc(sem("g_s_ready"), 1)
            pe.wait_ge(sem("gA_done"), 1)
            for t in range(T):
                for h in range(G_HEADS):
                    par, f = h % 2, h // 2
                    o, hs = ps[:, 6 + t, h * P:(h + 1) * P], slice(h * P, (h + 1) * P)
                    if t:
                        full(o, gO[par][:, f, :], gv[:, 0, hs], True, False)
                    m = full(o, gA[par][:, 2 * f + t, :], gv[:, t, hs], t == 0, True)
            m.then_inc(sem("g_o_ready"), 1)
            pe.wait_ge(sem("go_done"), T)
            for h in range(G_HEADS):
                for t in range(T):
                    m = pe.transpose(ps[:, 4 + h // 2, (h % 2) * S + t * P:(h % 2) * S + (t + 1) * P],
                                     go[:, t, h * P:(h + 1) * P], ident)
                if h % 2:
                    m.then_inc(sem("yT_ready"), 1)
            kt_major(U_OUT2, y_hi, y_lo, y_wait(2))
            norm(6)
            ffn(3)

            pe.wait_ge(sem("ple_loaded"), 16)
            pe.wait_ge(sem("x_done"), 14)
            for f in range(2):
                for t in range(T):
                    m = pe.transpose(ps[:, 4, f * S + t * P:f * S + (t + 1) * P], ple[:, t, f * P:(f + 1) * P], ident)
            m.then_inc(sem("pleT_ready"), 1)
            pe.wait_ge(sem("pleT_done"), 1)
            s = U_PROJ % SLOTS
            for k in range(2):
                pe.wait_ge(s_lo, pieces(U_PROJ, (k + 1) * D))
                for t in range(T):
                    tt = slice(t * P, (t + 1) * P)
                    for half in range(2):
                        r = slice(k * D + half * 512, k * D + half * 512 + 512)
                        m = three(ps[:, 2 * t + half, :], y_hi[:, 3 + k, tt], y_lo[:, 3 + k, tt],
                                  w_hi[:, s, r], w_lo[:, s, r], k == 0, k == 1)
            m.then_inc(s_used, 1)
            norm(7)
            pe.wait_ge(s_evac, EV[U_PROJ])
            kt_major(U_GATE, h_hi, h_lo, lambda k: pe.wait_ge(sem("hT_ready"), 4 * 7 + k // 2 + 1))

        @block.scalar
        def _(act):
            evac = Count(s_evac)

            def copy(o, i, scale=1.0):
                return act.activation(o, i, ACT.Copy, scale=scale)

            def hi(r, u, p):
                if u >= UNITS:
                    return
                s = u % SLOTS
                if p == 0:
                    act.wait_ge(rings[s], 16 * (u // SLOTS + 1) if r is None else r * 16 + 16 * (u // SLOTS + 1))
                    if u >= SLOTS:
                        act.wait_ge(s_used, u - 2 if r is None else r * 3 + (u - 2))
                a = slice(p * PIECE, (p + 1) * PIECE)
                copy(w_hi[:, s, a], raw[:, s, a]).then_inc(s_hi, 1)

            def split(u):
                for p in range(3):
                    hi(None, u, p)

            def unit(u, *moves):
                split(u + 2)
                act.wait_ge(s_used, u + 1)
                for move in moves[:-1]:
                    move()
                evac.inc(moves[-1]())

            def norm_a(i):
                if i:
                    act.wait_ge(sem("x_done"), 2 * i - 1)
                else:
                    act.wait_ge(sem("x_loaded"), 16)
                act.activation(junk[:, 0, :], x[:, 0, :], ACT.Square, accum_out=small[:, 0:1]).then_inc(sem("ss_done"), 1)
                act.wait_ge(sem("rstd_done"), i + 1)
                copy(xn[:, 0, :], x[:, 0, :], small[:, 72:73]).then_inc(sem("xn_done0"), 1)

            def norm_b(i, gain):
                for k in range(KT):
                    act.wait_ge(sem("xT_ready"), 4 * i + k // 2 + 1)
                    copy(h_hi[:, k, :], ps[:, 4 + k // 2, (k % 2) * S:(k % 2) * S + S], V(gain, k)).then_inc(sem("h_hi_done"), 1)

            def ffn(i):
                (U0, cw), n0 = FFNS[i], i * CH

                def at(r, n, per=3):
                    return n if r is None else r * per + n

                def body(r, j):
                    b, g = 4 + j % 3, j % 3
                    act.wait_ge(sem("up_ready"), at(r, n0 + j + 1))
                    if cw:
                        for z in range(2):
                            a = _cols[cw][0] + 8 * j + 4 * z

                            def w(n):
                                return vec[:, a + n:a + n + 1] if r is None else vec[:, bass.ds(r * 24 + (a + n), 1)]
                            m = act.activation(cv[:, g, z * S:(z + 1) * S], ps[:, b, z * S:(z + 1) * S],
                                               ACT.Identity, scale=w(2), bias=w(3))
                        m.then_inc(sem("ev_done"), 1)
                        hi(r, U0 + j + 2, 0)
                        act.wait_ge(sem("up_used"), at(r, UP0[i] + j + 1))
                        act.activation(sa[:, g, :], cv[:, g, 0:S], ACT.Silu).then_inc(sem("silu_done"), 1)
                    else:
                        act.activation(sa[:, g, :], ps[:, b, 0:S], ACT.Silu).then_inc(sem("silu_done"), 1)
                        hi(r, U0 + j + 2, 0)
                    hi(r, U0 + j + 2, 1)
                    act.wait_ge(sem("gate_done"), at(r, n0 + j + 1))
                    copy(y_hi[:, g, :], gg[:, g, :]).then_inc(sem("g_hi_done"), 1)
                    hi(r, U0 + j + 2, 2)

                body(None, 0)
                with act.Fori(0, (CH - 1) // 3) as r:
                    for j in range(1, 4):
                        body(r, j)
                split(U0 + CH + 2)

            def mem_kT(l):
                act.wait_ge(sem("mkT_ready"), l + 1)
                copy(mem_k[:, l, :, :].rearrange("p a b -> p (a b)"), ps[:, 4, :], V("mk", l)).then_inc(sem("mkT_done"), 1)

            def mem_attention(l):
                act.wait_ge(sem("ma_qT_ready"), l + 1)
                copy(ma_qT[:, :, :].rearrange("p a b -> p (a b)"), ps[:, 3, :], V("mq", l)).then_inc(sem("ma_qT_done"), 1)
                for g in range(4):
                    act.wait_ge(sem("ma_mx_done"), 4 * l + g + 1)
                    for pair in range(2):
                        n = 2 * g + pair
                        m = act.activation(ma_p[:, n, :], ps[:, 4 + g, pair * S:(pair + 1) * S], ACT.Exp,
                                           bias=small[:, 96 + n:97 + n], scale=MEM_HD ** -0.5,
                                           accum_out=small[:, 112 + n:113 + n])
                    m.then_inc(sem("ma_e_done"), 1)
                act.wait_ge(sem("ma_pT_ready"), l + 1)
                copy(ma_pT[:, 0:2, :].rearrange("p a b -> p (a b)"), ps[:, 0, :])
                copy(ma_pT[:, 2:4, :].rearrange("p a b -> p (a b)"), ps[:, 1, :]).then_inc(sem("ma_pT_done0"), 1)
                act.wait_ge(sem("ma_o_ready"), l + 1)
                copy(y_hi[:, 6:8, :].rearrange("p a b -> p (a b)"), ps[:, 4, :]).then_inc(sem("ma_y_hi"), 1)

            act.wait_ge(sem("vec_loaded"), 16)
            act.wait_ge(sem("lb_max"), 1)
            act.activation(small[:, 144:162], small[:, 144:162], ACT.Exp).then_inc(sem("lb_exp"), 1)
            act.wait_ge(sem("mem_loaded"), 16)
            act.activation(memn[:, 0:4, :].rearrange("p a b -> p (a b)"), junk[:, 0, :], ACT.Square,
                               accum_out=small[:, 0:1]).then_inc(sem("mss_done"), 1)
            act.wait_ge(sem("mrstd_done"), 1)
            copy(junk[:, 0, :], junk[:, 0, :], small[:, 72:73]).then_inc(sem("mn_done0"), 1)
            split(0)
            for b in range(4):
                act.wait_ge(sem("mnT_ready"), b + 1)
                m = copy(memn[:, 2 * b:2 * b + 2, :].rearrange("p a b -> p (a b)"), ps[:, 4 + b, :])
                m.then_inc(sem("memn_done"), 1)
            for k in range(KT):
                act.wait_ge(sem("memn_done"), k // 2 + 1)
                copy(y_hi[:, k, :], memn[:, k, :], V("mem0", k)).then_inc(sem("memT_hi_done"), 1)
            split(1)
            norm_a(0)
            unit(0, *[lambda t=t: copy(mk_tok[0][:, t, :], ps[:, t, 0:256]) for t in range(T)],
                 *[lambda t=t: copy(mem_v[:, 0, t, 0:P], ps[:, t, 256:384]) for t in range(T)])
            unit(1, *[lambda t=t: copy(mem_v[:, 0, t, P:256], ps[:, 2 + t, 0:P]) for t in range(T)])
            norm_b(0, "mix0")
            for k in range(KT):
                copy(y_hi[:, k, :], memn[:, k, :], V("mem1", k)).then_inc(sem("memT_hi_done"), 1)
            act.wait_ge(sem("ang_done"), 1)
            act.activation(trig[:, 0, :, :], tr[1], ACT.Sin).then_inc(sem("cos_done"), 1)
            act.activation(trig[:, 1, :, :], tr[0], ACT.Sin).then_inc(sem("sin_done"), 1)
            for n in range(2):
                h = 3 * n
                unit(U_F + n,
                     lambda: act.activation(hk[:, h:h + 2, :].rearrange("p a b -> p (a b)"), ps[:, 2 * n, :], ACT.Sigmoid),
                     lambda: act.activation(hk[:, h + 2, :], ps[:, 2 * n + 1, 0:S], ACT.Sigmoid))
            mem_kT(0)
            for n in range(2):
                h = 3 * n
                unit(U_Q + n,
                     lambda: act.activation(hq[:, h:h + 2, :].rearrange("p a b -> p (a b)"), ps[:, 2 * n, :], ACT.Silu),
                     lambda: act.activation(hq[:, h + 2, :], ps[:, 2 * n + 1, 0:S], ACT.Silu))
            for half in range(2):
                act.wait_ge(sem("fg_done"), half + 1)
                v = hD[:, 3 * half:3 * half + 3, :].rearrange("p a b -> p (a b)")
                act.activation(v, v, ACT.Ln).then_inc(sem("ln_done"), 1)

            def exps(l):
                m = 1 << l
                for half in range(2):
                    hh = slice(3 * half, 3 * half + 3)
                    if l:
                        act.wait_ge(sem("upd_done"), 2 * (l - 1) + half + 1)
                        act.wait_ge(sem("level_ready"), 2 * (l - 1) + half + 1)
                    else:
                        act.wait_ge(sem("ln_done"), half + 1)
                        act.wait_ge(sem("r_zero"), 1)
                    act.activation(right(hE[:, hh, :], m), right(hD[:, hh, :], m), ACT.Exp)
                    act.activation(left(hE[:, hh, :], m), left(hR[:, hh, :], m), ACT.Exp).then_inc(sem("exp_done"), 1)

            def tok(dst, b, n, a=0, col=0):
                return [lambda t=t: copy(dst[:, t, a:a + n], ps[:, b + t, col:col + n]) for t in range(T)]

            exps(0)
            for l in range(LEVELS - 1):
                exps(l + 1)
                if l >= len(HG_UNITS):
                    continue
                u = HG_UNITS[l]
                b = 4 if l % 2 == 0 else 6
                if u in (U_I, U_I + 1):
                    unit(u, *tok(hv, b, 384, (u - U_I) * 384))
                elif u == U_MEM1:
                    unit(u, *tok(mk_tok[1], b, 256), *tok(mem_v[:, 1], b, P, 0, 256))
                elif u == U_MEM1 + 1:
                    unit(u, *tok(mem_v[:, 1], b, P, P), *tok(qm0, b, MEM_W, 0, P))
                else:
                    split(u + 2)
            act.wait_ge(sem("mult_done"), 2 * LEVELS)
            for n in range(2):
                u = U_G + n
                act.wait_ge(s_used, u + 1)
                for t in range(T):
                    m = act.activation(hg[:, t, n * 384:(n + 1) * 384], ps[:, 4 + 2 * n + t, 0:384], ACT.Silu)
                evac.inc(m)
            act.wait_ge(sem("hg_o_ready"), 1)
            for t in range(T):
                copy(ho[:, t, 0:512], ps[:, 2 * t, :])
                copy(ho[:, t, 512:HW], ps[:, 2 * t + 1, 0:256]).then_inc(sem("ho_copied"), 1)
            mem_kT(1)
            for h in range(HEADS):
                act.wait_ge(sem("yT_ready"), h // 2 + 1)
                copy(y_hi[:, h, :], ps[:, h // 2, (h % 2) * S:(h % 2) * S + S], V("hgn")).then_inc(sem("y_hi_done"), 1)
            mem_attention(0)
            for u in range(U_OUT0, U_OUT0 + 3):
                split(u + 2)
            norm_a(1)
            norm_b(1, "ffn0")
            ffn(0)

            norm_a(2)
            norm_b(2, "mix1")
            unit(U_MLA, *tok(cq, 0, 384))
            unit(U_MLA + 1, *tok(ckv, 2, 320))
            unit(U_MLA + 2, *tok(qm1, 4, MEM_W))
            for i in range(5):
                b = (6, 6, 7, 7, 0)[i]
                act.wait_ge(sem("cT_ready"), (1, 1, 2, 2, 3)[i])
                g = V("qa", i) if i < 3 else V("kva", i - 3)
                copy(y_hi[:, i, :], ps[:, b, (i % 2) * S:(i % 2) * S + S], g).then_inc(sem("cT_hi_done"), 1)
            split(U_UQ + 2)
            act.wait_ge(sem("uq_ready"), 1)
            for m in tok(q, 1, 384):
                m()
            act.wait_ge(s_used, U_UQ + 1)
            for m in tok(q, 3, 384, 384)[:-1]:
                m()
            evac.inc(tok(q, 3, 384, 384)[-1]())
            unit(U_UQ + 1, *tok(q, 5, 384, 768))
            split(U_UKV + 2)
            act.wait_ge(sem("ukv_ready"), 1)
            copy(kv[:, 0, 0:512], ps[:, 7, :])
            copy(kv[:, 1, 0:512], ps[:, 0, :]).then_inc(sem("kv_copied"), 1)
            act.wait_ge(sem("ukv_ready"), 2)
            for t in range(T):
                m = copy(kv[:, t, 512:1024], ps[:, 1 + t, :])
            m.then_inc(sem("kv_copied"), 1)
            act.wait_ge(s_used, U_UKV + 1)
            for t in range(T):
                m = copy(kv[:, t, 1024:1536], ps[:, 3 + t, :])
            evac.inc(m)

            def head_T(h):
                act.wait_ge(sem("qkT_ready"), h + 1)
                if h >= 2:
                    act.wait_ge(sem("mla_s_ready"), h - 1)
                r = qkT[h % 2]
                for n in range(2):
                    copy(r[:, 2 * n, :], ps[:, 4 + n, 0:S])
                    m = copy(r[0:ROPE, 2 * n + 1, :], ps[0:ROPE, 4 + n, S:2 * S])
                m.then_inc(sem("qkT_done"), 1)

            def head_E(h):
                act.wait_ge(sem("mla_mx_done"), h + 1)
                p, c = mp[h % 2], 2 * (h % 2)
                act.activation(p[:, 0, :], p[:, 0, :], ACT.Exp, bias=small[:, 96 + c:97 + c],
                               accum_out=small[:, 112 + c:113 + c])
                v = p[:, 1:3, :].rearrange("p a b -> p (a b)")
                act.activation(v, v, ACT.Exp, bias=small[:, 97 + c:98 + c],
                                   accum_out=small[:, 113 + c:114 + c]).then_inc(sem("mla_e_done"), 1)

            def head_O(h):
                act.wait_ge(sem("mla_o_ready"), h + 1)
                copy(y_hi[:, h, :], ps[:, 6 + h % 2, 0:S]).then_inc(sem("y_hi_done"), 1)

            for i in range(HEADS + 3):
                if i < HEADS:
                    head_T(i)
                if 1 <= i <= HEADS:
                    head_E(i - 1)
                if i >= 3:
                    head_O(i - 3)
            mem_attention(1)
            for u in range(U_OUT1, U_OUT1 + 3):
                split(u + 2)
            norm_a(3)
            norm_b(3, "ffn1")
            ffn(1)

            norm_a(4)
            norm_b(4, "ffn2")
            ffn(2)
            norm_a(5)
            norm_b(5, "mix2")
            spots = [(ga, 0), (gs, 0), (ga, 1), (gs, 1), (ga, 2), (gs, 2), (ga, 3), (gs, 3),
                     (gq, 0), (gq, 1), (gk, 0), (gk, 1)]
            for n in range(4):
                def spot(j):
                    dst, i = spots[3 * n + j]
                    return act.activation(dst[:, i, :], ps[:, (n % 2) * 2 + j // 2, (j % 2) * S:(j % 2) * S + S],
                                          ACT.Sigmoid if dst is gs else ACT.Copy)
                unit(U_IN2 + n, *[lambda j=j: spot(j) for j in range(3)])
            unit(U_IN2 + 4,
                 *[lambda t=t: act.activation(gr[:, t, 256:512], ps[:, 4 + t, 0:256], ACT.Silu) for t in range(T)],
                 lambda: copy(glr, ps[:, 6, 0:S]))
            unit(U_IN2 + 5, *tok(gv, 0, 384))
            unit(U_IN2 + 6, *tok(gv, 2, P, 384),
                 *[lambda t=t: act.activation(gr[:, t, 0:256], ps[:, 2 + t, P:384], ACT.Silu) for t in range(T)])
            act.wait_ge(sem("gl_done"), 1)
            act.activation(g_abs, la, ACT.Abs).then_inc(sem("ga1"), 1)
            act.wait_ge(sem("ga1"), 1)
            act.activation(g_abs, g_abs, ACT.Exp, scale=-1.0).then_inc(sem("ga2"), 1)
            act.wait_ge(sem("ga2"), 1)
            act.activation(g_abs, g_abs, ACT.Ln, bias=1.0).then_inc(sem("g_ln_done"), 1)
            act.wait_ge(sem("cum_ready"), 1)
            copy(cum[:, :, :].rearrange("p a b -> p (a b)"), ps[:, 6, :]).then_inc(sem("cum_copied"), 1)
            for i in range(4):
                act.wait_ge(sem("yn_done"), 1)
                act.activation(ga[:, i, :], cy[:, i, :], ACT.Silu, scale=V("lng", i), bias=V("lnb", i)).then_inc(sem("cs_done"), 1)
            for i in range(4):
                act.wait_ge(sem("cs_done"), i + 1)
                copy(y_hi[:, i, :], ga[:, i, :]).then_inc(sem("y_hi_done"), 1)
            act.wait_ge(sem("conv_done"), 1)
            act.activation(ep, cum, ACT.Exp, scale=1.0 / 16)
            act.activation(en, cum, ACT.Exp, scale=-1.0 / 16).then_inc(sem("gexp_done"), 1)
            act.wait_ge(sem("ec_in_done"), 1)
            act.activation(ec, ec, ACT.Exp, scale=1.0 / 16).then_inc(sem("gexp_done"), 1)
            act.wait_ge(sem("g_o_ready"), 1)
            for t in range(T):
                copy(go[:, t, :], ps[:, 6 + t, :]).then_inc(sem("go_copied"), 1)
            for h in range(G_HEADS):
                act.wait_ge(sem("yT_ready"), 3 + h // 2 + 1)
                copy(y_hi[:, 4 + h, :], ps[:, 4 + h // 2, (h % 2) * S:(h % 2) * S + S], V("glan", h)).then_inc(sem("y_hi_done"), 1)
            for u in range(U_OUT2, U_OUT2 + 3):
                split(u + 2)
            norm_a(6)
            norm_b(6, "ffn3")
            ffn(3)
            act.wait_ge(sem("pleT_ready"), 1)
            copy(y_hi[:, 3:5, :].rearrange("p a b -> p (a b)"), ps[:, 4, :]).then_inc(sem("ple_hi_done"), 1)
            norm_a(7)
            unit(U_PROJ, *[lambda b=b: copy(proj[:, b // 2, (b % 2) * 512:(b % 2) * 512 + 512], ps[:, b, :])
                           for b in range(4)])
            norm_b(7, "ple")
            for u in range(U_GATE, U_GATE + 3):
                split(u + 2)
            act.wait_ge(s_used, UNITS)
            for b in range(4):
                act.activation(sg[:, b // 2, (b % 2) * 512:(b % 2) * 512 + 512], ps[:, b, :], ACT.Sigmoid).then_inc(sem("sg_done"), 1)
            act.wait_ge(sem("x_done"), 15)
            act.activation(junk[:, 0, :], x[:, 0, :], ACT.Square, accum_out=small[:, 0:1]).then_inc(sem("ss_done"), 1)

        @block.vector
        def _(dve):
            chain = Count(s_chain)

            def link(ins):
                chain.inc(ins)
                dve.wait_ge(s_chain, chain.at(chain.n))

            def lo(r, u, p):
                if u >= UNITS:
                    return
                n = 3 * u + p + 1
                dve.wait_ge(s_hi, n if r is None else r * 9 + n)
                s, a = u % SLOTS, slice(p * PIECE, (p + 1) * PIECE)
                dve.tensor_tensor(w_lo[:, s, a], raw[:, s, a], w_hi[:, s, a], ALU.subtract).then_inc(s_lo, 1)

            def split(u):
                for p in range(3):
                    lo(None, u, p)

            def rsqrt(out_, mean, n, t1, t2, scale=1.0):
                link(dve.tensor_scalar(t1, mean, scale, EPS, ALU.mult, ALU.add))
                link(dve.tensor_scalar(t2.bitcast(I32), t1.bitcast(I32), 1, None, ALU.logical_shift_right))
                link(dve.tensor_scalar(out_.bitcast(I32), t2.bitcast(I32), -1.0, float(0x5F3759DF), ALU.mult, ALU.add))
                for step in range(3):
                    link(dve.tensor_tensor(t2, out_, out_, ALU.mult))
                    link(dve.scalar_tensor_tensor(t2, t2, -0.5, t1, ALU.mult, ALU.mult))
                    link(dve.scalar_tensor_tensor(out_, t2, 1.5, out_, ALU.add, ALU.mult))

            def stat(n):
                return small[:, 72:72 + n], small[:, 0:n], n, small[:, 24:24 + n], small[:, 48:48 + n]

            def squares(o, i, acc, scale=1.0):
                return dve.tensor_tensor_reduce(o, i, i, scale, 0.0, ALU.mult, ALU.add, acc)

            def norm_a(i):
                if i:
                    dve.wait_ge(sem("x_done"), 2 * i)
                else:
                    dve.wait_ge(sem("x_loaded"), 16)
                link(squares(junk[:, 1, :], x[:, 1, :], small[:, 1:2]))
                dve.wait_ge(sem("ss_done"), i + 1)
                rsqrt(*stat(2), scale=1.0 / D)
                dve.tensor_copy(small[:, 71:72], small[:, 72:73]).then_inc(sem("rstd_done"), 1)
                dve.tensor_scalar(xn[:, 1, :], x[:, 1, :], small[:, 73:74], None, ALU.mult).then_inc(sem("xn_done1"), 1)

            def norm_b(i, gain):
                for k in range(KT):
                    dve.wait_ge(sem("h_hi_done"), 8 * i + 2 * (k // 2) + 2)
                    m = dve.scalar_tensor_tensor(h_lo[:, k, :], ps[:, 4 + k // 2, (k % 2) * S:(k % 2) * S + S],
                                                 V(gain, k), h_hi[:, k, :], ALU.mult, ALU.subtract)
                    if k % 2:
                        m.then_inc(sem("hT_ready"), 1)

            def residual(scale=1.0):
                for t in range(T):
                    for half in range(2):
                        r = slice(half * 512, half * 512 + 512)
                        m = dve.scalar_tensor_tensor(x[:, t, r], ps[:, 2 * t + half, :], scale, x[:, t, r],
                                                     ALU.mult, ALU.add)
                    m.then_inc(sem("x_done"), 1)

            def ffn(i):
                (U0, cw), n0 = FFNS[i], i * CH

                def at(r, n, per=3):
                    return n if r is None else r * per + n

                def body(r, j):
                    b, g = 4 + j % 3, j % 3
                    if cw:
                        dve.wait_ge(sem("ev_done"), at(r, UP0[i] + j + 1))
                        marks = []
                        for tap in (1, 0):
                            for z in range(2):
                                col = _cols[cw][0] + 8 * j + 4 * z + tap
                                w = vec[:, col:col + 1] if r is None else vec[:, bass.ds(r * 24 + col, 1)]
                                d = 2 - tap
                                c = cv[:, g, z * S + d:(z + 1) * S]
                                if tap == 0:
                                    dve.wait_ge(s_chain, chain.at(marks[z]))
                                m = dve.scalar_tensor_tensor(c, ps[:, b, z * S:(z + 1) * S - d], w, c,
                                                             ALU.mult, ALU.add)
                                if tap:
                                    marks.append(chain.inc(m))
                        m.then_inc(sem("up_used"), 1)
                        lo(r, U0 + j + 2, 0)
                        dve.wait_ge(sem("up_used"), at(r, UP0[i] + j + 1))
                        dve.wait_ge(sem("silu_done"), at(r, n0 + j + 1))
                        other = cv[:, g, S:2 * S]
                    else:
                        dve.wait_ge(sem("silu_done"), at(r, n0 + j + 1))
                        other = ps[:, b, S:2 * S]
                    dve.tensor_tensor(gg[:, g, :], sa[:, g, :], other, ALU.mult).then_inc(sem("gate_done"), 1)
                    if not cw:
                        lo(r, U0 + j + 2, 0)
                    lo(r, U0 + j + 2, 1)
                    dve.wait_ge(sem("g_hi_done"), at(r, n0 + j + 1))
                    dve.tensor_tensor(y_lo[:, g, :], gg[:, g, :], y_hi[:, g, :], ALU.subtract).then_inc(sem("g_lo_done"), 1)
                    lo(r, U0 + j + 2, 2)

                body(None, 0)
                with dve.Fori(0, (CH - 1) // 3) as r:
                    chain.enter(r, 6 if cw else 0)
                    for j in range(1, 4):
                        body(r, j)
                    chain.leave((CH - 1) // 3)
                split(U0 + CH + 2)
                dve.wait_ge(s_used, U0 + FFN_UNITS)
                residual(1.0 if cw else 0.5)

            def head_sums(sq, groups, w):
                v = sq.rearrange("p t (h w) -> p (t h) w", w=w)
                link(dve.tensor_reduce(small[:, 0:groups], v, AX, ALU.add))

            def mem_keys(l):
                src = mk_tok[l]
                dve.wait_ge(s_evac, EV[(U_MEM0, U_MEM1)[l]])
                link(dve.tensor_tensor(mk_sq, src, src, ALU.mult))
                head_sums(mk_sq, 8, MEM_HD)
                rsqrt(*stat(8), scale=1.0 / MEM_HD)
                v = src.rearrange("p t (h w) -> p (t h) w", w=MEM_HD)
                dve.tensor_tensor(v, v, small[:, 72:80].unsqueeze(2).to_broadcast([P, 8, MEM_HD]), ALU.mult).then_inc(sem("mk_done"), 1)

            def mem_attention(l):
                qm = (qm0, qm1)[l]
                link(dve.tensor_tensor(ma_sq, qm, qm, ALU.mult))
                head_sums(ma_sq, 8, MEM_HD)
                rsqrt(*stat(8), scale=1.0 / MEM_HD)
                v = qm.rearrange("p t (h w) -> p (t h) w", w=MEM_HD)
                dve.tensor_tensor(v, v, small[:, 72:80].unsqueeze(2).to_broadcast([P, 8, MEM_HD]), ALU.mult).then_inc(sem("ma_q_done"), 1)
                for g in range(4):
                    dve.wait_ge(sem("ma_s_ready"), 4 * l + g + 1)
                    n = 2 * g
                    link(dve.tensor_reduce(small[:, 128 + n:130 + n],
                                           ps[:, 4 + g, :].rearrange("p (a b) -> p a b", b=S), AX, ALU.max))
                    dve.tensor_scalar(small[:, 96 + n:98 + n], small[:, 128 + n:130 + n], -MEM_HD ** -0.5, None,
                                          ALU.mult).then_inc(sem("ma_mx_done"), 1)
                for g in range(4):
                    n = 2 * g
                    dve.wait_ge(sem("ma_e_done"), 4 * l + g + 1)
                    link(dve.reciprocal(small[:, 128 + n:130 + n], small[:, 112 + n:114 + n]))
                    for i in range(n, n + 2):
                        m = dve.tensor_scalar(ma_p[:, i, :], ma_p[:, i, :], small[:, 128 + i:129 + i], None, ALU.mult)
                    m.then_inc(sem("ma_p_done"), 1)
                dve.wait_ge(sem("ma_pT_ready"), l + 1)
                dve.tensor_copy(ma_pT[:, 4:6, :].rearrange("p a b -> p (a b)"), ps[:, 2, :])
                dve.tensor_copy(ma_pT[:, 6:8, :].rearrange("p a b -> p (a b)"), ps[:, 3, :]).then_inc(sem("ma_pT_done1"), 1)
                dve.wait_ge(sem("ma_y_hi"), l + 1)
                for i in range(2):
                    dve.tensor_tensor(y_lo[:, 6 + i, :], ps[:, 4, i * S:(i + 1) * S], y_hi[:, 6 + i, :],
                                          ALU.subtract).then_inc(sem("y_ready"), 1)

            dve.wait_ge(sem("vec_loaded"), 16)
            e = small[:, 144:162]
            lg = V("lb", 0, 18).rearrange("p (l h) -> p l h", h=HEADS)
            link(dve.tensor_tensor(small[:, 162:168], lg[:, 0, :], lg[:, 1, :], ALU.max))
            link(dve.tensor_tensor(small[:, 162:168], small[:, 162:168], lg[:, 2, :], ALU.max))
            dve.tensor_tensor(e.rearrange("p (l h) -> p l h", h=HEADS), lg,
                                  small[:, 162:168].unsqueeze(1).to_broadcast([P, 3, HEADS]), ALU.subtract).then_inc(sem("lb_max"), 1)
            dve.wait_ge(sem("mem_loaded"), 16)
            link(squares(memn[:, 4:8, :].rearrange("p a b -> p (a b)"), junk[:, 1, :], small[:, 1:2]))
            dve.wait_ge(sem("mss_done"), 1)
            rsqrt(*stat(2), scale=1.0 / D)
            dve.tensor_copy(small[:, 71:72], small[:, 72:73]).then_inc(sem("mrstd_done"), 1)
            dve.tensor_scalar(junk[:, 1, :], junk[:, 1, :], small[:, 73:74], None, ALU.mult).then_inc(sem("mn_done1"), 1)
            split(0)

            def mem_T(l):
                for k in range(KT):
                    dve.wait_ge(sem("memT_hi_done"), 8 * l + k + 1)
                    m = dve.scalar_tensor_tensor(y_lo[:, k, :], memn[:, k, :], V(f"mem{l}", k), y_hi[:, k, :],
                                                 ALU.mult, ALU.subtract)
                m.then_inc(sem("memT_lo_done"), 1)

            mem_T(0)
            split(1)
            norm_a(0)
            split(2)
            split(3)
            norm_b(0, "mix0")
            mem_keys(0)
            mem_T(1)
            dve.wait_ge(sem("pos_loaded"), 16)
            link(dve.tensor_copy(small[:, 188:190], small[:, 186:188].bitcast(I32)))
            for t in range(T):
                m = dve.tensor_scalar(tr[0][:, t, :], V("inv", 0, HALF), small[:, 188 + t:189 + t], None, ALU.mult)
            link(m)
            link(dve.tensor_scalar(tr[2], tr[0], float(1 / (2 * np.pi)), None, ALU.mult))
            link(dve.tensor_scalar(tr[2], tr[2], 12582912.0, None, ALU.add))
            link(dve.tensor_scalar(tr[2], tr[2], -12582912.0, None, ALU.add))
            for part in TWO_PI:
                link(dve.scalar_tensor_tensor(tr[0], tr[2], -part, tr[0], ALU.mult, ALU.add))
            link(dve.tensor_scalar(tr[1], tr[0], float(np.pi / 2), None, ALU.add))
            link(dve.tensor_scalar(tr[3], tr[1], float(np.pi), float(-2 * np.pi), ALU.is_gt, ALU.mult))
            link(dve.tensor_tensor(tr[1], tr[1], tr[3], ALU.add))
            link(dve.tensor_scalar(tr[1], tr[1], 3.1415925, -3.1415925, ALU.min, ALU.max))
            dve.tensor_scalar(tr[0], tr[0], 3.1415925, -3.1415925, ALU.min, ALU.max).then_inc(sem("ang_done"), 1)
            dve.wait_ge(sem("msk_loaded"), 16)
            link(dve.tensor_copy(msk[:, :], msk_f))
            dve.wait_ge(sem("lb_exp"), 1)
            ev = e.rearrange("p (l h) -> p l h", h=HEADS)
            link(dve.tensor_tensor(small[:, 162:168], ev[:, 0, :], ev[:, 1, :], ALU.add))
            link(dve.tensor_tensor(small[:, 162:168], small[:, 162:168], ev[:, 2, :], ALU.add))
            link(dve.reciprocal(small[:, 168:174], small[:, 162:168]))
            link(dve.tensor_tensor(small[:, 162:168], ev[:, 0, :], small[:, 168:174], ALU.mult))
            link(dve.tensor_scalar(small[:, 168:174], small[:, 162:168], -1.0, 1.0, ALU.mult, ALU.add))
            dve.memset(A(4608, HEADS * S), 0.0).then_inc(sem("r_zero"), 1)
            for half in range(2):
                split(U_F + half + 2)
                dve.wait_ge(s_evac, EV[U_F + half])
                for h in range(3 * half, 3 * half + 3):
                    m = dve.tensor_scalar(hD[:, h, :], hk[:, h, :], small[:, 168 + h:169 + h],
                                          small[:, 162 + h:163 + h], ALU.mult, ALU.add)
                link(m)
                hh = slice(3 * half, 3 * half + 3)
                dve.tensor_scalar(hk[:, hh, :], hD[:, hh, :], -1.0, 1.0, ALU.mult, ALU.add).then_inc(sem("hk_done"), 1)
                dve.tensor_scalar(hD[:, hh, :], hD[:, hh, :], 2.0 ** -63, None, ALU.max).then_inc(sem("fg_done"), 1)
            split(U_Q + 2)
            split(U_Q + 3)
            qs = P ** -0.5
            for b in range(3):
                dve.wait_ge(sem("diag_ready"), b + 1)
                dve.scalar_tensor_tensor(hA[:, 4 * b:4 * b + 4, :], ps[:, b, :].rearrange("p (a b) -> p a b", b=P),
                                             qs, ident.unsqueeze(1).to_broadcast([P, 4, P]), ALU.mult, ALU.mult).then_inc(sem("pred_done"), 1)

            def decays(l):
                m = 1 << l
                for half in range(2):
                    hh = slice(3 * half, 3 * half + 3)
                    dve.wait_ge(sem("exp_done"), 2 * l + half + 1)
                    dve.scalar_tensor_tensor(right(hE[:, hh, :], m), right(hq[:, hh, :], m), qs,
                                             right(hE[:, hh, :], m), ALU.mult, ALU.mult)
                    dve.tensor_tensor(left(hE[:, hh, :], m), left(hk[:, hh, :], m), left(hE[:, hh, :], m),
                                          ALU.mult).then_inc(sem("mult_done"), 1)
                for half in range(2 if l < LEVELS - 1 else 0):
                    hh = slice(3 * half, 3 * half + 3)
                    rD, lD, lR = right(hD[:, hh, :], m), left(hD[:, hh, :], m), left(hR[:, hh, :], m)
                    n = 3 * S // (2 * m)
                    link(dve.tensor_tensor(lR, lR, rD[:, :, m - 1:m].to_broadcast([P, n, m]), ALU.add))
                    dve.tensor_tensor(rD, rD, lD[:, :, m - 1:m].to_broadcast([P, n, m]), ALU.add).then_inc(sem("upd_done"), 1)

            def place(l):
                m = 1 << l
                for half in range(2):
                    n = 2 * l + half
                    dve.wait_ge(sem("level_ready"), n + 1)
                    if l < LEVELS - 1:
                        dst = hA[:, 6 * half:6 * half + 6, :].rearrange("p a (b z m) -> p a b z m", z=2, m=m)[:, :, :, 1, :]
                        mk = msk[:, l * 64:(l + 1) * 64].rearrange("p (b m) -> p b m", m=m).unsqueeze(1)\
                            .to_broadcast([P, 6, 64 // m, m])
                        src = ps[:, n % 4, 0:384].rearrange("p (a b m) -> p a b m", a=6, m=m)
                        dve.copy_predicated(dst, mk, src).then_inc(sem("pred_done"), 1)
                    else:
                        dve.tensor_copy(hO[:, 3 * half:3 * half + 3, :].rearrange("p a b -> p (a b)"),
                                            ps[:, n % 4, 0:384]).then_inc(sem("pred_done"), 1)

            decays(0)
            for l in range(LEVELS):
                if l < LEVELS - 1:
                    dve.wait_ge(sem("upd_done"), 2 * l + 2)
                    decays(l + 1)
                if l == 4:
                    mem_keys(1)
                if l < len(HG_UNITS):
                    split(HG_UNITS[l] + 2)
                if l:
                    dve.wait_ge(sem("pred_done"), 3 + 2 * l)
                else:
                    dve.wait_ge(sem("pred_done"), 3)
                place(l)
            for t in range(T):
                dve.wait_ge(sem("ho_copied"), t + 1)
                link(dve.tensor_tensor(hsq[:, t, :], ho[:, t, :], ho[:, t, :], ALU.mult))
            head_sums(hsq, 12, P)
            rsqrt(*stat(12), scale=1.0 / P)
            dve.wait_ge(s_evac, EV[U_G + 1])
            for t in range(T):
                for h in range(HEADS):
                    v = ho[:, t, h * P:(h + 1) * P]
                    i = 72 + t * HEADS + h
                    m = dve.scalar_tensor_tensor(v, v, small[:, i:i + 1], hg[:, t, h * P:(h + 1) * P],
                                                 ALU.mult, ALU.mult)
                m.then_inc(sem("ho_done"), 1)

            def y_lo_from(k, b, col, gain, n):
                dve.wait_ge(sem("y_hi_done"), n)
                src = ps[:, b, col:col + S]
                if gain is None:
                    m = dve.tensor_tensor(y_lo[:, k, :], src, y_hi[:, k, :], ALU.subtract)
                else:
                    m = dve.scalar_tensor_tensor(y_lo[:, k, :], src, gain, y_hi[:, k, :], ALU.mult, ALU.subtract)
                m.then_inc(sem("y_ready"), 1)

            for h in range(HEADS):
                y_lo_from(h, h // 2, (h % 2) * S, V("hgn"), 2 * (h // 2) + 2)
            mem_attention(0)
            for u in range(U_OUT0, U_OUT0 + 3):
                split(u + 2)
            dve.wait_ge(s_used, U_OUT0 + 3)
            dve.wait_ge(sem("x_back"), 16)
            residual()
            norm_a(1)
            norm_b(1, "ffn0")
            ffn(0)

            norm_a(2)
            norm_b(2, "mix1")
            split(U_MLA + 2)
            dve.wait_ge(s_evac, EV[U_MLA])
            for t in range(T):
                link(squares(rt[0][:, :, :].rearrange("p a b -> p (a b)"), cq[:, t, :], small[:, t:t + 1], 1.0 / 384))
            split(U_MLA + 3)
            dve.wait_ge(s_evac, EV[U_MLA + 1])
            for t in range(T):
                link(squares(rt[0][:, :, :].rearrange("p a b -> p (a b)")[:, 0:256], ckv[:, t, 0:256],
                             small[:, 2 + t:3 + t], 1.0 / 256))
                link(squares(kr[:, t, :], ckv[:, t, 256:320], small[:, 190 + t:191 + t], 1.0 / QK))
            rsqrt(*stat(4))
            for t in range(T):
                dve.tensor_scalar(cq[:, t, :], cq[:, t, :], small[:, 72 + t:73 + t], None, ALU.mult)
            for t in range(T):
                m = dve.tensor_scalar(ckv[:, t, 0:256], ckv[:, t, 0:256], small[:, 74 + t:75 + t], None, ALU.mult)
            m.then_inc(sem("c_done"), 1)
            for i in range(5):
                b = (6, 6, 7, 7, 0)[i]
                g = V("qa", i) if i < 3 else V("kva", i - 3)
                dve.wait_ge(sem("cT_hi_done"), (2, 2, 4, 4, 5)[i])
                m = dve.scalar_tensor_tensor(y_lo[:, i, :], ps[:, b, (i % 2) * S:(i % 2) * S + S], g, y_hi[:, i, :],
                                             ALU.mult, ALU.subtract)
                if i in (1, 3, 4):
                    m.then_inc(sem("cT_done"), 1)
            split(U_MLA + 4)
            cosb, sinb = trig[:, 0, :, :], trig[:, 1, :, :]
            link(dve.tensor_tensor(kr, ckv[:, :, 256:320], V("kn", P, ROPE).unsqueeze(1).to_broadcast([P, T, ROPE]),
                                   ALU.mult))
            dve.wait_ge(sem("cos_done"), 1)
            dve.wait_ge(sem("sin_done"), 1)
            x1, x2 = kr[:, :, 0:HALF], kr[:, :, HALF:ROPE]
            k4 = [rt[i][:, :, 0:HALF] for i in range(4)]
            dve.tensor_tensor(k4[0], x1, cosb, ALU.mult)
            dve.tensor_tensor(k4[1], x2, sinb, ALU.mult)
            dve.tensor_tensor(k4[2], x1, sinb, ALU.mult)
            link(dve.tensor_tensor(k4[3], x2, cosb, ALU.mult))
            dve.tensor_tensor(x1, k4[0], k4[1], ALU.subtract)
            link(dve.tensor_tensor(x2, k4[2], k4[3], ALU.add))
            split(U_UQ + 2)
            split(U_UQ + 3)
            dve.wait_ge(s_evac, EV[U_UQ + 1])
            sq = [rt[i][:, 0, :] for i in range(4)]
            for t in range(T):
                for h in range(HEADS):
                    i = t * HEADS + h
                    if i >= 4:
                        dve.wait_ge(s_chain, chain.at(chain.n - 3))
                    chain.inc(squares(sq[i % 4], q[:, t, h * QK:(h + 1) * QK], small[:, i:i + 1], 1.0 / QK))
            dve.wait_ge(s_chain, chain.at(chain.n))
            rsqrt(*stat(12))
            for t in range(T):
                for h in range(HEADS):
                    i, v = 72 + t * HEADS + h, q[:, t, h * QK:(h + 1) * QK]
                    m = dve.scalar_tensor_tensor(v, v, small[:, i:i + 1], V("qn", 0, QK), ALU.mult, ALU.mult)
            link(m)
            r4 = [rt[i].rearrange("p t (h w) -> p t h w", w=HALF) for i in range(4)]
            for t in range(T):
                v = q[:, t, :].rearrange("p (h w) -> p h w", w=QK)
                a1, a2 = v[:, :, P:P + HALF], v[:, :, P + HALF:QK]
                cb = trig[:, 0, t, :].unsqueeze(1).to_broadcast([P, HEADS, HALF])
                sb_ = trig[:, 1, t, :].unsqueeze(1).to_broadcast([P, HEADS, HALF])
                dve.tensor_tensor(r4[0][:, t], a1, cb, ALU.mult)
                dve.tensor_tensor(r4[1][:, t], a2, sb_, ALU.mult)
                dve.tensor_tensor(r4[2][:, t], a1, sb_, ALU.mult)
                link(dve.tensor_tensor(r4[3][:, t], a2, cb, ALU.mult))
                dve.tensor_tensor(a1, r4[0][:, t], r4[1][:, t], ALU.subtract)
                m = dve.tensor_tensor(a2, r4[2][:, t], r4[3][:, t], ALU.add)
            m.then_inc(sem("q_done"), 1)
            split(U_UKV + 2)
            dve.wait_ge(s_evac, EV[U_UKV])
            for t in range(T):
                for h in range(HEADS):
                    i = t * HEADS + h
                    if i >= 4:
                        dve.wait_ge(s_chain, chain.at(chain.n - 3))
                    chain.inc(squares(sq[i % 4][:, 0:P], kv[:, t, h * 256:h * 256 + P], small[:, i:i + 1], 1.0 / QK))
            dve.wait_ge(s_chain, chain.at(chain.n))
            for t in range(T):
                v = small[:, t * HEADS:(t + 1) * HEADS]
                m = dve.tensor_scalar(v, v, small[:, 190 + t:191 + t], None, ALU.add)
            link(m)
            rsqrt(*stat(12))
            for t in range(T):
                for h in range(HEADS):
                    i, v = 72 + t * HEADS + h, kv[:, t, h * 256:h * 256 + P]
                    dve.scalar_tensor_tensor(v, v, small[:, i:i + 1], V("kn", 0, P), ALU.mult, ALU.mult)
                m = dve.tensor_tensor(krh[:, t, :].rearrange("p (h w) -> p h w", w=ROPE),
                                      kr[:, t, :].unsqueeze(1).to_broadcast([P, HEADS, ROPE]),
                                      small[:, 72 + t * HEADS:78 + t * HEADS].unsqueeze(2)
                                      .to_broadcast([P, HEADS, ROPE]), ALU.mult)
            m.then_inc(sem("k_done"), 1)
            scale = QK ** -0.5

            def head_S(h):
                dve.wait_ge(sem("mla_s_ready"), h + 1)
                p, c = mp[h % 2], 2 * (h % 2)
                if h >= 2:
                    dve.wait_ge(sem("mla_pT_ready"), h - 1)
                bank = ps[:, h % 2, :].rearrange("p (a b) -> p a b", b=P)
                dve.scalar_tensor_tensor(p[:, 0:2, :], bank[:, 0:2, :], scale,
                                         causal.unsqueeze(1).to_broadcast([P, 2, P]), ALU.mult, ALU.add)
                n = dve.tensor_scalar(p[:, 2, :], bank[:, 2, :], scale, None, ALU.mult)
                n.then_inc(sem("mla_sm_done"), 1)
                dve.wait_ge(sem("mla_sm_done"), h + 1)
                dve.tensor_reduce(small[:, 128 + c:129 + c], p[:, 0:1, :], AX, ALU.max)
                link(dve.tensor_reduce(small[:, 129 + c:130 + c], p[:, 1:3, :].rearrange("p a b -> p (a b)"), AX, ALU.max))
                dve.tensor_scalar(small[:, 96 + c:98 + c], small[:, 128 + c:130 + c], -1.0, None, ALU.mult).then_inc(sem("mla_mx_done"), 1)

            def head_P(h):
                dve.wait_ge(sem("mla_e_done"), h + 1)
                p, c = mp[h % 2], 2 * (h % 2)
                link(dve.reciprocal(small[:, 128 + c:130 + c], small[:, 112 + c:114 + c]))
                dve.tensor_scalar(p[:, 0, :], p[:, 0, :], small[:, 128 + c:129 + c], None, ALU.mult)
                v = p[:, 1:3, :].rearrange("p a b -> p (a b)")
                dve.tensor_scalar(v, v, small[:, 129 + c:130 + c], None, ALU.mult).then_inc(sem("mla_p_done"), 1)

            def head_pT(h):
                dve.wait_ge(sem("mla_pT_ready"), h + 1)
                if h >= 2:
                    dve.wait_ge(sem("mla_o_ready"), h - 1)
                dve.tensor_copy(mpT[h % 2][:, :, :].rearrange("p a b -> p (a b)"), ps[:, 2 + h % 2, 0:384]).then_inc(sem("mla_pT_done"), 1)

            for i in range(HEADS + 3):
                if 1 <= i <= HEADS:
                    head_S(i - 1)
                    head_P(i - 1)
                if 2 <= i <= HEADS + 1:
                    head_pT(i - 2)
                if i >= 3:
                    h = i - 3
                    y_lo_from(h, 6 + h % 2, 0, None, HEADS + h + 1)
            mem_attention(1)
            for u in range(U_OUT1, U_OUT1 + 3):
                split(u + 2)
            dve.wait_ge(s_used, U_OUT1 + 3)
            residual()
            norm_a(3)
            norm_b(3, "ffn1")
            ffn(1)

            norm_a(4)
            norm_b(4, "ffn2")
            ffn(2)
            norm_a(5)
            norm_b(5, "mix2")
            link(dve.memset(glu[:, :, 0:TAPS - 1], 0.0))
            pad = TAPS - 1
            for n in range(4):
                split(U_IN2 + n + 2)
                dve.wait_ge(s_evac, EV[U_IN2 + n])
                for i in ((0,), (1,), (2, 3), ())[n]:
                    m = dve.tensor_tensor(glu[:, i, pad:pad + S], ga[:, i, :], gs[:, i, :], ALU.mult)
                if n == 2:
                    link(m)
            split(U_IN2 + 6)
            split(U_IN2 + 7)
            split(U_IN2 + 8)
            dve.wait_ge(sem("gate_ready"), 1)
            dve.tensor_tensor(la, ps[:, 7, :].rearrange("p (a b) -> p a b", b=256),
                                  V("gb", 0, 256).unsqueeze(1).to_broadcast([P, T, 256]), ALU.add).then_inc(sem("gl_done"), 1)
            dve.wait_ge(sem("g_ln_done"), 1)
            dve.scalar_tensor_tensor(la, la, 0.0, g_abs, ALU.min, ALU.subtract).then_inc(sem("la_done"), 1)
            marks = []
            for tap in range(TAPS - 1, -1, -1):
                for i in range(4):
                    w = V("dw", i * TAPS + tap)
                    g_ = glu[:, i, tap:tap + S]
                    if tap == TAPS - 1:
                        m = dve.tensor_scalar(cy[:, i, :], g_, w, V("db", i), ALU.mult, ALU.add)
                    else:
                        dve.wait_ge(s_chain, chain.at(marks[-4]))
                        m = dve.scalar_tensor_tensor(cy[:, i, :], g_, w, cy[:, i, :], ALU.mult, ALU.add)
                    marks.append(chain.inc(m))
            dve.wait_ge(s_chain, chain.at(chain.n))
            dve.tensor_copy(small[:, 140:141], small[:, 72:73]).then_inc(sem("cy_done"), 1)
            dve.wait_ge(sem("mean_ready"), 1)
            mean = ps[:, 4, 0:S].unsqueeze(1).to_broadcast([P, 4, S])
            link(dve.tensor_tensor(cy, cy, mean, ALU.subtract))
            dve.tensor_tensor(ga, cy, cy, ALU.mult).then_inc(sem("ysq_done"), 1)
            dve.wait_ge(sem("var_ready"), 1)
            dve.tensor_copy(lnr[3], ps[:, 5, 0:S]).then_inc(sem("var_used"), 1)
            dve.wait_ge(sem("var_used"), 1)
            rsqrt(lnr[2], lnr[3], S, lnr[0], lnr[1])
            dve.tensor_tensor(cy, cy, lnr[2].unsqueeze(1).to_broadcast([P, 4, S]), ALU.mult).then_inc(sem("yn_done"), 1)
            for i in range(4):
                dve.wait_ge(sem("y_hi_done"), 12 + i + 1)
                m = dve.tensor_tensor(y_lo[:, i, :], ga[:, i, :], y_hi[:, i, :], ALU.subtract)
                m.then_inc(sem("y_ready"), 1)
            dve.wait_ge(sem("y_ready"), 2 * KT + 4)
            dve.tensor_copy(small[:, 140:141], small[:, 72:73]).then_inc(sem("conv_done"), 1)
            dve.wait_ge(sem("cum_copied"), 1)
            c8, e8 = [v.rearrange("p f (c s) -> p (f c) s", s=CHUNK) for v in (cum, ec)]
            dve.tensor_tensor(e8, c8[:, :, CHUNK - 1:CHUNK].to_broadcast([P, 8, CHUNK]), c8, ALU.subtract).then_inc(sem("ec_in_done"), 1)
            dve.wait_ge(sem("gexp_done"), 1)
            gsc = G_K ** -0.5
            link(dve.scalar_tensor_tensor(qd, gq, gsc, ep, ALU.mult, ALU.mult))
            dve.scalar_tensor_tensor(qu, gq, gsc, en, ALU.mult, ALU.mult)
            dve.tensor_tensor(kd, gk, en, ALU.mult)
            dve.tensor_tensor(ku, gk, ep, ALU.mult)
            dve.wait_ge(sem("gexp_done"), 2)
            link(dve.tensor_tensor(ke, gk, ec, ALU.mult))
            for f in range(2):
                dve.tensor_scalar(k7[:, f, 0:CHUNK], ke[:, f, 0:CHUNK], ep[:, f, 127:128], None, ALU.mult)
                dve.tensor_copy(k7[:, f, CHUNK:P], ke[:, f, CHUNK:P])
                dve.tensor_copy(q7[:, f, 0:CHUNK], qd[:, f, P:P + CHUNK])
                m = dve.tensor_scalar(q7[:, f, CHUNK:P], qd[:, f, P + CHUNK:S], ep[:, f, 191:192], None, ALU.mult)
            m.then_inc(sem("gla_in_done"), 1)

            def three_d(b, n=4):
                return ps[:, b, 0:n * P].rearrange("p (a b) -> p a b", b=P)

            dve.wait_ge(sem("g_s_ready"), 1)
            for par in range(2):
                chain.inc(dve.tensor_copy(gA[par], three_d(par)))
            dve.wait_ge(s_chain, chain.at(chain.n))
            dve.wait_ge(sem("g_s_ready"), 2)
            for par in range(2):
                chain.inc(dve.copy_predicated(gA[par], msk[:, MU:MU + P].unsqueeze(1).to_broadcast([P, 4, P]),
                                              three_d(6 + par)))
            dve.wait_ge(s_chain, chain.at(chain.n))
            dve.wait_ge(sem("g_s_ready"), 3)
            for par in range(2):
                chain.inc(dve.copy_predicated(gA[par], msk[:, MX:MX + P].unsqueeze(1).to_broadcast([P, 4, P]),
                                              three_d(4 + par)))
            dve.wait_ge(s_chain, chain.at(chain.n))
            dve.wait_ge(sem("g_s_ready"), 4)
            for par in range(2):
                dve.memset(gA[par][CHUNK:P, :, 0:CHUNK], 0.0)
                m = dve.tensor_copy(gO[par], three_d(2 + par, 2))
            m.then_inc(sem("gA_done"), 1)
            for t in range(T):
                dve.wait_ge(sem("go_copied"), t + 1)
                link(dve.tensor_tensor(gosq[:, t, :], go[:, t, :], go[:, t, :], ALU.mult))
            head_sums(gosq, 8, P)
            rsqrt(*stat(8), scale=1.0 / P)
            for t in range(T):
                for h in range(G_HEADS):
                    v = go[:, t, h * P:(h + 1) * P]
                    i = 72 + t * G_HEADS + h
                    m = dve.scalar_tensor_tensor(v, v, small[:, i:i + 1], gr[:, t, h * P:(h + 1) * P],
                                                 ALU.mult, ALU.mult)
                m.then_inc(sem("go_done"), 1)
            for h in range(G_HEADS):
                y_lo_from(4 + h, 4 + h // 2, (h % 2) * S, V("glan", h), 16 + 2 * (h // 2) + 2)
            for u in range(U_OUT2 + 0, U_OUT2 + 3):
                if u + 2 > U_IN2 + 8:
                    split(u + 2)
            dve.wait_ge(s_used, U_OUT2 + 3)
            residual()
            norm_a(6)
            norm_b(6, "ffn3")
            ffn(3)
            dve.wait_ge(sem("ple_hi_done"), 1)
            for i in range(2):
                m = dve.tensor_tensor(y_lo[:, 3 + i, :], ps[:, 4, i * S:(i + 1) * S], y_hi[:, 3 + i, :], ALU.subtract)
            m.then_inc(sem("pleT_done"), 1)
            norm_a(7)
            split(U_PROJ + 2)
            norm_b(7, "ple")
            split(U_PROJ + 3)
            dve.wait_ge(s_evac, EV[U_PROJ])
            for t in range(T):
                dve.wait_ge(sem("sg_done"), 2 * t + 2)
                link(dve.tensor_tensor(proj[:, t, :], proj[:, t, :], sg[:, t, :], ALU.mult))
                dve.tensor_tensor(x[:, t, :], x[:, t, :], proj[:, t, :], ALU.add).then_inc(sem("x_done"), 1)
            dve.wait_ge(sem("x_done"), 16)
            link(squares(junk[:, 1, :], x[:, 1, :], small[:, 1:2]))
            dve.wait_ge(sem("ss_done"), 9)
            rsqrt(*stat(2), scale=1.0 / D)
            dve.wait_ge(sem("fin_loaded"), 16)
            for t in range(T):
                for half in range(2):
                    r = slice(half * 512, half * 512 + 512)
                    dve.scalar_tensor_tensor(xn[:, t, r], x[:, t, r], small[:, 72 + t:73 + t], fin[:, r],
                                                 ALU.mult, ALU.mult).then_inc(sem("out_done"), 1)


def lay_out(i):
    def grid(w, cols=None):
        k, n = w.shape
        g = w.reshape(k // P, P, n).transpose(1, 0, 2)
        return g if cols is None or cols == n else np.concatenate(
            [g, np.zeros((P, k // P, cols - n), w.dtype)], axis=2)

    def unit(*parts):
        flat = [p.reshape(P, -1) for p in parts]
        n = sum(p.shape[1] for p in flat)
        return np.concatenate(flat + [np.zeros((P, UNIT - n), np.float32)], axis=1)

    def model(w, a, b, w2=None, a2=0, b2=0):
        parts = [w[:, a:b]] + ([w2[:, a2:b2]] if w2 is not None else [])
        return unit(grid(np.concatenate(parts, axis=1), NC3))

    def kt_major(w):
        g = grid(w)
        return [unit(g[:, 3 * j:3 * j + 3]) for j in range(-(-g.shape[1] // 3))]

    def ffn(w_up, w_down):
        units = []
        for c in range(FFN_UNITS):
            parts = []
            for z in range(2):
                a = z * D_FF + c * P
                parts.append(grid(w_up[:, a:a + P]) if c < CH else np.zeros((P, PIECE), np.float32))
            parts.append(w_down[(c - 1) * P:c * P] if c else np.zeros((P, PIECE), np.float32))
            units.append(unit(*parts))
        return units

    mk, hg, mla, w2 = i["w_mem_kv"], i["hg_w_in"][0], i["mla_w_in"][0], i["w_in_2"][0]
    uq, ukv = i["mla_w_uq"][0], i["mla_w_ukv"][0]
    u = [model(mk[0], 0, 384), model(mk[0], 384, 512)]
    for a in (768, 0, 1536):
        u += [model(hg, a, a + 384), model(hg, a + 384, a + 768)]
    u += [model(mk[1], 0, 384), model(mk[1], 384, 512, hg, 3072, 3328)]
    u += [model(hg, 2304, 2688), model(hg, 2688, 3072)]
    u += kt_major(i["w_out"][0]) + ffn(i["w_up"][0], i["w_down"][0])
    u += [model(mla, 0, 384), model(mla, 384, 704), model(mla, 704, 960)]
    u += [unit(grid(uq[:, 0:768])), unit(grid(uq[:, 768:1152])), unit(grid(ukv))]
    u += kt_major(i["w_out"][1]) + ffn(i["w_up"][1], i["w_down"][1])
    u += ffn(i["ffn1_w_in_2"][0], i["ffn1_w_out_2"][0])
    tile = {"a": 0, "b": 512, "q": 1024, "k": 1280}
    order = ["a0", "b0", "a1", "b1", "a2", "b2", "a3", "b3", "q0", "q1", "k0", "k1"]
    starts = [tile[n[0]] + P * int(n[1]) for n in order]
    for n in range(4):
        u.append(unit(grid(np.concatenate([w2[:, a:a + P] for a in starts[3 * n:3 * n + 3]], axis=1))))
    u += [model(w2, 2304, 2560, w2, 2560, 2576), model(w2, 1536, 1920), model(w2, 1920, 2048, w2, 2048, 2304)]
    u += kt_major(i["w_out_2"][0]) + ffn(i["ffn2_w_in_2"][0], i["ffn2_w_out_2"][0])
    u += kt_major(i["ple_w_proj_2"][0]) + kt_major(i["ple_w_gate_2"][0])
    assert len(u) == UNITS
    stream = np.stack(u)

    def col(g):
        return g.reshape(-1, P).T

    def every(v):
        return np.broadcast_to(v.reshape(1, -1), (P, v.size))

    def conv(layer):
        w, b = i["conv_w"][layer], i["conv_b"][layer]
        g = np.concatenate([w, b[None]], axis=0).reshape(4, 2, CH, P)
        return g.transpose(3, 2, 1, 0).reshape(P, CH * 8)

    r = np.arange(P)
    same = r[:, None] // CHUNK == r[None, :] // CHUNK
    f32 = np.float32
    v = {
        "mix0": col(i["mix_norm_g"][0]), "mix1": col(i["mix_norm_g"][1]), "ffn0": col(i["ffn_norm_g"][0]),
        "ffn1": col(i["ffn_norm_g"][1]), "mem0": col(i["mem_norm_g"][0]), "mem1": col(i["mem_norm_g"][1]),
        "ffn2": col(i["ffn1_norm_2"][0]), "mix2": col(i["mix_norm_2"][0]), "ffn3": col(i["ffn2_norm_2"][0]),
        "ple": col(i["ple_norm_2"][0]), "cw0": conv(0), "cw1": conv(1),
        "mq": np.concatenate([i["mem_q_norm_g"]] * 2, axis=1).T, "mk": np.concatenate([i["mem_k_norm_g"]] * 2, axis=1).T,
        "lb": i["hg_lb_logits"].reshape(3, HEADS, P).transpose(2, 0, 1).reshape(P, 18),
        "hgn": col(i["hg_out_norm_g"][0]), "qa": col(i["mla_qa_norm_g"][0]), "kva": col(i["mla_kva_norm_g"][0]),
        "dw": i["conv_w_2"][0].reshape(TAPS, 4, P).transpose(2, 1, 0).reshape(P, 4 * TAPS),
        "db": col(i["conv_b_2"][0]), "lng": col(i["conv_ln_g_2"][0]), "lnb": col(i["conv_ln_b_2"][0]),
        "glan": col(i["gla_norm_2"][0]), "gb": every(i["gate_b_2"][0]),
        "qn": every(i["mla_q_norm_g"][0]), "kn": every(i["mla_k_norm_g"][0]),
        "inv": every((f32(10000.0) ** (-np.arange(HALF, dtype=f32) / f32(HALF))).astype(f32)),
        "gup": np.concatenate([i["gate_w_up_2"][0], np.zeros((P - 16, 256), f32)], axis=0),
        "ident": np.eye(P, dtype=f32),
        "causal": np.where(r[None, :] <= r[:, None], 0.0, -1e30).astype(f32),
        "tri": (same & (r[:, None] <= r[None, :])).astype(f32),
        "ones": np.full((P, P), 1.0 / 512, f32),
    }
    assert list(v) == list(_cols)
    vectors = np.concatenate([v[n] for n in _cols], axis=1)
    assert vectors.shape == (P, NV) and all(v[n].shape[1] == _cols[n][1] for n in _cols)

    masks = []
    for l in range(MASKS):
        m = 1 << l
        j = np.arange(64)
        t = (j // m) * 2 * m + m + j % m
        masks.append((r[:, None] // (2 * m) == t[None, :] // (2 * m)) & (r[:, None] % (2 * m) < m))
    masks.append(same & (r[:, None] > r[None, :]))
    masks.append((r[:, None] < CHUNK) & (r[None, :] >= CHUNK))
    tok = lambda a: a.reshape(T, P, -1).transpose(1, 0, 2)
    return {
        "stream": stream, "vectors": vectors, "masks": np.concatenate(masks, axis=1).astype(f32),
        "x": tok(i["x"][0]), "mem": tok(i["mem"][0]), "positions": i["positions"][0].reshape(T, P).T,
        "ple": tok(i["p_2"][0, 0]), "final": every(i["final_norm_2"]),
    }


def kernel(**inputs):
    import concourse.bacc as _bacc
    from concourse.bass_utils import run_bass_kernel_spmd as _run

    inputs = {k: np.asarray(v) for k, v in inputs.items()}
    nc = _bacc.Bacc("TRN2", target_bir_lowering=False, num_devices=1)
    arrays, args = {}, []
    for name, a in lay_out(inputs).items():
        a = np.ascontiguousarray(a)
        arrays[f"in_{name}"] = a
        args.append(nc.dram_tensor(f"in_{name}", a.shape, mybir.dt.from_np(a.dtype), kind="ExternalInput").ap())
    args.append(nc.dram_tensor("out", (S, D), F32, kind="ExternalOutput").ap())
    build(nc, *args)
    r = _run(nc, [arrays], core_ids=[0])
    return r.results[0]["out"].reshape(1, S, D)
```

```python
from contextlib import ExitStack

import numpy as np

import concourse.bass as bass
from concourse import mybir

F32 = mybir.dt.float32
F32R = mybir.dt.float32r
BF16 = mybir.dt.bfloat16
I32 = mybir.dt.int32
U8 = mybir.dt.uint8
ALU = mybir.AluOpType
ACT = mybir.ActivationFunctionType
AX = mybir.AxisListType.X

P = 128
S = 256
T = S // P
D = 1024
KT = D // P
EPS = 1e-6
UNIT = 3072
PIECE = UNIT // 3
NC3 = UNIT // KT
SLOTS = 3
D_FF = 2816
CH = D_FF // P
FFN_UNITS = CH + 1
HEADS = 6
HW = HEADS * P
MEM_HEADS, MEM_HD, MEM_W = 4, 64, 256
ROPE, HALF, QK = 64, 32, 192
G_HEADS, G_K = 4, 64
TAPS = 31
SHARED = 13
CHUNK = 64
WARM = 16
LEVELS = 8

U_MEM0 = 0
U_F = 2
U_Q = 4
U_I = 6
U_MEM1 = 8
U_G = 10
U_OUT0 = 12
U_FFN0 = U_OUT0 + 3
U_MLA = U_FFN0 + FFN_UNITS
U_UQ = U_MLA + 3
U_UKV = U_UQ + 2
U_OUT1 = U_UKV + 1
U_FFN1 = U_OUT1 + 3
U_FFN2 = U_FFN1 + FFN_UNITS
U_IN2 = U_FFN2 + FFN_UNITS
U_OUT2 = U_IN2 + 7
U_FFN3 = U_OUT2 + 3
U_PROJ = U_FFN3 + FFN_UNITS
U_GATE = U_PROJ + 1
UNITS = U_GATE + 3

_cols = {}
_at = 0
for _name, _n in (
    ("mix0", KT), ("mix1", KT), ("ffn0", KT), ("ffn1", KT), ("mem0", KT), ("mem1", KT),
    ("ffn2", KT), ("mix2", KT), ("ffn3", KT), ("ple", KT),
    ("cw0", CH * 8), ("cw1", CH * 8), ("mq", 2), ("mk", 2), ("lb", 18), ("hgn", 1), ("qa", 3), ("kva", 2),
    ("dw", 4 * TAPS), ("db", 4), ("lng", 4), ("lnb", 4), ("glan", 4),
    ("gb", 256), ("qn", 1), ("kn", 1), ("qnr", ROPE), ("knr", ROPE), ("inv", HALF), ("gup", 256),
    ("ident", P), ("causal", P), ("tri", P), ("ones", P),
):
    _cols[_name] = (_at, _n)
    _at += _n
NV = _at
MASKS = LEVELS - 1
MU, MX = MASKS * 64, MASKS * 64 + P
NM = MX + P


TWO_PI = (6.28125, 0.0019350051879882812, float(2 * np.pi - 6.28125 - 0.0019350051879882812))


def extent(u, p):
    if u in (U_FFN0, U_FFN1, U_FFN2, U_FFN3):
        used = 2 * PIECE
    elif u in (U_FFN0 + CH, U_FFN1 + CH, U_FFN2 + CH, U_FFN3 + CH):
        used = UNIT if p == 2 else 0
    else:
        used = {U_UQ: 3 * 768, U_UQ + 1: 3 * 384, U_OUT0 + 2: 2 * D, U_OUT1 + 2: 2 * D, U_OUT2 + 2: 2 * D,
                U_PROJ: 2 * D, U_GATE + 2: 2 * D}.get(u, UNIT)
    return slice(p * PIECE, p * PIECE + min(max(used - p * PIECE, 2), PIECE))


class Count:

    def __init__(self, sem):
        self.sem, self.n, self.turn, self.per = sem, 0, None, 0

    def inc(self, ins):
        ins.then_inc(self.sem, 1)
        self.n += 1
        return self.n

    def at(self, n):
        return n if self.turn is None else self.turn * self.per + n

    def enter(self, turn, per):
        self.turn, self.per, self.was = turn, per, self.n

    def leave(self, turns):
        assert self.n - self.was == self.per, (self.n, self.was, self.per)
        self.turn, self.n = None, self.was + self.per * turns


def build(nc, stream, vectors, masks, x_in, mem_in, pos_in, ple_in, fin_in, out):
    with ExitStack() as ctx:
        def sb(name, shape, dt=F32):
            return ctx.enter_context(nc.sbuf_tensor(name, shape, dt))

        sems = {}

        def sem(name):
            if name not in sems:
                sems[name] = ctx.enter_context(nc.semaphore(name))
            return sems[name]

        raw = sb("raw", [P, SLOTS, UNIT])
        w_hi = sb("w_hi", [P, SLOTS, UNIT], F32R)
        w_lo = sb("w_lo", [P, SLOTS, UNIT], F32R)
        x = sb("x", [P, T, D])
        h_hi = sb("h_hi", [P, KT, S], F32R)
        h_lo = sb("h_lo", [P, KT, S], F32R)
        y_hi = sb("y_hi", [P, KT, S], F32R)
        y_lo = sb("y_lo", [P, KT, S], F32R)
        mem_k = sb("mem_k", [P, 2, 2, S])
        mem_v = sb("mem_v", [P, 2, T, MEM_W])
        vec = sb("vec", [P, NV])
        msk = sb("msk", [P, NM], U8)
        zero = sb("zero", [P, P], BF16)
        trig = sb("trig", [P, 2, T, HALF])
        small = sb("small", [P, 192])
        mk_flat = sb("mk_sq", [P, T * MEM_W])
        arena = sb("arena", [P, 9984])
        ps = ctx.enter_context(nc.psum_tensor("ps", [P, 8, 512], F32))

        def V(name, i=0, n=1):
            a, w = _cols[name]
            return vec[:, a + i:a + i + n]

        def room(tile, at, shape):
            v = tile[:, at:at + int(np.prod(shape))]
            if len(shape) == 2:
                v = v.rearrange("p (a b) -> p a b", b=shape[1])
            return v

        def A(at, *shape):
            return room(arena, at, shape)

        mk_sq = room(mk_flat, 0, (T, MEM_W))
        xflat = x[:, :, :].rearrange("p t d -> p (t d)")
        kflat = mem_k[:, :, :, :].rearrange("p a b c -> p (a b c)")
        vflat = mem_v[:, :, :, :].rearrange("p a b c -> p (a b c)")
        ident, causal, tri, ones = V("ident", 0, P), V("causal", 0, P), V("tri", 0, P), V("ones", 0, P)

        xn, junk = A(0, T, D), A(2048, T, D)
        diag = A(0, T, P)
        memn = A(4096, KT, S)
        mk_tok = [mem_k[:, l, :, :] for l in range(2)]
        tr = [A(7168 + 64 * i, T, HALF) for i in range(4)]
        msk_f = A(8192, NM)
        hq, hk = A(0, HEADS, S), A(1536, HEADS, S)
        hD, hR = A(3072, HEADS, S), A(4608, HEADS, S)
        hE = A(6144, HEADS, S)
        hA = A(7680, HEADS * T, P)
        hO = A(9216, HEADS, P)
        hv, qm0 = room(xflat, 0, (T, HW)), room(xflat, 1536, (T, MEM_W))
        ho, hsq, hg = A(3072, T, HW), A(4608, T, HW), A(0, T, HW)
        ma_sq, ma_qT, ma_p, ma_pT = mk_sq, room(mk_flat, 0, (2, S)), A(3072, 8, S), A(5120, 8, S)
        cq, ckv, qm1 = A(0, T, 384), A(768, T, 320), A(1408, T, MEM_W)
        q, kv, kdiag = A(1920, T, 1152), A(4224, T, 1536), A(7296, 6, P)
        rt = [A(8064 + 384 * i, T, 192) for i in range(4)]
        kr = A(9856, T, ROPE)
        qkT = (A(0, 4, S), A(8064, 4, S))
        mp = (A(9088, 3, P), A(9472, 3, P))
        mpT = (room(kflat, 0, (3, P)), room(vflat, 0, (3, P)))
        ksq = [r[:, i, :] for r, n in ((kdiag, 6), (mpT[0], 3), (mpT[1], 3)) for i in range(n)]
        ga, gs, glu, cy = A(0, 4, S), A(1024, 4, S), A(2048, 4, S + TAPS - 1), A(3192, 4, S)
        gq, gk, glr = A(4216, 2, S), A(4728, 2, S), A(5240, S)
        gv, gr, la = A(5496, T, 512), A(6520, T, 512), A(7544, T, 256)
        lnr = [A(a, S) for a in (5240, 8568, 8824, 9600)]
        tapd = A(9088, 7, P)
        ple = A(9088, T, 256)
        ep, en, ec, qd = [A(512 * i, 2, S) for i in range(4)]
        kd, ke = A(7544, 2, S), mk_sq
        qu, ku = gq, gk
        csq = A(2048, 4, S)
        q7, k7 = A(8056, 2, P), A(8312, 2, P)
        gA = [room(kflat, 512 * i, (4, P)) for i in range(2)]
        gO = [room(vflat, 256 * i, (2, P)) for i in range(2)]
        cum = room(vflat, 512, (2, S))
        go, gosq = A(0, T, 512), A(1024, T, 512)
        g_abs = A(8056, T, 256)
        cv, sa, gg = A(0, 3, 512), A(1536, 3, S), A(2304, 3, S)
        fin, proj, sg = A(4096, D), A(5120, T, D), A(0, T, D)

        rings = [sem(f"raw_loaded{i}") for i in range(SLOTS)]
        s_hi, s_lo, s_used = sem("hi_ready"), sem("lo_ready"), sem("unit_used")
        s_evac, s_chain = sem("unit_evacuated"), sem("dve_chain")
        FFNS = ((U_FFN0, "cw0"), (U_FFN1, "cw1"), (U_FFN2, None), (U_FFN3, None))
        UP0 = (0, CH, None, None)
        FFN_NORM = (1, 3, 4, 6)
        HG_UNITS = [U_I, U_I + 1, U_MEM1, U_MEM1 + 1, U_G, U_G + 1]
        IN2_TILES = (U_IN2, U_IN2 + 1, U_IN2 + 3, U_IN2 + 4)
        PE_TAPS = [(3, tap) for tap in range(TAPS)] + [(2, tap) for tap in range(SHARED)]
        PLAIN = [0, 1, 2, 3, 4, 5] + HG_UNITS + [U_MLA, U_MLA + 1, U_MLA + 2, U_UQ, U_UQ + 1, U_UKV] + \
                list(range(U_IN2, U_IN2 + 7)) + [U_PROJ]
        EV = {u: i + 1 for i, u in enumerate(PLAIN)}

        def right(v, m):
            return v.rearrange("p h (b z m) -> p (h b) z m", z=2, m=m)[:, :, 1, :]

        def left(v, m):
            return v.rearrange("p h (b z m) -> p (h b) z m", z=2, m=m)[:, :, 0, :]

        block = ctx.enter_context(nc.Block())

        @block.sync
        def _(sp):
            sp.dma_start(junk, mem_in).then_inc(sem("mem_loaded"), 16)
            sp.dma_start(vec[:, :], vectors).then_inc(sem("vec_loaded"), 16)
            for s in range(SLOTS):
                sp.dma_start(raw[:, s, :], stream[s]).then_inc(rings[s], 16)
                if s == 0:
                    sp.dma_start(x[:, :, :], x_in).then_inc(sem("x_loaded"), 16)
                    sp.dma_start(small[:, 186:188].bitcast(I32), pos_in).then_inc(sem("pos_loaded"), 16)
                    sp.dma_start(msk_f, masks).then_inc(sem("msk_loaded"), 16)

            turns = (UNITS - SLOTS) // SLOTS
            with sp.Fori(0, turns) as i:
                for s in range(SLOTS):
                    sp.wait_ge(s_lo, i * 9 + (3 * s + 3))
                    sp.dma_start(raw[:, s, :],
                                 stream[bass.ds(i * SLOTS + (SLOTS + s), 1)].rearrange("a p n -> p (a n)"))\
                        .then_inc(rings[s], 16)
            for u in range(SLOTS * (turns + 1), UNITS):
                sp.wait_ge(s_lo, (u - SLOTS) * 3 + 3)
                sp.dma_start(raw[:, u % SLOTS, :], stream[u]).then_inc(rings[u % SLOTS], 16)
            for i in range(2 * T):
                sp.wait_ge(sem("out_done"), i + 1)
                t, half = i // 2, i % 2
                sp.dma_start(out[t * P:(t + 1) * P, half * 512:half * 512 + 512],
                             xn[:, t, half * 512:half * 512 + 512]).then_inc(sem("out_stored"), 16)
            sp.wait_ge(sem("out_stored"), 16 * 2 * T)

        @block.gpsimd
        def _(pool):
            pool.memset(zero[:, :], 0.0).then_inc(sem("zero_set"), 1)
            pool.wait_ge(sem("hg_o_ready"), 1)
            pool.wait_ge(sem("ma_qT_ready"), 1)
            pool.dma_start(x[:, :, :], x_in).then_inc(sem("x_back"), 16)
            pool.wait_ge(sem("x_done"), 4 * 6)
            pool.dma_start(ple, ple_in).then_inc(sem("ple_loaded"), 16)
            pool.dma_start(fin, fin_in).then_inc(sem("fin_loaded"), 16)

        @block.tensor
        def _(pe):
            def pieces(u, end):
                return u * 3 + -(-end // PIECE)

            def three(o, lh, ll, rh, rl, start, stop):
                pe.matmul(o, lh, rh, start=start, stop=False, skip_group_check=True)
                pe.matmul(o, lh, rl, start=False, stop=False, skip_group_check=True)
                return pe.matmul(o, ll, rh, start=False, stop=stop, skip_group_check=True)

            def full(o, l, r, start=True, stop=True):
                return pe.matmul(o, l, r, start=start, stop=stop, skip_group_check=True)

            def rows(u, c0, n, banks, ah, al, kts=KT, width=NC3, col=0, norm=None):
                s = u % SLOTS
                for k in range(kts):
                    r = slice(k * width + c0, k * width + c0 + n)
                    pe.wait_ge(s_lo, pieces(u, r.stop))
                    if norm is not None:
                        pe.wait_ge(sem("hT_ready"), 4 * norm + k // 2 + 1)
                    for t in range(T):
                        tt = slice(t * P, (t + 1) * P)
                        m = three(ps[:, banks[t], col:col + n], ah[:, k, tt], al[:, k, tt],
                                  w_hi[:, s, r], w_lo[:, s, r], k == 0, k == kts - 1)
                return m

            def cols(u, j, o, norm=None):
                s = u % SLOTS
                for k in range(KT):
                    r = slice(k * NC3 + j * P, k * NC3 + j * P + P)
                    pe.wait_ge(s_lo, pieces(u, r.stop))
                    if norm is not None:
                        pe.wait_ge(sem("hT_ready"), 4 * norm + k // 2 + 1)
                    m = three(o, w_hi[:, s, r], w_lo[:, s, r], h_hi[:, k, :], h_lo[:, k, :], k == 0, k == KT - 1)
                return m

            def norm(i):
                if i:
                    warm(WARM)
                for k in range(KT):
                    for t in range(T):
                        if k == 0:
                            pe.wait_ge(sem("factors_done"), T * i + t + 1)
                        m = full(ps[:, 4 + k // 2, (k % 2) * S + t * P:(k % 2) * S + (t + 1) * P],
                                 x[:, t, k * P:(k + 1) * P], diag[:, t, :])
                    if k % 2:
                        m.then_inc(sem("xT_ready"), 1)

            def kt_major(u, ah, al, ready):
                for k in range(KT):
                    s, e = (u + k // 3) % SLOTS, (k % 3) * D
                    pe.wait_ge(s_lo, pieces(u + k // 3, e + D))
                    ready(k)
                    for t in range(T):
                        tt = slice(t * P, (t + 1) * P)
                        for half in range(2):
                            r = slice(e + half * 512, e + half * 512 + 512)
                            m = three(ps[:, 2 * t + half, :], ah[:, k, tt], al[:, k, tt],
                                      w_hi[:, s, r], w_lo[:, s, r], k == 0, k == KT - 1)
                            if k == KT - 1 and 2 * t + half < 3:
                                m.then_inc(sem("sum_ready"), 1)
                    if k % 3 == 2 or k == KT - 1:
                        m.then_inc(s_used, 1)

            def ffn(i):
                U0, n0 = FFNS[i][0], i * CH

                def lo_at(r, j, p):
                    return 3 * (U0 + j) + p + 1 if r is None else r * 9 + (3 * (U0 + j) + p + 1)

                def up(r, j, norm=None):
                    s = (U0 + j) % SLOTS
                    for z in range(2):
                        pe.wait_ge(s_lo, lo_at(r, j, z))
                        for k in range(KT):
                            a = slice(z * PIECE + k * P, z * PIECE + k * P + P)
                            if norm is not None:
                                pe.wait_ge(sem("hT_ready"), 4 * norm + k // 2 + 1)
                            m = three(ps[:, 4 + j % 3, z * S:(z + 1) * S], w_hi[:, s, a], w_lo[:, s, a],
                                      h_hi[:, k, :], h_lo[:, k, :], k == 0, k == KT - 1)
                    m.then_inc(sem("up_ready"), 1)

                def down(r, j):
                    s, g = (U0 + j) % SLOTS, (j - 1) % 3
                    pe.wait_ge(s_lo, lo_at(r, j, 2))
                    pe.wait_ge(sem("g_lo_done"), n0 + j if r is None else r * 3 + (n0 + j))
                    for t in range(T):
                        tt = slice(t * P, (t + 1) * P)
                        for half in range(2):
                            a = slice(2 * PIECE + half * 512, 2 * PIECE + half * 512 + 512)
                            m = three(ps[:, 2 * t + half, :], y_hi[:, g, tt], y_lo[:, g, tt],
                                      w_hi[:, s, a], w_lo[:, s, a], False, True)
                            if j == CH and 2 * t + half < 3:
                                m.then_inc(sem("sum_ready"), 1)
                    m.then_inc(s_used, 1)

                up(None, 0, FFN_NORM[i])
                pe.wait_ge(s_lo, lo_at(None, 0, 2))
                for b in range(4):
                    m = full(ps[:, b, :], zero[:, :], zero[:, 0:1].to_broadcast([P, 512]))
                m.then_inc(s_used, 1)
                with pe.Fori(0, (CH - 1) // 3) as r:
                    for j in range(1, 4):
                        up(r, j)
                        down(r, j)
                if i == 3:
                    pe.wait_ge(sem("ple_loaded"), 16)
                    for f in range(2):
                        for t in range(T):
                            m = pe.transpose(ps[:, 7, f * S + t * P:f * S + (t + 1) * P],
                                             ple[:, t, f * P:(f + 1) * P], ident)
                    m.then_inc(sem("pleT_ready"), 1)
                down(None, CH)

            def warm(n, o=ps[:, 7, :]):
                for _ in range(n):
                    full(o, zero[:, :], zero[:, 0:1].to_broadcast([P, o.shape[1]]))

            def mem_keys(l):
                pe.wait_ge(sem("mk_done"), l + 1)
                for pair in range(2):
                    for t in range(T):
                        m = pe.transpose(ps[:, 4, pair * S + t * P:pair * S + (t + 1) * P],
                                         mk_tok[l][:, t, pair * P:(pair + 1) * P], ident)
                m.then_inc(sem("mkT_ready"), 1)

            def ma_queries(l):
                qm = (qm0, qm1)[l]
                pe.wait_ge(sem("ma_q_done"), l + 1)
                for pair in range(2):
                    for t in range(T):
                        m = pe.transpose(ps[:, 5, pair * S + t * P:pair * S + (t + 1) * P],
                                         qm[:, t, pair * P:(pair + 1) * P], ident)
                m.then_inc(sem("ma_qT_ready"), 1)

            def ma_scores(l):
                pe.wait_ge(sem("ma_qT_done"), l + 1)
                pe.wait_ge(sem("mkT_done"), l + 1)
                for t in range(T):
                    for par in range(2):
                        for pair in range(2):
                            r = slice(par * 64, par * 64 + 64)
                            m = full(ps[:, 4 + 2 * t + par, pair * S:(pair + 1) * S],
                                     ma_qT[r, pair, t * P:(t + 1) * P], mem_k[r, l, pair, :])
                        m.then_inc(sem("ma_s_ready"), 1)

            def ma_transposes(l):
                pe.wait_ge(sem("ma_p_done"), 4 * l + 4)
                for t in range(T):
                    for par in range(2):
                        for pair in range(2):
                            for mt in range(T):
                                m = pe.transpose(ps[:, 4 + 2 * pair + par, mt * S + t * P:mt * S + (t + 1) * P],
                                                 ma_p[:, 2 * (2 * t + par) + pair, mt * P:(mt + 1) * P], ident)
                m.then_inc(sem("ma_pT_ready"), 1)

            def ma_output(l):
                pe.wait_ge(sem("ma_pT_done0"), l + 1)
                pe.wait_ge(sem("ma_pT_done1"), l + 1)
                for h in range(MEM_HEADS):
                    par, pair = h % 2, h // 2
                    for mt in range(T):
                        m = full(ps[par * 64:par * 64 + 64, 4, pair * S:(pair + 1) * S],
                                 mem_v[:, l, mt, h * 64:(h + 1) * 64], ma_pT[:, 2 * h + mt, :], mt == 0, mt == 1)
                m.then_inc(sem("ma_o_ready"), 1)

            def beside_memory(l):
                def ready(k):
                    if k == 3:
                        ma_transposes(l)
                    if k == 5:
                        ma_output(l)
                    pe.wait_ge(sem("y_ready"), KT * l + max(k + 1, HEADS))
                return ready

            pe.wait_ge(sem("zero_set"), 1)
            pe.wait_ge(sem("vec_loaded"), 16)
            pe.wait_ge(sem("mn_done0"), 1)
            pe.wait_ge(sem("mn_done1"), 1)
            for k in range(KT):
                for t in range(T):
                    m = pe.transpose(ps[:, 4 + k // 2, (k % 2) * S + t * P:(k % 2) * S + (t + 1) * P],
                                     junk[:, t, k * P:(k + 1) * P], ident)
                if k % 2:
                    m.then_inc(sem("mnT_ready"), 1)
            pe.wait_ge(sem("memT_lo_done"), 1)
            rows(U_MEM0, 0, 384, (0, 1), y_hi, y_lo).then_inc(s_used, 1)
            rows(U_MEM0 + 1, 0, P, (2, 3), y_hi, y_lo).then_inc(s_used, 1)
            norm(0)
            for n, u in enumerate((U_F, U_F + 1, U_Q, U_Q + 1)):
                pe.wait_ge(s_evac, EV[u - 2])
                for j in range(3):
                    m = cols(u, j, ps[:, (n % 2) * 2 + j // 2, (j % 2) * S:(j % 2) * S + S], 0)
                m.then_inc(s_used, 1)
                if n == 1:
                    mem_keys(0)
            pe.wait_ge(s_evac, EV[U_Q + 1])
            pe.wait_ge(sem("hk_done"), 2)
            for n in range(HEADS * T):
                h, t = n // T, n % T
                tt = slice(t * P, (t + 1) * P)
                m = full(ps[:, n // 4, (n % 4) * P:(n % 4 + 1) * P], hk[:, h, tt], hq[:, h, tt])
                if n % 4 == 3:
                    m.then_inc(sem("diag_ready"), 1)

            def level(l):
                m_ = 1 << l
                for half in range(2):
                    n = 2 * l + half
                    pe.wait_ge(sem("mult_done"), n + 1)
                    pe.wait_ge(sem("pred_done"), max(min(n + 1, 3), n))
                    for i in range(3):
                        h = 3 * half + i
                        if l < LEVELS - 1:
                            for t in range(T):
                                v = hE[:, h, t * P:(t + 1) * P]
                                qs = v.rearrange("p (b z m) -> p b z m", z=2, m=m_)[:, :, 1, :]
                                c = (2 * i + t) * 64
                                m = full(ps[:, n % 4, c:c + 64].rearrange("p (b m) -> p b m", m=m_), v, qs)
                        else:
                            m = full(ps[:, n % 4, i * P:(i + 1) * P], hE[:, h, 0:P], hE[:, h, P:S])
                    m.then_inc(sem("level_ready"), 1)

            for l in range(LEVELS):
                level(l)
                if l >= len(HG_UNITS):
                    continue
                u = HG_UNITS[l]
                b = (4, 5) if l % 2 == 0 else (6, 7)
                if l >= 2:
                    pe.wait_ge(s_evac, EV[HG_UNITS[l - 2]])
                else:
                    pe.wait_ge(sem("mkT_done"), 1)
                if u in (U_I, U_I + 1):
                    m = rows(u, 0, 384, b, h_hi, h_lo)
                elif u == U_MEM1:
                    pe.wait_ge(sem("memT_lo_done"), 2)
                    m = rows(u, 0, 384, b, y_hi, y_lo)
                elif u == U_MEM1 + 1:
                    rows(u, 0, P, b, y_hi, y_lo)
                    m = rows(u, P, MEM_W, b, h_hi, h_lo, col=P)
                else:
                    m = rows(u, 0, 384, b, h_hi, h_lo)
                m.then_inc(s_used, 1)
            pe.wait_ge(sem("pred_done"), 3 + 2 * LEVELS)
            for t in range(T):
                for h in range(HEADS):
                    o = ps[:, 2 * t + h // 4, (h % 4) * P:(h % 4 + 1) * P]
                    hs = slice(h * P, (h + 1) * P)
                    if t:
                        full(o, hO[:, h, :], hv[:, 0, hs], True, False)
                    m = full(o, hA[:, h * T + t, :], hv[:, t, hs], t == 0, True)
            m.then_inc(sem("hg_o_ready"), 1)
            pe.wait_ge(s_evac, EV[U_G + 1])
            mem_keys(1)
            ma_queries(0)
            pe.wait_ge(sem("mkT_done"), 2)
            ma_scores(0)
            pe.wait_ge(sem("ho_done"), T)
            for h in range(HEADS):
                for t in range(T):
                    m = pe.transpose(ps[:, h // 2, (h % 2) * S + t * P:(h % 2) * S + (t + 1) * P],
                                     ho[:, t, h * P:(h + 1) * P], ident)
                if h % 2:
                    m.then_inc(sem("yT_ready"), 1)
            kt_major(U_OUT0, y_hi, y_lo, beside_memory(0))
            norm(1)
            ffn(0)

            norm(2)
            rows(U_MLA, 0, 384, (0, 1), h_hi, h_lo, norm=2).then_inc(s_used, 1)
            rows(U_MLA + 1, 0, 320, (2, 3), h_hi, h_lo).then_inc(s_used, 1)
            rows(U_MLA + 2, 0, MEM_W, (4, 5), h_hi, h_lo).then_inc(s_used, 1)
            pe.wait_ge(sem("c_done"), 1)
            for i in range(5):
                src = cq[:, :, i * P:(i + 1) * P] if i < 3 else ckv[:, :, (i - 3) * P:(i - 2) * P]
                b = (6, 6, 7, 7, 0)[i]
                for t in range(T):
                    m = pe.transpose(ps[:, b, (i % 2) * S + t * P:(i % 2) * S + (t + 1) * P], src[:, t, :], ident)
                if i % 2 or i == 4:
                    m.then_inc(sem("cT_ready"), 1)
            pe.wait_ge(sem("cT_done"), 3)
            pe.wait_ge(s_evac, EV[U_MLA + 2])
            rows(U_UQ, 0, 384, (1, 2), y_hi, y_lo, 3, 768).then_inc(sem("uq_ready"), 1)
            rows(U_UQ, 384, 384, (3, 4), y_hi, y_lo, 3, 768).then_inc(s_used, 1)
            rows(U_UQ + 1, 0, 384, (5, 6), y_hi, y_lo, 3, 384).then_inc(s_used, 1)
            for j, b in enumerate(((7, 0), (1, 2), (3, 4))):
                if j:
                    pe.wait_ge(s_evac, EV[U_UQ])
                m = rows(U_UKV, 512 * j, 512, b, y_hi[:, 3:5, :], y_lo[:, 3:5, :], 2, 1536)
                m.then_inc(sem("ukv_ready") if j < 2 else s_used, 1)
            ma_queries(1)
            pe.wait_ge(sem("q_done"), 1)
            pe.wait_ge(s_evac, EV[U_UKV])
            pe.wait_ge(sem("ma_qT_done"), 2)

            def head_T(h):
                for n, (src, a, w) in enumerate(((q, h * QK, P), (q, h * QK + P, ROPE))):
                    for t in range(T):
                        pe.transpose(ps[0:w, 4, n * S + t * P:n * S + (t + 1) * P], src[:, t, a:a + w], ident)
                pe.wait_ge(sem("kdiag_ready"), h + 1)
                for n, (src, a, w) in enumerate(((kv, h * 256, P), (kr, 0, ROPE))):
                    for t in range(T):
                        m = full(ps[0:w, 5, n * S + t * P:n * S + (t + 1) * P], src[:, t, a:a + w],
                                 kdiag[:, 2 * (h % 3) + t, :])
                m.then_inc(sem("qkT_ready"), 1)

            def head_S(h):
                r = qkT[h % 2]
                pe.wait_ge(sem("qkT_done"), h + 1)
                if h >= 2:
                    pe.wait_ge(sem("mla_sm_done"), h - 1)
                for n, (t, s_) in enumerate(((0, 0), (1, 1), (1, 0))):
                    o = ps[:, h % 2, n * P:(n + 1) * P]
                    tt, ss = slice(t * P, t * P + P), slice(s_ * P, s_ * P + P)
                    full(o, r[:, 0, tt], r[:, 2, ss], True, False)
                    m = full(o, r[0:ROPE, 1, tt], r[0:ROPE, 3, ss], False, True)
                m.then_inc(sem("mla_s_ready"), 1)

            def head_P(h):
                pe.wait_ge(sem("mla_p_done"), h + 1)
                if h >= 2:
                    pe.wait_ge(sem("mla_pT_done"), h - 1)
                for n, at in enumerate((0, 2, 1)):
                    m = pe.transpose(ps[:, 2 + h % 2, n * P:(n + 1) * P], mp[h % 2][:, at, :], ident)
                m.then_inc(sem("mla_pT_ready"), 1)

            def head_O(h):
                pe.wait_ge(sem("mla_pT_done"), h + 1)
                if h >= 2:
                    pe.wait_ge(sem("y_ready"), KT + h - 1)
                o, vs = ps[:, 6 + h % 2, 0:S], slice(h * 256 + P, h * 256 + 256)
                pT = mpT[h % 2]
                full(o, kv[:, 0, vs], pT[:, 0:2, :].rearrange("p a b -> p (a b)"), True, False)
                full(ps[:, 6 + h % 2, P:S], kv[:, 1, vs], pT[:, 2, :], False, True).then_inc(sem("mla_o_ready"), 1)

            for i in range(HEADS + 3):
                if 1 <= i <= HEADS:
                    head_S(i - 1)
                if i < HEADS:
                    head_T(i)
                if 2 <= i <= HEADS + 1:
                    head_P(i - 2)
                if i >= 3:
                    head_O(i - 3)
            pe.wait_ge(sem("y_ready"), KT + HEADS)
            ma_scores(1)
            kt_major(U_OUT1, y_hi, y_lo, beside_memory(1))
            norm(3)
            ffn(1)

            norm(4)
            ffn(2)
            norm(5)
            for n, u in enumerate(IN2_TILES):
                if n >= 2:
                    pe.wait_ge(s_evac, EV[IN2_TILES[n - 2]])
                for j in range(3):
                    m = cols(u, j, ps[:, (n % 2) * 2 + j // 2, (j % 2) * S:(j % 2) * S + S], 5)
                m.then_inc(s_used, 1)
                if n == 1:
                    rows(U_IN2 + 2, 0, 256, (4, 5), h_hi, h_lo)
                    cols(U_IN2 + 2, 2, ps[:, 6, 0:S]).then_inc(s_used, 1)
                if n == 2:
                    pe.wait_ge(s_evac, EV[U_IN2 + 2])
                    for t in range(T):
                        m = full(ps[:, 7, t * 256:(t + 1) * 256], glr[:, t * P:(t + 1) * P], V("gup", 0, 256))
                    m.then_inc(sem("gate_ready"), 1)
            def conv(a, b):
                for n in range(a, b):
                    i, tap = PE_TAPS[n]
                    pe.wait_ge(sem("tap_ready"), n + 1)
                    o = ps[:, 5, (3 - i) * S:(4 - i) * S]
                    full(o, tapd[:, n % 7, :], glu[:, i, tap:tap + S], tap == 0,
                         tap == (TAPS if i == 3 else SHARED) - 1).then_inc(sem("tap_used"), 1)

            pe.wait_ge(sem("la_done"), 1)
            for f in range(2):
                for t in range(T):
                    m = full(ps[:, 6, f * S + t * P:f * S + (t + 1) * P], la[:, t, f * P:(f + 1) * P], tri)
            m.then_inc(sem("cum_ready"), 1)
            pe.wait_ge(sem("glu3_ready"), 1)
            conv(0, 7)
            pe.wait_ge(s_evac, EV[IN2_TILES[2]])
            rows(U_IN2 + 5, 0, 384, (0, 1), h_hi, h_lo).then_inc(s_used, 1)
            conv(7, 14)
            pe.wait_ge(s_evac, EV[IN2_TILES[3]])
            rows(U_IN2 + 6, 0, 384, (2, 3), h_hi, h_lo).then_inc(s_used, 1)
            conv(14, len(PE_TAPS))
            pe.wait_ge(s_evac, EV[U_IN2 + 6])
            pe.wait_ge(sem("gla_in_done"), 1)

            def pair_scores(bank, lhs, rhs):
                for par in range(2):
                    r = slice(par * 64, par * 64 + 64)
                    for f in range(2):
                        for t in range(T):
                            tt = slice(t * P, (t + 1) * P)
                            m = full(ps[:, bank + par, (2 * f + t) * P:(2 * f + t + 1) * P],
                                     lhs[r, f, tt], rhs[r, f, tt])
                return m
            pair_scores(0, kd, qd).then_inc(sem("g_s_ready"), 1)
            pair_scores(6, ku, qu).then_inc(sem("g_s_ready"), 1)
            pe.wait_ge(sem("cy3_done"), 1)
            pair_scores(4, ke, qd).then_inc(sem("g_s_ready"), 1)
            for par in range(2):
                r = slice(par * 64, par * 64 + 64)
                for f in range(2):
                    m = full(ps[:, 2 + par, f * P:(f + 1) * P], k7[r, f, :], q7[r, f, :])
            m.then_inc(sem("g_s_ready"), 1)
            warm(24, ps[:, 2, S:2 * S])
            pe.wait_ge(sem("cy_done"), 1)
            for i in range(4):
                m = full(ps[:, 2, S:2 * S], ones, cy[:, i, :], i == 0, i == 3)
            m.then_inc(sem("mean_ready"), 1)
            warm(20, ps[:, 3, S:2 * S])
            pe.wait_ge(sem("ysq_done"), 1)
            for i in range(4):
                m = full(ps[:, 3, S:2 * S], ones, csq[:, i, :], i == 0, i == 3)
            m.then_inc(sem("var_ready"), 1)
            pe.wait_ge(sem("gA_done"), 1)
            for t in range(T):
                for h in range(G_HEADS):
                    par, f = h % 2, h // 2
                    o, hs = ps[:, 6 + t, h * P:(h + 1) * P], slice(h * P, (h + 1) * P)
                    if t:
                        full(o, gO[par][:, f, :], gv[:, 0, hs], True, False)
                    m = full(o, gA[par][:, 2 * f + t, :], gv[:, t, hs], t == 0, True)
            m.then_inc(sem("g_o_ready"), 1)

            def gla_y(k):
                if k == 4:
                    pe.wait_ge(sem("go_done"), T)
                    for h in range(G_HEADS):
                        for t in range(T):
                            m = pe.transpose(ps[:, 4 + h // 2, (h % 2) * S + t * P:(h % 2) * S + (t + 1) * P],
                                             go[:, t, h * P:(h + 1) * P], ident)
                        if h % 2:
                            m.then_inc(sem("yT_ready"), 1)
                pe.wait_ge(sem("y_ready"), KT * 2 + k + 1)

            kt_major(U_OUT2, y_hi, y_lo, gla_y)
            norm(6)
            ffn(3)

            pe.wait_ge(sem("pleT_done"), 1)
            pe.wait_ge(sem("x_done"), 4 * 7)
            s = U_PROJ % SLOTS
            for k in range(2):
                pe.wait_ge(s_lo, pieces(U_PROJ, (k + 1) * D))
                for t in range(T):
                    tt = slice(t * P, (t + 1) * P)
                    for half in range(2):
                        r = slice(k * D + half * 512, k * D + half * 512 + 512)
                        m = three(ps[:, 2 * t + half, :], y_hi[:, 3 + k, tt], y_lo[:, 3 + k, tt],
                                  w_hi[:, s, r], w_lo[:, s, r], k == 0, k == 1)
            m.then_inc(s_used, 1)
            norm(7)
            pe.wait_ge(s_evac, EV[U_PROJ])
            kt_major(U_GATE, h_hi, h_lo, lambda k: pe.wait_ge(sem("hT_ready"), 4 * 7 + k // 2 + 1))

        @block.scalar
        def _(act):
            evac = Count(s_evac)

            def copy(o, i, scale=1.0):
                return act.activation(o, i, ACT.Copy, scale=scale)

            def hi(r, u, p):
                if u >= UNITS:
                    return
                s = u % SLOTS
                if p == 0:
                    act.wait_ge(rings[s], 16 * (u // SLOTS + 1) if r is None else r * 16 + 16 * (u // SLOTS + 1))
                    if u >= SLOTS:
                        act.wait_ge(s_used, u - 2 if r is None else r * 3 + (u - 2))
                a = extent(u, p) if r is None else slice(p * PIECE, (p + 1) * PIECE)
                copy(w_hi[:, s, a], raw[:, s, a]).then_inc(s_hi, 1)

            def split(u):
                for p in range(3):
                    hi(None, u, p)

            def unit(u, *moves):
                split(u + 2)
                act.wait_ge(s_used, u + 1)
                for move in moves[:-1]:
                    move()
                evac.inc(moves[-1]())

            def norm_a(i, between=None):
                for b in range(4):
                    t, r = b // 2, slice((b % 2) * 512, (b % 2) * 512 + 512)
                    if i:
                        act.wait_ge(sem("x_done"), 4 * (i - 1) + b + 1)
                    else:
                        act.wait_ge(sem("x_loaded"), 16)
                    act.activation(junk[:, t, r], x[:, t, r], ACT.Square, scale=D ** -0.5,
                                   accum_out=small[:, b:b + 1]).then_inc(sem("ss_done"), 1)
                if between:
                    hi(None, between, 2)

            def norm_b(i, gain):
                for k in range(KT):
                    act.wait_ge(sem("xT_ready"), 4 * i + k // 2 + 1)
                    copy(h_hi[:, k, :], ps[:, 4 + k // 2, (k % 2) * S:(k % 2) * S + S], V(gain, k)).then_inc(sem("h_hi_done"), 1)

            def ffn(i):
                (U0, cw), n0 = FFNS[i], i * CH

                def at(r, n, per=3):
                    return n if r is None else r * per + n

                def body(r, j):
                    b, g = 4 + j % 3, j % 3
                    act.wait_ge(sem("up_ready"), at(r, n0 + j + 1))
                    if cw:
                        for z in range(2):
                            a = _cols[cw][0] + 8 * j + 4 * z

                            def w(n):
                                return vec[:, a + n:a + n + 1] if r is None else vec[:, bass.ds(r * 24 + (a + n), 1)]
                            m = act.activation(cv[:, g, z * S:(z + 1) * S], ps[:, b, z * S:(z + 1) * S],
                                               ACT.Identity, scale=w(2), bias=w(3))
                        m.then_inc(sem("ev_done"), 1)
                        if j < CH - 1:
                            hi(r, U0 + j + 2, 0)
                        act.wait_ge(sem("up_used"), at(r, UP0[i] + j + 1))
                        act.activation(sa[:, g, :], cv[:, g, 0:S], ACT.Silu).then_inc(sem("silu_done"), 1)
                    else:
                        act.activation(sa[:, g, :], ps[:, b, 0:S], ACT.Silu).then_inc(sem("silu_done"), 1)
                        if j < CH - 1:
                            hi(r, U0 + j + 2, 0)
                    if j < CH - 1:
                        hi(r, U0 + j + 2, 1)
                    act.wait_ge(sem("gate_done"), at(r, n0 + j + 1))
                    copy(y_hi[:, g, :], gg[:, g, :]).then_inc(sem("g_hi_done"), 1)
                    if j < CH - 1:
                        hi(r, U0 + j + 2, 2)

                body(None, 0)
                with act.Fori(0, (CH - 1) // 3 - 1) as r:
                    for j in range(1, 4):
                        body(r, j)
                for j in range(CH - 3, CH):
                    body(None, j)
                for p in range(2):
                    hi(None, U0 + CH + 1, p)

            def mem_kT(l):
                act.wait_ge(sem("mkT_ready"), l + 1)
                copy(mem_k[:, l, :, :].rearrange("p a b -> p (a b)"), ps[:, 4, :], V("mk", l)).then_inc(sem("mkT_done"), 1)

            def ma_queries(l):
                act.wait_ge(sem("ma_qT_ready"), l + 1)
                copy(ma_qT[:, :, :].rearrange("p a b -> p (a b)"), ps[:, 5, :], V("mq", l)).then_inc(sem("ma_qT_done"), 1)

            def mem_attention(l):
                for g in range(4):
                    act.wait_ge(sem("ma_mx_done"), 4 * l + g + 1)
                    for pair in range(2):
                        n = 2 * g + pair
                        m = act.activation(ma_p[:, n, :], ps[:, 4 + g, pair * S:(pair + 1) * S], ACT.Exp,
                                           bias=small[:, 96 + n:97 + n], scale=MEM_HD ** -0.5,
                                           accum_out=small[:, 112 + n:113 + n])
                    m.then_inc(sem("ma_e_done"), 1)
                act.wait_ge(sem("ma_pT_ready"), l + 1)
                copy(ma_pT[:, 0:2, :].rearrange("p a b -> p (a b)"), ps[:, 4, :])
                copy(ma_pT[:, 2:4, :].rearrange("p a b -> p (a b)"), ps[:, 5, :]).then_inc(sem("ma_pT_done0"), 1)
                act.wait_ge(sem("ma_o_ready"), l + 1)
                copy(y_hi[:, 6:8, :].rearrange("p a b -> p (a b)"), ps[:, 4, :]).then_inc(sem("ma_y_hi"), 1)

            act.wait_ge(sem("vec_loaded"), 16)
            act.wait_ge(sem("lb_max"), 1)
            act.activation(small[:, 144:162], small[:, 144:162], ACT.Exp).then_inc(sem("lb_exp"), 1)
            act.wait_ge(sem("mem_loaded"), 16)
            act.activation(memn[:, 0:4, :].rearrange("p a b -> p (a b)"), junk[:, 0, :], ACT.Square,
                               accum_out=small[:, 0:1]).then_inc(sem("mss_done"), 1)
            act.wait_ge(sem("mrstd_done"), 1)
            copy(junk[:, 0, :], junk[:, 0, :], small[:, 72:73]).then_inc(sem("mn_done0"), 1)
            split(0)
            for b in range(4):
                act.wait_ge(sem("mnT_ready"), b + 1)
                m = copy(memn[:, 2 * b:2 * b + 2, :].rearrange("p a b -> p (a b)"), ps[:, 4 + b, :])
                m.then_inc(sem("memn_done"), 1)
            for k in range(KT):
                act.wait_ge(sem("memn_done"), k // 2 + 1)
                copy(y_hi[:, k, :], memn[:, k, :], V("mem0", k)).then_inc(sem("memT_hi_done"), 1)
            split(1)
            norm_a(0)
            unit(0, *[lambda t=t: copy(mk_tok[0][:, t, :], ps[:, t, 0:256]) for t in range(T)],
                 *[lambda t=t: copy(mem_v[:, 0, t, 0:P], ps[:, t, 256:384]) for t in range(T)])
            unit(1, *[lambda t=t: copy(mem_v[:, 0, t, P:256], ps[:, 2 + t, 0:P]) for t in range(T)])
            norm_b(0, "mix0")
            for k in range(KT):
                copy(y_hi[:, k, :], memn[:, k, :], V("mem1", k)).then_inc(sem("memT_hi_done"), 1)
            act.wait_ge(sem("ang_done"), 1)
            act.activation(trig[:, 0, :, :], tr[1], ACT.Sin).then_inc(sem("cos_done"), 1)
            act.activation(trig[:, 1, :, :], tr[0], ACT.Sin).then_inc(sem("sin_done"), 1)
            for n in range(2):
                h = 3 * n
                unit(U_F + n,
                     lambda: act.activation(hk[:, h:h + 2, :].rearrange("p a b -> p (a b)"), ps[:, 2 * n, :], ACT.Sigmoid),
                     lambda: act.activation(hk[:, h + 2, :], ps[:, 2 * n + 1, 0:S], ACT.Sigmoid))
            mem_kT(0)
            for n in range(2):
                h = 3 * n
                unit(U_Q + n,
                     lambda: act.activation(hq[:, h:h + 2, :].rearrange("p a b -> p (a b)"), ps[:, 2 * n, :], ACT.Silu),
                     lambda: act.activation(hq[:, h + 2, :], ps[:, 2 * n + 1, 0:S], ACT.Silu))
            for half in range(2):
                act.wait_ge(sem("fg_done"), half + 1)
                v = hD[:, 3 * half:3 * half + 3, :].rearrange("p a b -> p (a b)")
                act.activation(v, v, ACT.Ln).then_inc(sem("ln_done"), 1)

            def exps(l):
                m = 1 << l
                for half in range(2):
                    hh = slice(3 * half, 3 * half + 3)
                    if l:
                        act.wait_ge(sem("upd_done"), 2 * (l - 1) + half + 1)
                        act.wait_ge(sem("level_ready"), 2 * (l - 1) + half + 1)
                    else:
                        act.wait_ge(sem("ln_done"), half + 1)
                        act.wait_ge(sem("r_zero"), 1)
                    act.activation(right(hE[:, hh, :], m), right(hD[:, hh, :], m), ACT.Exp)
                    act.activation(left(hE[:, hh, :], m), left(hR[:, hh, :], m), ACT.Exp).then_inc(sem("exp_done"), 1)

            def tok(dst, b, n, a=0, col=0):
                return [lambda t=t: copy(dst[:, t, a:a + n], ps[:, b + t, col:col + n]) for t in range(T)]

            exps(0)
            for l in range(LEVELS - 1):
                exps(l + 1)
                if l >= len(HG_UNITS):
                    continue
                u = HG_UNITS[l]
                b = 4 if l % 2 == 0 else 6
                if u in (U_I, U_I + 1):
                    unit(u, *tok(hv, b, 384, (u - U_I) * 384))
                elif u == U_MEM1:
                    unit(u, *tok(mk_tok[1], b, 256), *tok(mem_v[:, 1], b, P, 0, 256))
                elif u == U_MEM1 + 1:
                    unit(u, *tok(mem_v[:, 1], b, P, P), *tok(qm0, b, MEM_W, 0, P))
                else:
                    split(u + 2)
            act.wait_ge(sem("mult_done"), 2 * LEVELS)
            for n in range(2):
                u = U_G + n
                act.wait_ge(s_used, u + 1)
                for t in range(T):
                    m = act.activation(hg[:, t, n * 384:(n + 1) * 384], ps[:, 4 + 2 * n + t, 0:384], ACT.Silu)
                evac.inc(m)
            split(U_OUT0 + 2)
            act.wait_ge(sem("hg_o_ready"), 1)
            for t in range(T):
                copy(ho[:, t, 0:512], ps[:, 2 * t, :])
                copy(ho[:, t, 512:HW], ps[:, 2 * t + 1, 0:256]).then_inc(sem("ho_copied"), 1)
            mem_kT(1)
            ma_queries(0)
            for h in range(HEADS):
                act.wait_ge(sem("yT_ready"), h // 2 + 1)
                copy(y_hi[:, h, :], ps[:, h // 2, (h % 2) * S:(h % 2) * S + S], V("hgn")).then_inc(sem("y_hi_done"), 1)
            mem_attention(0)
            split(U_OUT0 + 3)
            split(U_OUT0 + 4)
            norm_a(1)
            norm_b(1, "ffn0")
            ffn(0)

            norm_a(2, U_MLA)
            norm_b(2, "mix1")
            split(U_MLA + 1)
            unit(U_MLA, *tok(cq, 0, 384))
            unit(U_MLA + 1, *tok(ckv, 2, 320))
            unit(U_MLA + 2, *tok(qm1, 4, MEM_W))
            for i in range(5):
                b = (6, 6, 7, 7, 0)[i]
                act.wait_ge(sem("cT_ready"), (1, 1, 2, 2, 3)[i])
                g = V("qa", i) if i < 3 else V("kva", i - 3)
                copy(y_hi[:, i, :], ps[:, b, (i % 2) * S:(i % 2) * S + S], g).then_inc(sem("cT_hi_done"), 1)
            split(U_UQ + 2)
            act.wait_ge(sem("uq_ready"), 1)
            for m in tok(q, 1, 384):
                m()
            act.wait_ge(s_used, U_UQ + 1)
            for m in tok(q, 3, 384, 384)[:-1]:
                m()
            evac.inc(tok(q, 3, 384, 384)[-1]())
            unit(U_UQ + 1, *tok(q, 5, 384, 768))
            split(U_UKV + 2)
            for j, banks in enumerate(((7, 0), (1, 2), (3, 4))):
                if j < 2:
                    act.wait_ge(sem("ukv_ready"), j + 1)
                else:
                    act.wait_ge(s_used, U_UKV + 1)
                for t in range(T):
                    m = copy(kv[:, t, 512 * j:512 * j + 512], ps[:, banks[t], :])
                if j == 0:
                    m.then_inc(sem("kv_copied"), 1)
                for t in range(T):
                    for h in range(2 * j, 2 * j + 2):
                        i = t * HEADS + h
                        m = act.activation(ksq[i], ps[:, banks[t], (h % 2) * 256:(h % 2) * 256 + P],
                                           ACT.Square, scale=QK ** -0.5, accum_out=small[:, 12 + i:13 + i])
            evac.inc(m)

            def key_diag(h):
                if h >= 3:
                    act.wait_ge(sem("qkT_ready"), h - 2)
                for t in range(T):
                    i = 72 + t * HEADS + h
                    m = copy(kdiag[:, 2 * (h % 3) + t, :], ident, small[:, i:i + 1])
                m.then_inc(sem("kdiag_ready"), 1)

            def head_T(h):
                act.wait_ge(sem("qkT_ready"), h + 1)
                if h >= 2:
                    act.wait_ge(sem("mla_s_ready"), h - 1)
                r = qkT[h % 2]
                for n in range(2):
                    copy(r[:, 2 * n, :], ps[:, 4 + n, 0:S], V(("qn", "kn")[n]))
                    m = copy(r[0:ROPE, 2 * n + 1, :], ps[0:ROPE, 4 + n, S:2 * S])
                m.then_inc(sem("qkT_done"), 1)

            def head_E(h):
                act.wait_ge(sem("mla_mx_done"), h + 1)
                p, c = mp[h % 2], 2 * (h % 2)
                act.activation(p[:, 0, :], p[:, 0, :], ACT.Exp, bias=small[:, 96 + c:97 + c],
                               accum_out=small[:, 112 + c:113 + c])
                v = p[:, 1:3, :].rearrange("p a b -> p (a b)")
                act.activation(v, v, ACT.Exp, bias=small[:, 97 + c:98 + c],
                                   accum_out=small[:, 113 + c:114 + c]).then_inc(sem("mla_e_done"), 1)

            def head_O(h):
                act.wait_ge(sem("mla_o_ready"), h + 1)
                copy(y_hi[:, h, :], ps[:, 6 + h % 2, 0:S]).then_inc(sem("y_hi_done"), 1)

            ma_queries(1)
            act.wait_ge(sem("k_factors"), 1)
            key_diag(0)
            key_diag(1)
            for i in range(HEADS + 3):
                if i < HEADS:
                    head_T(i)
                if i + 2 < HEADS:
                    key_diag(i + 2)
                if 1 <= i <= HEADS:
                    head_E(i - 1)
                if i >= 3:
                    head_O(i - 3)
                if 4 <= i < 7:
                    hi(None, U_OUT1 + 2, i - 4)
            mem_attention(1)
            split(U_OUT1 + 3)
            split(U_OUT1 + 4)
            norm_a(3)
            norm_b(3, "ffn1")
            ffn(1)

            norm_a(4, U_FFN2)
            norm_b(4, "ffn2")
            split(U_FFN2 + 1)
            ffn(2)
            norm_a(5, U_IN2)
            norm_b(5, "mix2")
            split(U_IN2 + 1)
            spots = [(ga, 0), (gs, 0), (ga, 1), (gs, 1), (ga, 2), (gs, 2), (ga, 3), (gs, 3),
                     (gq, 0), (gq, 1), (gk, 0), (gk, 1)]
            def spots_of(n):
                def spot(j):
                    dst, i = spots[3 * n + j]
                    return act.activation(dst[:, i, :], ps[:, (n % 2) * 2 + j // 2, (j % 2) * S:(j % 2) * S + S],
                                          ACT.Sigmoid if dst is gs else ACT.Copy)
                return [lambda j=j: spot(j) for j in range(3)]

            unit(U_IN2, *spots_of(0))
            unit(U_IN2 + 1, *spots_of(1))
            unit(U_IN2 + 2,
                 *[lambda t=t: act.activation(gr[:, t, 256:512], ps[:, 4 + t, 0:256], ACT.Silu) for t in range(T)],
                 lambda: copy(glr, ps[:, 6, 0:S]))
            unit(U_IN2 + 3, *spots_of(2))
            act.wait_ge(sem("gl_done"), 1)
            act.activation(g_abs, la, ACT.Abs).then_inc(sem("ga1"), 1)
            act.wait_ge(sem("ga1"), 1)
            act.activation(g_abs, g_abs, ACT.Exp, scale=-1.0).then_inc(sem("ga2"), 1)
            act.wait_ge(sem("ga2"), 1)
            act.activation(g_abs, g_abs, ACT.Ln, bias=1.0).then_inc(sem("g_ln_done"), 1)

            def tap_diags(a, b):
                for n in range(a, b):
                    i, tap = PE_TAPS[n]
                    if n >= 7:
                        act.wait_ge(sem("tap_used"), n - 6)
                    copy(tapd[:, n % 7, :], ident, V("dw", i * TAPS + tap)).then_inc(sem("tap_ready"), 1)

            tap_diags(0, 7)
            unit(U_IN2 + 4, *spots_of(3))
            act.wait_ge(sem("cum_ready"), 1)
            copy(cum[:, :, :].rearrange("p a b -> p (a b)"), ps[:, 6, :]).then_inc(sem("cum_copied"), 1)
            act.wait_ge(sem("cum_copied"), 1)
            act.activation(ep, cum, ACT.Exp, scale=1.0 / 16)
            act.activation(en, cum, ACT.Exp, scale=-1.0 / 16).then_inc(sem("gexp_done"), 1)
            act.wait_ge(sem("ec_in_done"), 1)
            act.activation(ec, ec, ACT.Exp, scale=1.0 / 16).then_inc(sem("gexp_done"), 1)
            tap_diags(7, 14)
            unit(U_IN2 + 5, *tok(gv, 0, 384))
            tap_diags(14, 21)
            unit(U_IN2 + 6, *tok(gv, 2, P, 384),
                 *[lambda t=t: act.activation(gr[:, t, 0:256], ps[:, 2 + t, P:384], ACT.Silu) for t in range(T)])
            tap_diags(21, len(PE_TAPS))
            act.wait_ge(sem("yn_done"), 1)
            for i in range(4):
                act.activation(csq[:, i, :], cy[:, i, :], ACT.Silu, scale=V("lng", i), bias=V("lnb", i)).then_inc(sem("cs_done"), 1)
            for i in range(4):
                act.wait_ge(sem("cs_done"), i + 1)
                copy(y_hi[:, i, :], csq[:, i, :]).then_inc(sem("y_hi_done"), 1)
            split(U_OUT2 + 2)
            act.wait_ge(sem("g_o_ready"), 1)
            for t in range(T):
                copy(go[:, t, :], ps[:, 6 + t, :]).then_inc(sem("go_copied"), 1)
            for h in range(G_HEADS):
                act.wait_ge(sem("yT_ready"), 3 + h // 2 + 1)
                copy(y_hi[:, 4 + h, :], ps[:, 4 + h // 2, (h % 2) * S:(h % 2) * S + S], V("glan", h)).then_inc(sem("y_hi_done"), 1)
            split(U_OUT2 + 3)
            split(U_OUT2 + 4)
            norm_a(6)
            norm_b(6, "ffn3")
            ffn(3)
            act.wait_ge(sem("pleT_ready"), 1)
            copy(y_hi[:, 3:5, :].rearrange("p a b -> p (a b)"), ps[:, 7, :]).then_inc(sem("ple_hi_done"), 1)
            norm_a(7, U_PROJ)
            split(U_PROJ + 1)
            unit(U_PROJ, *[lambda b=b: copy(proj[:, b // 2, (b % 2) * 512:(b % 2) * 512 + 512], ps[:, b, :])
                           for b in range(4)])
            norm_b(7, "ple")
            for u in range(U_GATE, U_GATE + 3):
                split(u + 2)
            for b in range(4):
                if b < 3:
                    act.wait_ge(sem("sum_ready"), 3 * 7 + b + 1)
                else:
                    act.wait_ge(s_used, UNITS)
                act.activation(sg[:, b // 2, (b % 2) * 512:(b % 2) * 512 + 512], ps[:, b, :], ACT.Sigmoid).then_inc(sem("sg_done"), 1)
            act.wait_ge(sem("x_done"), 4 * 7 + 1)
            act.activation(junk[:, 0, :], x[:, 0, :], ACT.Square, accum_out=small[:, 0:1]).then_inc(sem("ss_done"), 1)

        @block.vector
        def _(dve):
            chain = Count(s_chain)

            def link(ins):
                chain.inc(ins)
                dve.wait_ge(s_chain, chain.at(chain.n))

            def lo(r, u, p):
                if u >= UNITS:
                    return
                n = 3 * u + p + 1
                dve.wait_ge(s_hi, n if r is None else r * 9 + n)
                s = u % SLOTS
                a = extent(u, p) if r is None else slice(p * PIECE, (p + 1) * PIECE)
                dve.tensor_tensor(w_lo[:, s, a], raw[:, s, a], w_hi[:, s, a], ALU.subtract).then_inc(s_lo, 1)

            def split(u):
                for p in range(3):
                    lo(None, u, p)

            def rsqrt(out_, mean, n, t1, t2, scale=1.0):
                if mean is not None:
                    link(dve.tensor_scalar(t1, mean, scale, EPS, ALU.mult, ALU.add))
                link(dve.tensor_scalar(t2.bitcast(I32), t1.bitcast(I32), 1, None, ALU.logical_shift_right))
                link(dve.tensor_scalar(out_.bitcast(I32), t2.bitcast(I32), -1.0, float(0x5F3759DF), ALU.mult, ALU.add))
                g = 0.375
                link(dve.tensor_tensor(t2, out_, out_, ALU.mult))
                link(dve.scalar_tensor_tensor(t2, t2, -0.5 * g, t1, ALU.mult, ALU.mult))
                link(dve.scalar_tensor_tensor(out_, t2, 1.5 * g, out_, ALU.add, ALU.mult))
                link(dve.tensor_tensor(t2, out_, out_, ALU.mult))
                link(dve.scalar_tensor_tensor(t2, t2, g ** -2, t1, ALU.mult, ALU.mult))
                link(dve.scalar_tensor_tensor(t2, t2, 10.0 / 3, t2, ALU.subtract, ALU.mult))
                link(dve.scalar_tensor_tensor(out_, t2, 5.0, out_, ALU.add, ALU.mult))

            def stat(n):
                return small[:, 72:72 + n], small[:, 0:n], n, small[:, 24:24 + n], small[:, 48:48 + n]

            def squares(o, i, acc, scale=1.0):
                return dve.tensor_tensor_reduce(o, i, i, scale, 0.0, ALU.mult, ALU.add, acc)

            def norm_a(i, between=None):
                dve.wait_ge(sem("ss_done"), 4 * i + 4)
                v = small[:, 0:4].rearrange("p (t h) -> p t h", h=2)
                link(dve.scalar_tensor_tensor(small[:, 24:26], v[:, :, 0], EPS, v[:, :, 1], ALU.add, ALU.add))
                rsqrt(small[:, 72:74], None, 2, small[:, 24:26], small[:, 48:50])
                for t in range(T):
                    dve.tensor_scalar(diag[:, t, :], ident, small[:, 72 + t:73 + t], None,
                                      ALU.mult).then_inc(sem("factors_done"), 1)
                if between:
                    lo(None, between, 2)

            def norm_b(i, gain):
                for k in range(KT):
                    dve.wait_ge(sem("h_hi_done"), 8 * i + 2 * (k // 2) + 2)
                    m = dve.scalar_tensor_tensor(h_lo[:, k, :], ps[:, 4 + k // 2, (k % 2) * S:(k % 2) * S + S],
                                                 V(gain, k), h_hi[:, k, :], ALU.mult, ALU.subtract)
                    if k % 2:
                        m.then_inc(sem("hT_ready"), 1)

            def residual(i, u, scale=1.0, after=None):
                for b in range(4):
                    t, r = b // 2, slice((b % 2) * 512, (b % 2) * 512 + 512)
                    if b < 3:
                        dve.wait_ge(sem("sum_ready"), 3 * i + b + 1)
                    else:
                        dve.wait_ge(s_used, u + 1)
                    dve.scalar_tensor_tensor(x[:, t, r], ps[:, b, :], scale, x[:, t, r],
                                             ALU.mult, ALU.add).then_inc(sem("x_done"), 1)
                if after:
                    lo(None, after, 1)

            def ffn(i):
                (U0, cw), n0 = FFNS[i], i * CH

                def at(r, n, per=3):
                    return n if r is None else r * per + n

                def body(r, j):
                    b, g = 4 + j % 3, j % 3
                    if cw:
                        dve.wait_ge(sem("ev_done"), at(r, UP0[i] + j + 1))
                        marks = []
                        for tap in (1, 0):
                            for z in range(2):
                                col = _cols[cw][0] + 8 * j + 4 * z + tap
                                w = vec[:, col:col + 1] if r is None else vec[:, bass.ds(r * 24 + col, 1)]
                                d = 2 - tap
                                c = cv[:, g, z * S + d:(z + 1) * S]
                                if tap == 0:
                                    dve.wait_ge(s_chain, chain.at(marks[z]))
                                m = dve.scalar_tensor_tensor(c, ps[:, b, z * S:(z + 1) * S - d], w, c,
                                                             ALU.mult, ALU.add)
                                if tap:
                                    marks.append(chain.inc(m))
                        m.then_inc(sem("up_used"), 1)
                        if j < CH - 1:
                            lo(r, U0 + j + 2, 0)
                        dve.wait_ge(sem("up_used"), at(r, UP0[i] + j + 1))
                        dve.wait_ge(sem("silu_done"), at(r, n0 + j + 1))
                        other = cv[:, g, S:2 * S]
                    else:
                        dve.wait_ge(sem("silu_done"), at(r, n0 + j + 1))
                        other = ps[:, b, S:2 * S]
                    dve.tensor_tensor(gg[:, g, :], sa[:, g, :], other, ALU.mult).then_inc(sem("gate_done"), 1)
                    if j < CH - 1:
                        if not cw:
                            lo(r, U0 + j + 2, 0)
                        lo(r, U0 + j + 2, 1)
                    dve.wait_ge(sem("g_hi_done"), at(r, n0 + j + 1))
                    dve.tensor_tensor(y_lo[:, g, :], gg[:, g, :], y_hi[:, g, :], ALU.subtract).then_inc(sem("g_lo_done"), 1)
                    if j < CH - 1:
                        lo(r, U0 + j + 2, 2)

                body(None, 0)
                with dve.Fori(0, (CH - 1) // 3 - 1) as r:
                    chain.enter(r, 6 if cw else 0)
                    for j in range(1, 4):
                        body(r, j)
                    chain.leave((CH - 1) // 3 - 1)
                for j in range(CH - 3, CH):
                    body(None, j)
                lo(None, U0 + CH + 1, 0)
                if i < 3:
                    residual(FFN_NORM[i], U0 + CH, 1.0 if cw else 0.5, U0 + CH + 1)

            def head_sums(sq, groups, w):
                v = sq.rearrange("p t (h w) -> p (t h) w", w=w)
                link(dve.tensor_reduce(small[:, 0:groups], v, AX, ALU.add))

            def mem_keys(l):
                src = mk_tok[l]
                dve.wait_ge(s_evac, EV[(U_MEM0, U_MEM1)[l]])
                link(dve.tensor_tensor(mk_sq, src, src, ALU.mult))
                head_sums(mk_sq, 8, MEM_HD)
                rsqrt(*stat(8), scale=1.0 / MEM_HD)
                v = src.rearrange("p t (h w) -> p (t h) w", w=MEM_HD)
                dve.tensor_tensor(v, v, small[:, 72:80].unsqueeze(2).to_broadcast([P, 8, MEM_HD]), ALU.mult).then_inc(sem("mk_done"), 1)

            def ma_queries(l):
                qm = (qm0, qm1)[l]
                link(dve.tensor_tensor(ma_sq, qm, qm, ALU.mult))
                head_sums(ma_sq, 8, MEM_HD)
                rsqrt(*stat(8), scale=1.0 / MEM_HD)
                v = qm.rearrange("p t (h w) -> p (t h) w", w=MEM_HD)
                dve.tensor_tensor(v, v, small[:, 72:80].unsqueeze(2).to_broadcast([P, 8, MEM_HD]), ALU.mult).then_inc(sem("ma_q_done"), 1)

            def ma_maxima(l):
                for g in range(4):
                    dve.wait_ge(sem("ma_s_ready"), 4 * l + g + 1)
                    n = 2 * g
                    link(dve.tensor_reduce(small[:, 128 + n:130 + n],
                                           ps[:, 4 + g, :].rearrange("p (a b) -> p a b", b=S), AX, ALU.max))
                    dve.tensor_scalar(small[:, 96 + n:98 + n], small[:, 128 + n:130 + n], -MEM_HD ** -0.5, None,
                                          ALU.mult).then_inc(sem("ma_mx_done"), 1)

            def mem_attention(l):
                for g in range(4):
                    n = 2 * g
                    dve.wait_ge(sem("ma_e_done"), 4 * l + g + 1)
                    link(dve.reciprocal(small[:, 128 + n:130 + n], small[:, 112 + n:114 + n]))
                    for i in range(n, n + 2):
                        m = dve.tensor_scalar(ma_p[:, i, :], ma_p[:, i, :], small[:, 128 + i:129 + i], None, ALU.mult)
                    m.then_inc(sem("ma_p_done"), 1)
                dve.wait_ge(sem("ma_pT_ready"), l + 1)
                dve.tensor_copy(ma_pT[:, 4:6, :].rearrange("p a b -> p (a b)"), ps[:, 6, :])
                dve.tensor_copy(ma_pT[:, 6:8, :].rearrange("p a b -> p (a b)"), ps[:, 7, :]).then_inc(sem("ma_pT_done1"), 1)
                dve.wait_ge(sem("ma_y_hi"), l + 1)
                for i in range(2):
                    dve.tensor_tensor(y_lo[:, 6 + i, :], ps[:, 4, i * S:(i + 1) * S], y_hi[:, 6 + i, :],
                                          ALU.subtract).then_inc(sem("y_ready"), 1)

            dve.wait_ge(sem("vec_loaded"), 16)
            e = small[:, 144:162]
            lg = V("lb", 0, 18).rearrange("p (l h) -> p l h", h=HEADS)
            link(dve.tensor_tensor(small[:, 162:168], lg[:, 0, :], lg[:, 1, :], ALU.max))
            link(dve.tensor_tensor(small[:, 162:168], small[:, 162:168], lg[:, 2, :], ALU.max))
            dve.tensor_tensor(e.rearrange("p (l h) -> p l h", h=HEADS), lg,
                                  small[:, 162:168].unsqueeze(1).to_broadcast([P, 3, HEADS]), ALU.subtract).then_inc(sem("lb_max"), 1)
            dve.wait_ge(sem("mem_loaded"), 16)
            link(squares(memn[:, 4:8, :].rearrange("p a b -> p (a b)"), junk[:, 1, :], small[:, 1:2]))
            dve.wait_ge(sem("mss_done"), 1)
            rsqrt(*stat(2), scale=1.0 / D)
            dve.tensor_copy(small[:, 71:72], small[:, 72:73]).then_inc(sem("mrstd_done"), 1)
            dve.tensor_scalar(junk[:, 1, :], junk[:, 1, :], small[:, 73:74], None, ALU.mult).then_inc(sem("mn_done1"), 1)
            split(0)

            def mem_T(l):
                for k in range(KT):
                    dve.wait_ge(sem("memT_hi_done"), 8 * l + k + 1)
                    m = dve.scalar_tensor_tensor(y_lo[:, k, :], memn[:, k, :], V(f"mem{l}", k), y_hi[:, k, :],
                                                 ALU.mult, ALU.subtract)
                m.then_inc(sem("memT_lo_done"), 1)

            mem_T(0)
            split(1)
            norm_a(0)
            split(2)
            split(3)
            norm_b(0, "mix0")
            mem_keys(0)
            mem_T(1)
            dve.wait_ge(sem("pos_loaded"), 16)
            link(dve.tensor_copy(small[:, 188:190], small[:, 186:188].bitcast(I32)))
            for t in range(T):
                m = dve.tensor_scalar(tr[0][:, t, :], V("inv", 0, HALF), small[:, 188 + t:189 + t], None, ALU.mult)
            link(m)
            link(dve.tensor_scalar(tr[2], tr[0], float(1 / (2 * np.pi)), None, ALU.mult))
            link(dve.tensor_scalar(tr[2], tr[2], 12582912.0, None, ALU.add))
            link(dve.tensor_scalar(tr[2], tr[2], -12582912.0, None, ALU.add))
            for part in TWO_PI:
                link(dve.scalar_tensor_tensor(tr[0], tr[2], -part, tr[0], ALU.mult, ALU.add))
            link(dve.tensor_scalar(tr[1], tr[0], float(np.pi / 2), None, ALU.add))
            link(dve.tensor_scalar(tr[3], tr[1], float(np.pi), float(-2 * np.pi), ALU.is_gt, ALU.mult))
            link(dve.tensor_tensor(tr[1], tr[1], tr[3], ALU.add))
            link(dve.tensor_scalar(tr[1], tr[1], 3.1415925, -3.1415925, ALU.min, ALU.max))
            dve.tensor_scalar(tr[0], tr[0], 3.1415925, -3.1415925, ALU.min, ALU.max).then_inc(sem("ang_done"), 1)
            dve.wait_ge(sem("msk_loaded"), 16)
            link(dve.tensor_copy(msk[:, :], msk_f))
            dve.wait_ge(sem("lb_exp"), 1)
            ev = e.rearrange("p (l h) -> p l h", h=HEADS)
            link(dve.tensor_tensor(small[:, 162:168], ev[:, 0, :], ev[:, 1, :], ALU.add))
            link(dve.tensor_tensor(small[:, 162:168], small[:, 162:168], ev[:, 2, :], ALU.add))
            link(dve.reciprocal(small[:, 168:174], small[:, 162:168]))
            link(dve.tensor_tensor(small[:, 162:168], ev[:, 0, :], small[:, 168:174], ALU.mult))
            link(dve.tensor_scalar(small[:, 168:174], small[:, 162:168], -1.0, 1.0, ALU.mult, ALU.add))
            dve.memset(A(4608, HEADS * S), 0.0).then_inc(sem("r_zero"), 1)
            for half in range(2):
                split(U_F + half + 2)
                dve.wait_ge(s_evac, EV[U_F + half])
                for h in range(3 * half, 3 * half + 3):
                    m = dve.tensor_scalar(hD[:, h, :], hk[:, h, :], small[:, 168 + h:169 + h],
                                          small[:, 162 + h:163 + h], ALU.mult, ALU.add)
                link(m)
                hh = slice(3 * half, 3 * half + 3)
                dve.tensor_scalar(hk[:, hh, :], hD[:, hh, :], -1.0, 1.0, ALU.mult, ALU.add).then_inc(sem("hk_done"), 1)
                dve.tensor_scalar(hD[:, hh, :], hD[:, hh, :], 2.0 ** -63, None, ALU.max).then_inc(sem("fg_done"), 1)
            split(U_Q + 2)
            split(U_Q + 3)
            qs = P ** -0.5
            for b in range(3):
                dve.wait_ge(sem("diag_ready"), b + 1)
                dve.scalar_tensor_tensor(hA[:, 4 * b:4 * b + 4, :], ps[:, b, :].rearrange("p (a b) -> p a b", b=P),
                                             qs, ident.unsqueeze(1).to_broadcast([P, 4, P]), ALU.mult, ALU.mult).then_inc(sem("pred_done"), 1)

            def decays(l):
                m = 1 << l
                for half in range(2):
                    hh = slice(3 * half, 3 * half + 3)
                    dve.wait_ge(sem("exp_done"), 2 * l + half + 1)
                    dve.scalar_tensor_tensor(right(hE[:, hh, :], m), right(hq[:, hh, :], m), qs,
                                             right(hE[:, hh, :], m), ALU.mult, ALU.mult)
                    dve.tensor_tensor(left(hE[:, hh, :], m), left(hk[:, hh, :], m), left(hE[:, hh, :], m),
                                          ALU.mult).then_inc(sem("mult_done"), 1)
                for half in range(2 if l < LEVELS - 1 else 0):
                    hh = slice(3 * half, 3 * half + 3)
                    rD, lD, lR = right(hD[:, hh, :], m), left(hD[:, hh, :], m), left(hR[:, hh, :], m)
                    n = 3 * S // (2 * m)
                    link(dve.tensor_tensor(lR, lR, rD[:, :, m - 1:m].to_broadcast([P, n, m]), ALU.add))
                    dve.tensor_tensor(rD, rD, lD[:, :, m - 1:m].to_broadcast([P, n, m]), ALU.add).then_inc(sem("upd_done"), 1)

            def place(l):
                m = 1 << l
                for half in range(2):
                    n = 2 * l + half
                    dve.wait_ge(sem("level_ready"), n + 1)
                    if l < LEVELS - 1:
                        dst = hA[:, 6 * half:6 * half + 6, :].rearrange("p a (b z m) -> p a b z m", z=2, m=m)[:, :, :, 1, :]
                        mk = msk[:, l * 64:(l + 1) * 64].rearrange("p (b m) -> p b m", m=m).unsqueeze(1)\
                            .to_broadcast([P, 6, 64 // m, m])
                        src = ps[:, n % 4, 0:384].rearrange("p (a b m) -> p a b m", a=6, m=m)
                        dve.copy_predicated(dst, mk, src).then_inc(sem("pred_done"), 1)
                    else:
                        dve.tensor_copy(hO[:, 3 * half:3 * half + 3, :].rearrange("p a b -> p (a b)"),
                                            ps[:, n % 4, 0:384]).then_inc(sem("pred_done"), 1)

            decays(0)
            for l in range(LEVELS):
                if l < LEVELS - 1:
                    dve.wait_ge(sem("upd_done"), 2 * l + 2)
                    decays(l + 1)
                if l == 4:
                    mem_keys(1)
                if l < len(HG_UNITS):
                    split(HG_UNITS[l] + 2)
                if l:
                    dve.wait_ge(sem("pred_done"), 3 + 2 * l)
                else:
                    dve.wait_ge(sem("pred_done"), 3)
                place(l)
            ma_queries(0)
            split(U_OUT0 + 2)
            for t in range(T):
                dve.wait_ge(sem("ho_copied"), t + 1)
                link(dve.tensor_tensor(hsq[:, t, :], ho[:, t, :], ho[:, t, :], ALU.mult))
            head_sums(hsq, 12, P)
            rsqrt(*stat(12), scale=1.0 / P)
            dve.wait_ge(s_evac, EV[U_G + 1])
            for t in range(T):
                for h in range(HEADS):
                    v = ho[:, t, h * P:(h + 1) * P]
                    i = 72 + t * HEADS + h
                    m = dve.scalar_tensor_tensor(v, v, small[:, i:i + 1], hg[:, t, h * P:(h + 1) * P],
                                                 ALU.mult, ALU.mult)
                m.then_inc(sem("ho_done"), 1)

            def y_lo_from(k, b, col, gain, n):
                dve.wait_ge(sem("y_hi_done"), n)
                src = ps[:, b, col:col + S]
                if gain is None:
                    m = dve.tensor_tensor(y_lo[:, k, :], src, y_hi[:, k, :], ALU.subtract)
                else:
                    m = dve.scalar_tensor_tensor(y_lo[:, k, :], src, gain, y_hi[:, k, :], ALU.mult, ALU.subtract)
                m.then_inc(sem("y_ready"), 1)

            ma_maxima(0)
            for h in range(HEADS):
                y_lo_from(h, h // 2, (h % 2) * S, V("hgn"), 2 * (h // 2) + 2)
            mem_attention(0)
            split(U_OUT0 + 3)
            split(U_OUT0 + 4)
            dve.wait_ge(sem("x_back"), 16)
            residual(0, U_OUT0 + 2)
            norm_a(1)
            norm_b(1, "ffn0")
            ffn(0)

            norm_a(2, U_MLA)
            norm_b(2, "mix1")
            split(U_MLA + 1)
            split(U_MLA + 2)
            dve.wait_ge(s_evac, EV[U_MLA])
            for t in range(T):
                link(squares(rt[0][:, :, :].rearrange("p a b -> p (a b)"), cq[:, t, :], small[:, t:t + 1], 1.0 / 384))
            split(U_MLA + 3)
            dve.wait_ge(s_evac, EV[U_MLA + 1])
            for t in range(T):
                link(squares(rt[0][:, :, :].rearrange("p a b -> p (a b)")[:, 0:256], ckv[:, t, 0:256],
                             small[:, 2 + t:3 + t], 1.0 / 256))
                link(squares(kr[:, t, :], ckv[:, t, 256:320], small[:, 190 + t:191 + t], 1.0 / QK))
            rsqrt(*stat(4))
            for t in range(T):
                dve.tensor_scalar(cq[:, t, :], cq[:, t, :], small[:, 72 + t:73 + t], None, ALU.mult)
            for t in range(T):
                m = dve.tensor_scalar(ckv[:, t, 0:256], ckv[:, t, 0:256], small[:, 74 + t:75 + t], None, ALU.mult)
            m.then_inc(sem("c_done"), 1)
            for i in range(5):
                b = (6, 6, 7, 7, 0)[i]
                g = V("qa", i) if i < 3 else V("kva", i - 3)
                dve.wait_ge(sem("cT_hi_done"), (2, 2, 4, 4, 5)[i])
                m = dve.scalar_tensor_tensor(y_lo[:, i, :], ps[:, b, (i % 2) * S:(i % 2) * S + S], g, y_hi[:, i, :],
                                             ALU.mult, ALU.subtract)
                if i in (1, 3, 4):
                    m.then_inc(sem("cT_done"), 1)
            split(U_MLA + 4)
            cosb, sinb = trig[:, 0, :, :], trig[:, 1, :, :]
            link(dve.tensor_tensor(kr, ckv[:, :, 256:320], V("knr", 0, ROPE).unsqueeze(1).to_broadcast([P, T, ROPE]),
                                   ALU.mult))
            dve.wait_ge(sem("cos_done"), 1)
            dve.wait_ge(sem("sin_done"), 1)
            x1, x2 = kr[:, :, 0:HALF], kr[:, :, HALF:ROPE]
            k4 = [rt[i][:, :, 0:HALF] for i in range(4)]
            dve.tensor_tensor(k4[0], x1, cosb, ALU.mult)
            dve.tensor_tensor(k4[1], x2, sinb, ALU.mult)
            dve.tensor_tensor(k4[2], x1, sinb, ALU.mult)
            link(dve.tensor_tensor(k4[3], x2, cosb, ALU.mult))
            dve.tensor_tensor(x1, k4[0], k4[1], ALU.subtract)
            link(dve.tensor_tensor(x2, k4[2], k4[3], ALU.add))
            split(U_UQ + 2)
            split(U_UQ + 3)
            dve.wait_ge(s_evac, EV[U_UQ + 1])
            sq = [rt[i][:, 0, :] for i in range(4)]
            for t in range(T):
                for h in range(HEADS):
                    i = t * HEADS + h
                    if i >= 4:
                        dve.wait_ge(s_chain, chain.at(chain.n - 3))
                    chain.inc(squares(sq[i % 4], q[:, t, h * QK:(h + 1) * QK], small[:, i:i + 1], 1.0 / QK))
            dve.wait_ge(s_chain, chain.at(chain.n))
            rsqrt(*stat(12))
            dve.tensor_scalar(small[:, 84:96], small[:, 72:84], QK ** -0.5, None, ALU.mult).then_inc(sem("q_factors"), 1)
            for t in range(T):
                v = q[:, t, :].rearrange("p (h w) -> p h w", w=QK)[:, :, P:QK]
                m = dve.tensor_tensor(v, v, V("qnr", 0, ROPE).unsqueeze(1).to_broadcast([P, HEADS, ROPE]), ALU.mult)
            link(m)
            r4 = [rt[i].rearrange("p t (h w) -> p t h w", w=HALF) for i in range(4)]
            for t in range(T):
                v = q[:, t, :].rearrange("p (h w) -> p h w", w=QK)
                a1, a2 = v[:, :, P:P + HALF], v[:, :, P + HALF:QK]
                cb = trig[:, 0, t, :].unsqueeze(1).to_broadcast([P, HEADS, HALF])
                sb_ = trig[:, 1, t, :].unsqueeze(1).to_broadcast([P, HEADS, HALF])
                dve.tensor_tensor(r4[0][:, t], a1, cb, ALU.mult)
                dve.tensor_tensor(r4[1][:, t], a2, sb_, ALU.mult)
                dve.tensor_tensor(r4[2][:, t], a1, sb_, ALU.mult)
                link(dve.tensor_tensor(r4[3][:, t], a2, cb, ALU.mult))
                dve.tensor_tensor(a1, r4[0][:, t], r4[1][:, t], ALU.subtract)
                m = dve.tensor_tensor(a2, r4[2][:, t], r4[3][:, t], ALU.add)
            m.then_inc(sem("q_done"), 1)
            ma_queries(1)
            dve.wait_ge(s_evac, EV[U_UKV])
            for t in range(T):
                m = dve.tensor_scalar(small[:, t * HEADS:(t + 1) * HEADS], small[:, 12 + t * HEADS:18 + t * HEADS],
                                      small[:, 190 + t:191 + t], None, ALU.add)
            link(m)
            rsqrt(*stat(12))
            dve.tensor_copy(small[:, 142:143], small[:, 72:73]).then_inc(sem("k_factors"), 1)
            dve.wait_ge(sem("q_factors"), 1)

            def head_S(h):
                dve.wait_ge(sem("mla_s_ready"), h + 1)
                p, c = mp[h % 2], 2 * (h % 2)
                if h >= 2:
                    dve.wait_ge(sem("mla_pT_ready"), h - 1)
                bank = ps[:, h % 2, :].rearrange("p (a b) -> p a b", b=P)
                for t in range(T):
                    dve.scalar_tensor_tensor(p[:, t, :], bank[:, t, :], small[:, 84 + t * HEADS + h:85 + t * HEADS + h],
                                             causal, ALU.mult, ALU.add)
                n = dve.tensor_scalar(p[:, 2, :], bank[:, 2, :], small[:, 90 + h:91 + h], None, ALU.mult)
                n.then_inc(sem("mla_sm_done"), 1)
                dve.wait_ge(sem("mla_sm_done"), h + 1)
                dve.tensor_reduce(small[:, 128 + c:129 + c], p[:, 0:1, :], AX, ALU.max)
                link(dve.tensor_reduce(small[:, 129 + c:130 + c], p[:, 1:3, :].rearrange("p a b -> p (a b)"), AX, ALU.max))
                dve.tensor_scalar(small[:, 96 + c:98 + c], small[:, 128 + c:130 + c], -1.0, None, ALU.mult).then_inc(sem("mla_mx_done"), 1)

            def head_P(h):
                dve.wait_ge(sem("mla_e_done"), h + 1)
                p, c = mp[h % 2], 2 * (h % 2)
                link(dve.reciprocal(small[:, 128 + c:130 + c], small[:, 112 + c:114 + c]))
                dve.tensor_scalar(p[:, 0, :], p[:, 0, :], small[:, 128 + c:129 + c], None, ALU.mult)
                v = p[:, 1:3, :].rearrange("p a b -> p (a b)")
                dve.tensor_scalar(v, v, small[:, 129 + c:130 + c], None, ALU.mult).then_inc(sem("mla_p_done"), 1)

            def head_pT(h):
                dve.wait_ge(sem("mla_pT_ready"), h + 1)
                if h >= 2:
                    dve.wait_ge(sem("mla_o_ready"), h - 1)
                dve.tensor_copy(mpT[h % 2][:, :, :].rearrange("p a b -> p (a b)"), ps[:, 2 + h % 2, 0:384]).then_inc(sem("mla_pT_done"), 1)

            for i in range(HEADS + 3):
                if 1 <= i <= HEADS:
                    head_S(i - 1)
                    head_P(i - 1)
                if 2 <= i <= HEADS + 1:
                    head_pT(i - 2)
                if i >= 3:
                    h = i - 3
                    y_lo_from(h, 6 + h % 2, 0, None, HEADS + h + 1)
                if 1 <= i < 7:
                    lo(None, U_OUT1 + 1 + (i - 1) // 3, (i - 1) % 3)
            ma_maxima(1)
            mem_attention(1)
            split(U_OUT1 + 3)
            split(U_OUT1 + 4)
            residual(2, U_OUT1 + 2)
            norm_a(3)
            norm_b(3, "ffn1")
            ffn(1)

            norm_a(4, U_FFN2)
            norm_b(4, "ffn2")
            split(U_FFN2 + 1)
            ffn(2)
            norm_a(5, U_IN2)
            norm_b(5, "mix2")
            split(U_IN2 + 1)
            link(dve.memset(glu[:, :, 0:TAPS - 1], 0.0))
            pad = TAPS - 1
            taps = [(i, tap) for tap in range(TAPS - 1, -1, -1) for i in range(3) if (i, tap) not in PE_TAPS]
            done, last = [0], {}

            def conv(n):
                for i, tap in taps[done[0]:done[0] + n]:
                    w, g_ = V("dw", i * TAPS + tap), glu[:, i, tap:tap + S]
                    if tap == TAPS - 1:
                        m = dve.tensor_scalar(cy[:, i, :], g_, w, V("db", i), ALU.mult, ALU.add)
                    else:
                        dve.wait_ge(s_chain, last[i])
                        m = dve.scalar_tensor_tensor(cy[:, i, :], g_, w, cy[:, i, :], ALU.mult, ALU.add)
                    last[i] = chain.inc(m)
                done[0] += n

            def gated(i):
                return dve.tensor_tensor(glu[:, i, pad:pad + S], ga[:, i, :], gs[:, i, :], ALU.mult)

            split(U_IN2 + 2)
            dve.wait_ge(s_evac, EV[U_IN2])
            gated(0)
            split(U_IN2 + 3)
            dve.wait_ge(s_evac, EV[U_IN2 + 1])
            gated(1)
            link(gated(2))
            conv(9)
            split(U_IN2 + 4)
            conv(12)
            split(U_IN2 + 5)
            dve.wait_ge(s_evac, EV[U_IN2 + 3])
            gated(3).then_inc(sem("glu3_ready"), 1)
            dve.wait_ge(sem("gate_ready"), 1)
            dve.tensor_tensor(la, ps[:, 7, :].rearrange("p (a b) -> p a b", b=256),
                                  V("gb", 0, 256).unsqueeze(1).to_broadcast([P, T, 256]), ALU.add).then_inc(sem("gl_done"), 1)
            conv(8)
            dve.wait_ge(sem("g_ln_done"), 1)
            dve.scalar_tensor_tensor(la, la, 0.0, g_abs, ALU.min, ALU.subtract).then_inc(sem("la_done"), 1)
            split(U_IN2 + 6)
            conv(8)
            dve.wait_ge(sem("cum_copied"), 1)
            c8, e8 = [v.rearrange("p f (c s) -> p (f c) s", s=CHUNK) for v in (cum, ec)]
            dve.tensor_tensor(e8, c8[:, :, CHUNK - 1:CHUNK].to_broadcast([P, 8, CHUNK]), c8, ALU.subtract).then_inc(sem("ec_in_done"), 1)
            split(U_IN2 + 7)
            dve.wait_ge(sem("gexp_done"), 1)
            gsc = G_K ** -0.5
            link(dve.scalar_tensor_tensor(qd, gq, gsc, ep, ALU.mult, ALU.mult))
            dve.scalar_tensor_tensor(qu, gq, gsc, en, ALU.mult, ALU.mult)
            dve.tensor_tensor(kd, gk, en, ALU.mult)
            dve.wait_ge(sem("gexp_done"), 2)
            link(dve.tensor_tensor(ke, gk, ec, ALU.mult))
            dve.tensor_tensor(ku, gk, ep, ALU.mult)
            for f in range(2):
                dve.tensor_scalar(k7[:, f, 0:CHUNK], ke[:, f, 0:CHUNK], ep[:, f, 127:128], None, ALU.mult)
                dve.tensor_copy(k7[:, f, CHUNK:P], ke[:, f, CHUNK:P])
                dve.tensor_copy(q7[:, f, 0:CHUNK], qd[:, f, P:P + CHUNK])
                m = dve.tensor_scalar(q7[:, f, CHUNK:P], qd[:, f, P + CHUNK:S], ep[:, f, 191:192], None, ALU.mult)
            m.then_inc(sem("gla_in_done"), 1)
            split(U_IN2 + 8)
            conv(30)
            dve.wait_ge(sem("tap_used"), len(PE_TAPS))
            dve.tensor_scalar(cy[:, 3, :], ps[:, 5, 0:S], V("db", 3), None, ALU.add)
            dve.wait_ge(s_chain, last[2])
            last[2] = chain.inc(dve.tensor_tensor(cy[:, 2, :], ps[:, 5, S:2 * S], cy[:, 2, :], ALU.add))
            dve.tensor_copy(small[:, 141:142], small[:, 72:73]).then_inc(sem("cy3_done"), 1)
            conv(len(taps) - done[0])
            dve.wait_ge(s_chain, chain.at(chain.n))
            dve.tensor_copy(small[:, 140:141], small[:, 72:73]).then_inc(sem("cy_done"), 1)

            def three_d(b, n=4):
                return ps[:, b, 0:n * P].rearrange("p (a b) -> p a b", b=P)

            dve.wait_ge(sem("mean_ready"), 1)
            mean = ps[:, 2, S:2 * S].unsqueeze(1).to_broadcast([P, 4, S])
            link(dve.tensor_tensor(cy, cy, mean, ALU.subtract))
            dve.tensor_tensor(csq, cy, cy, ALU.mult).then_inc(sem("ysq_done"), 1)
            dve.wait_ge(sem("g_s_ready"), 1)
            for par in range(2):
                chain.inc(dve.tensor_copy(gA[par], three_d(par)))
            dve.wait_ge(sem("var_ready"), 1)
            dve.tensor_copy(lnr[3], ps[:, 3, S:2 * S]).then_inc(sem("var_used"), 1)
            dve.wait_ge(sem("var_used"), 1)
            rsqrt(lnr[2], lnr[3], S, lnr[0], lnr[1])
            dve.tensor_tensor(cy, cy, lnr[2].unsqueeze(1).to_broadcast([P, 4, S]), ALU.mult).then_inc(sem("yn_done"), 1)
            for n, (mask, bank) in enumerate(((MU, 6), (MX, 4))):
                dve.wait_ge(s_chain, chain.at(chain.n))
                dve.wait_ge(sem("g_s_ready"), n + 2)
                for par in range(2):
                    chain.inc(dve.copy_predicated(gA[par], msk[:, mask:mask + P].unsqueeze(1).to_broadcast([P, 4, P]),
                                                  three_d(bank + par)))
            dve.wait_ge(s_chain, chain.at(chain.n))
            dve.wait_ge(sem("g_s_ready"), 4)
            for par in range(2):
                dve.memset(gA[par][CHUNK:P, :, 0:CHUNK], 0.0)
                m = dve.tensor_copy(gO[par], three_d(2 + par, 2))
            m.then_inc(sem("gA_done"), 1)
            for i in range(4):
                dve.wait_ge(sem("y_hi_done"), 12 + i + 1)
                m = dve.tensor_tensor(y_lo[:, i, :], csq[:, i, :], y_hi[:, i, :], ALU.subtract)
                m.then_inc(sem("y_ready"), 1)
            split(U_OUT2 + 2)
            for t in range(T):
                dve.wait_ge(sem("go_copied"), t + 1)
                link(dve.tensor_tensor(gosq[:, t, :], go[:, t, :], go[:, t, :], ALU.mult))
            head_sums(gosq, 8, P)
            rsqrt(*stat(8), scale=1.0 / P)
            for t in range(T):
                for h in range(G_HEADS):
                    v = go[:, t, h * P:(h + 1) * P]
                    i = 72 + t * G_HEADS + h
                    m = dve.scalar_tensor_tensor(v, v, small[:, i:i + 1], gr[:, t, h * P:(h + 1) * P],
                                                 ALU.mult, ALU.mult)
                m.then_inc(sem("go_done"), 1)
            for h in range(G_HEADS):
                y_lo_from(4 + h, 4 + h // 2, (h % 2) * S, V("glan", h), 16 + 2 * (h // 2) + 2)
            split(U_OUT2 + 3)
            split(U_OUT2 + 4)
            residual(5, U_OUT2 + 2)
            norm_a(6)
            norm_b(6, "ffn3")
            ffn(3)
            dve.wait_ge(sem("ple_hi_done"), 1)
            for i in range(2):
                m = dve.tensor_tensor(y_lo[:, 3 + i, :], ps[:, 7, i * S:(i + 1) * S], y_hi[:, 3 + i, :], ALU.subtract)
            m.then_inc(sem("pleT_done"), 1)
            residual(6, U_FFN3 + CH, 0.5, U_PROJ)
            norm_a(7, U_PROJ)
            split(U_PROJ + 1)
            split(U_PROJ + 2)
            norm_b(7, "ple")
            split(U_PROJ + 3)
            dve.wait_ge(s_evac, EV[U_PROJ])
            for t in range(T):
                dve.wait_ge(sem("sg_done"), 2 * t + 2)
                link(dve.tensor_tensor(proj[:, t, :], proj[:, t, :], sg[:, t, :], ALU.mult))
                dve.tensor_tensor(x[:, t, :], x[:, t, :], proj[:, t, :], ALU.add).then_inc(sem("x_done"), 1)
            dve.wait_ge(sem("x_done"), 4 * 7 + 2)
            link(squares(junk[:, 1, :], x[:, 1, :], small[:, 1:2]))
            dve.wait_ge(sem("ss_done"), 4 * 8 + 1)
            rsqrt(*stat(2), scale=1.0 / D)
            dve.wait_ge(sem("fin_loaded"), 16)
            for t in range(T):
                for half in range(2):
                    r = slice(half * 512, half * 512 + 512)
                    dve.scalar_tensor_tensor(xn[:, t, r], x[:, t, r], small[:, 72 + t:73 + t], fin[:, r],
                                                 ALU.mult, ALU.mult).then_inc(sem("out_done"), 1)


def lay_out(i):
    def grid(w, cols=None):
        k, n = w.shape
        g = w.reshape(k // P, P, n).transpose(1, 0, 2)
        return g if cols is None or cols == n else np.concatenate(
            [g, np.zeros((P, k // P, cols - n), w.dtype)], axis=2)

    def unit(*parts):
        flat = [p.reshape(P, -1) for p in parts]
        n = sum(p.shape[1] for p in flat)
        return np.concatenate(flat + [np.zeros((P, UNIT - n), np.float32)], axis=1)

    def model(w, a, b, w2=None, a2=0, b2=0):
        parts = [w[:, a:b]] + ([w2[:, a2:b2]] if w2 is not None else [])
        return unit(grid(np.concatenate(parts, axis=1), NC3))

    def kt_major(w):
        g = grid(w)
        return [unit(g[:, 3 * j:3 * j + 3]) for j in range(-(-g.shape[1] // 3))]

    def ffn(w_up, w_down):
        units = []
        for c in range(FFN_UNITS):
            parts = []
            for z in range(2):
                a = z * D_FF + c * P
                parts.append(grid(w_up[:, a:a + P]) if c < CH else np.zeros((P, PIECE), np.float32))
            parts.append(w_down[(c - 1) * P:c * P] if c else np.zeros((P, PIECE), np.float32))
            units.append(unit(*parts))
        return units

    mk, hg, mla, w2 = i["w_mem_kv"], i["hg_w_in"][0], i["mla_w_in"][0], i["w_in_2"][0]
    uq, ukv = i["mla_w_uq"][0], i["mla_w_ukv"][0]
    u = [model(mk[0], 0, 384), model(mk[0], 384, 512)]
    for a in (768, 0, 1536):
        u += [model(hg, a, a + 384), model(hg, a + 384, a + 768)]
    u += [model(mk[1], 0, 384), model(mk[1], 384, 512, hg, 3072, 3328)]
    u += [model(hg, 2304, 2688), model(hg, 2688, 3072)]
    u += kt_major(i["w_out"][0]) + ffn(i["w_up"][0], i["w_down"][0])
    u += [model(mla, 0, 384), model(mla, 384, 704), model(mla, 704, 960)]
    u += [unit(grid(uq[:, 0:768])), unit(grid(uq[:, 768:1152])), unit(grid(ukv))]
    u += kt_major(i["w_out"][1]) + ffn(i["w_up"][1], i["w_down"][1])
    u += ffn(i["ffn1_w_in_2"][0], i["ffn1_w_out_2"][0])
    tile = {"a": 0, "b": 512, "q": 1024, "k": 1280}
    order = ["a0", "b0", "a1", "b1", "a2", "b2", "a3", "b3", "q0", "q1", "k0", "k1"]
    starts = [tile[n[0]] + P * int(n[1]) for n in order]
    for n in range(4):
        u.append(unit(grid(np.concatenate([w2[:, a:a + P] for a in starts[3 * n:3 * n + 3]], axis=1))))
        if n == 1:
            u.append(model(w2, 2304, 2560, w2, 2560, 2576))
    u += [model(w2, 1536, 1920), model(w2, 1920, 2048, w2, 2048, 2304)]
    u += kt_major(i["w_out_2"][0]) + ffn(i["ffn2_w_in_2"][0], i["ffn2_w_out_2"][0])
    u += kt_major(i["ple_w_proj_2"][0]) + kt_major(i["ple_w_gate_2"][0])
    assert len(u) == UNITS
    stream = np.stack(u)

    def col(g):
        return g.reshape(-1, P).T

    def every(v):
        return np.broadcast_to(v.reshape(1, -1), (P, v.size))

    def conv(layer):
        w, b = i["conv_w"][layer], i["conv_b"][layer]
        g = np.concatenate([w, b[None]], axis=0).reshape(4, 2, CH, P)
        return g.transpose(3, 2, 1, 0).reshape(P, CH * 8)

    r = np.arange(P)
    same = r[:, None] // CHUNK == r[None, :] // CHUNK
    f32 = np.float32
    v = {
        "mix0": col(i["mix_norm_g"][0]), "mix1": col(i["mix_norm_g"][1]), "ffn0": col(i["ffn_norm_g"][0]),
        "ffn1": col(i["ffn_norm_g"][1]), "mem0": col(i["mem_norm_g"][0]), "mem1": col(i["mem_norm_g"][1]),
        "ffn2": col(i["ffn1_norm_2"][0]), "mix2": col(i["mix_norm_2"][0]), "ffn3": col(i["ffn2_norm_2"][0]),
        "ple": col(i["ple_norm_2"][0]), "cw0": conv(0), "cw1": conv(1),
        "mq": np.concatenate([i["mem_q_norm_g"]] * 2, axis=1).T, "mk": np.concatenate([i["mem_k_norm_g"]] * 2, axis=1).T,
        "lb": i["hg_lb_logits"].reshape(3, HEADS, P).transpose(2, 0, 1).reshape(P, 18),
        "hgn": col(i["hg_out_norm_g"][0]), "qa": col(i["mla_qa_norm_g"][0]), "kva": col(i["mla_kva_norm_g"][0]),
        "dw": i["conv_w_2"][0].reshape(TAPS, 4, P).transpose(2, 1, 0).reshape(P, 4 * TAPS),
        "db": col(i["conv_b_2"][0]), "lng": col(i["conv_ln_g_2"][0]), "lnb": col(i["conv_ln_b_2"][0]),
        "glan": col(i["gla_norm_2"][0]), "gb": every(i["gate_b_2"][0]),
        "qn": col(i["mla_q_norm_g"][0][0:P]), "kn": col(i["mla_k_norm_g"][0][0:P]),
        "qnr": every(i["mla_q_norm_g"][0][P:]), "knr": every(i["mla_k_norm_g"][0][P:]),
        "inv": every((f32(10000.0) ** (-np.arange(HALF, dtype=f32) / f32(HALF))).astype(f32)),
        "gup": np.concatenate([i["gate_w_up_2"][0], np.zeros((P - 16, 256), f32)], axis=0),
        "ident": np.eye(P, dtype=f32),
        "causal": np.where(r[None, :] <= r[:, None], 0.0, -1e30).astype(f32),
        "tri": (same & (r[:, None] <= r[None, :])).astype(f32),
        "ones": np.full((P, P), 1.0 / 512, f32),
    }
    assert list(v) == list(_cols)
    vectors = np.concatenate([v[n] for n in _cols], axis=1)
    assert vectors.shape == (P, NV) and all(v[n].shape[1] == _cols[n][1] for n in _cols)

    masks = []
    for l in range(MASKS):
        m = 1 << l
        j = np.arange(64)
        t = (j // m) * 2 * m + m + j % m
        masks.append((r[:, None] // (2 * m) == t[None, :] // (2 * m)) & (r[:, None] % (2 * m) < m))
    masks.append(same & (r[:, None] > r[None, :]))
    masks.append((r[:, None] < CHUNK) & (r[None, :] >= CHUNK))
    tok = lambda a: a.reshape(T, P, -1).transpose(1, 0, 2)
    return {
        "stream": stream, "vectors": vectors, "masks": np.concatenate(masks, axis=1).astype(f32),
        "x": tok(i["x"][0]), "mem": tok(i["mem"][0]), "positions": i["positions"][0].reshape(T, P).T,
        "ple": tok(i["p_2"][0, 0]), "final": every(i["final_norm_2"]),
    }


def kernel(**inputs):
    import concourse.bacc as _bacc
    from concourse.bass_utils import run_bass_kernel_spmd as _run

    inputs = {k: np.asarray(v) for k, v in inputs.items()}
    nc = _bacc.Bacc("TRN2", target_bir_lowering=False, num_devices=1)
    arrays, args = {}, []
    for name, a in lay_out(inputs).items():
        a = np.ascontiguousarray(a)
        arrays[f"in_{name}"] = a
        args.append(nc.dram_tensor(f"in_{name}", a.shape, mybir.dt.from_np(a.dtype), kind="ExternalInput").ap())
    args.append(nc.dram_tensor("out", (S, D), F32, kind="ExternalOutput").ap())
    build(nc, *args)
    r = _run(nc, [arrays], core_ids=[0])
    return r.results[0]["out"].reshape(1, S, D)
```
